# Optimizing a Trainium2 kernel written in Bass

```python
import jax, jax.numpy as jnp
from jax import lax
import numpy as np
import math

D_MODEL = 1024
BATCH = 1
SEQ = 512
DEPTH = 2

GRID_W = 64
CTX_LEN = 256
EPS = 1e-6

F_GROUPS = 4
F_GROUP_DIM = D_MODEL // 16
F_WIDTH = F_GROUPS * F_GROUP_DIM
M_HEADS = 4
M_HEAD_DIM = 3 * D_MODEL // 32
M_WIDTH = M_HEADS * M_HEAD_DIM
M_CHUNK = 64
K_CONV = 5
A_HEADS = 4
A_NOPE = 64
A_ROPE = 32
A_V = 3 * D_MODEL // 32
A_WIDTH = A_HEADS * A_V
Q_LORA = D_MODEL // 4
KV_LORA = D_MODEL // 8
Q_BLOCK = 128
ROPE_THETA = 10000.0
MLP_HIDDEN = 4 * D_MODEL
IN_WIDTHS = (F_WIDTH, M_WIDTH, M_WIDTH, M_WIDTH, M_WIDTH, 4 * M_HEADS, Q_LORA, KV_LORA, A_ROPE)
IN_WIDTH = F_WIDTH + 4 * M_WIDTH + 4 * M_HEADS + Q_LORA + KV_LORA + A_ROPE
MIX_WIDTH = F_WIDTH + M_WIDTH + A_WIDTH


def rmsnorm(x, g):
    xf = x.astype(jnp.float32)
    y = xf * lax.rsqrt(jnp.mean(xf * xf, axis=-1, keepdims=True) + EPS)
    return (y * g.astype(jnp.float32)).astype(x.dtype)

def modulate(h, shift, scale):
    return h * (1 + scale) + shift

def split_proj(p):
    out, off = [], 0
    for w in IN_WIDTHS:
        out.append(p[..., off:off + w])
        off += w
    return out

def axial_rope(n):
    rows = n // GRID_W
    row = jnp.repeat(jnp.arange(rows, dtype=jnp.float32), GRID_W)
    col = jnp.tile(jnp.arange(GRID_W, dtype=jnp.float32), rows)
    nf = A_ROPE // 4
    freqs = ROPE_THETA ** (-jnp.arange(nf, dtype=jnp.float32) / nf)
    ang = jnp.stack([row[:, None] * freqs, col[:, None] * freqs], axis=1)
    return jnp.cos(ang), jnp.sin(ang)

def apply_rope(x, cos, sin):
    xs = x.reshape(x.shape[:-1] + (2, 2, A_ROPE // 4)).astype(jnp.float32)
    x1, x2 = xs[..., 0, :], xs[..., 1, :]
    out = jnp.stack([x1 * cos - x2 * sin, x1 * sin + x2 * cos], axis=-2)
    return out.reshape(x.shape).astype(x.dtype)

def fourier_mix(u):
    B, N, _ = u.shape
    ug = u.astype(jnp.float32).reshape(B, N, F_GROUPS, F_GROUP_DIM)
    y = jnp.fft.fft2(ug, axes=(1, 3), norm="ortho").real
    return y.reshape(B, N, F_WIDTH).astype(u.dtype)

def dwconv_centred(u, w):
    C = u.shape[-1]
    pad = w.shape[0] // 2
    return lax.conv_general_dilated(u, w[:, None, :].astype(u.dtype), (1,), [(pad, pad)],
                                    dimension_numbers=("NWC", "WIO", "NWC"), feature_group_count=C)

def mlstm_inputs(mq, mk, mv, mg, conv_w, b_g):
    B, N, _ = mq.shape
    qk = jax.nn.silu(dwconv_centred(jnp.concatenate([mq, mk], axis=-1), conv_w))
    heads = lambda a: a.reshape(B, N, M_HEADS, M_HEAD_DIM).transpose(0, 2, 1, 3).astype(jnp.float32)
    q = heads(qk[..., :M_WIDTH]) * (M_HEAD_DIM ** -0.5)
    k = heads(qk[..., M_WIDTH:])
    v = heads(mv)
    g = (mg.astype(jnp.float32) + b_g.astype(jnp.float32)).reshape(B, N, 4, M_HEADS).transpose(2, 0, 3, 1)
    fwd = (q, k, v, g[0], jax.nn.log_sigmoid(g[1]))
    bwd = (q, k, v, g[2], jax.nn.log_sigmoid(g[3]))
    return fwd, bwd

def mlstm_zero_state(B):
    return (jnp.zeros((B, M_HEADS, M_HEAD_DIM, M_HEAD_DIM), jnp.float32),
            jnp.zeros((B, M_HEADS, M_HEAD_DIM), jnp.float32),
            jnp.zeros((B, M_HEADS), jnp.float32))

def mlstm_chunkwise(q, k, v, li, lf, state):
    B, H, N, _ = q.shape
    L = M_CHUNK
    nc = N // L
    to_chunks = lambda a: jnp.moveaxis(a.reshape((B, H, nc, L) + a.shape[3:]), 2, 0)
    tri = jnp.tril(jnp.ones((L, L), dtype=bool))

    def step(carry, inp):
        C, n, m = carry
        qb, kb, vb, ib, fb = inp
        b = jnp.cumsum(fb, axis=-1)
        dmat = jnp.where(tri, b[..., :, None] - b[..., None, :] + ib[..., None, :], -jnp.inf)
        inter = b + m[..., None]
        m_t = jnp.maximum(inter, dmat.max(axis=-1))
        w_intra = jnp.exp(dmat - m_t[..., None])
        w_inter = jnp.exp(inter - m_t)
        s = jnp.einsum("bhtd,bhsd->bhts", qb, kb) * w_intra
        num = jnp.einsum("bhts,bhsv->bhtv", s, vb) + w_inter[..., None] * jnp.einsum("bhtd,bhdv->bhtv", qb, C)
        den = s.sum(axis=-1) + w_inter * jnp.einsum("bhtd,bhd->bht", qb, n)
        h = num / jnp.maximum(jnp.abs(den), jnp.exp(-m_t))[..., None]
        b_last = b[..., -1]
        g = b_last[..., None] - b + ib
        m_new = jnp.maximum(b_last + m, g.max(axis=-1))
        decay = jnp.exp(b_last + m - m_new)
        wk = jnp.exp(g - m_new[..., None])
        C_new = decay[..., None, None] * C + jnp.einsum("bhs,bhsd,bhsv->bhdv", wk, kb, vb)
        n_new = decay[..., None] * n + jnp.einsum("bhs,bhsd->bhd", wk, kb)
        return (C_new, n_new, m_new), h

    state, hc = lax.scan(step, state, tuple(to_chunks(a) for a in (q, k, v, li, lf)))
    h = jnp.moveaxis(hc, 0, 2).reshape(B, H, N, -1)
    return h, state

def mlstm_direction(seq, state, reverse):
    if reverse:
        seq = tuple(jnp.flip(a, axis=2) for a in seq)
    h, state = mlstm_chunkwise(*seq, state)
    if reverse:
        h = jnp.flip(h, axis=2)
    return h, state

def mlstm_output(h_f, h_b, mo, g_m):
    B, H, N, dv = h_f.shape
    h = (h_f + h_b).transpose(0, 2, 1, 3)
    h = h * lax.rsqrt(jnp.mean(h * h, axis=-1, keepdims=True) + EPS)
    h = h.reshape(B, N, M_WIDTH) * g_m.astype(jnp.float32) * jax.nn.sigmoid(mo.astype(jnp.float32))
    return h.astype(mo.dtype)

def mla_queries(cq, g_qn, w_uq, rope):
    B, N, _ = cq.shape
    q = (rmsnorm(cq, g_qn) @ w_uq).reshape(B, N, A_HEADS, A_NOPE + A_ROPE).transpose(0, 2, 1, 3)
    qn, qr = q[..., :A_NOPE], q[..., A_NOPE:]
    if rope is not None:
        qr = apply_rope(qr, *rope)
    return qn, qr

def mla_keys(ckv, kr, g_kvn, w_ukv, rope):
    B, N, _ = ckv.shape
    kv = (rmsnorm(ckv, g_kvn) @ w_ukv).reshape(B, N, A_HEADS, A_NOPE + A_V).transpose(0, 2, 1, 3)
    kn, v = kv[..., :A_NOPE], kv[..., A_NOPE:]
    if rope is not None:
        kr = apply_rope(kr, *rope)
    return kn, kr, v

def softmax_attend(qn, qr, key_sets):
    scale = (A_NOPE + A_ROPE) ** -0.5
    s = jnp.concatenate([jnp.einsum("bhqd,bhkd->bhqk", qn, kn) + jnp.einsum("bhqr,bkr->bhqk", qr, kr)
                         for kn, kr, _ in key_sets], axis=-1)
    p = jax.nn.softmax(s.astype(jnp.float32) * scale, axis=-1)
    out, off = None, 0
    for _, _, v in key_sets:
        nk = v.shape[2]
        o = jnp.einsum("bhqk,bhkd->bhqd", p[..., off:off + nk].astype(v.dtype), v)
        out = o if out is None else out + o
        off += nk
    return out

def blocked_attend(qn, qr, key_sets):
    B, H, N, _ = qn.shape
    nb = N // Q_BLOCK
    blk = lambda a: jnp.moveaxis(a.reshape(B, H, nb, Q_BLOCK, a.shape[-1]), 2, 0)
    out = lax.map(lambda qs: softmax_attend(qs[0], qs[1], key_sets), (blk(qn), blk(qr)))
    return jnp.moveaxis(out, 0, 2).reshape(B, H, N, -1)

def merge_heads(y):
    B, H, N, dv = y.shape
    return y.transpose(0, 2, 1, 3).reshape(B, N, H * dv)

def sqrelu_mlp(h, w_up, w_down):
    return jnp.square(jax.nn.relu(h @ w_up)) @ w_down

def first_inputs(seed: int = 0) -> dict:
    key = jax.random.key(seed)
    ks = jax.random.split(key, 24)
    nrm = lambda k, shape, s: jax.random.normal(k, shape, jnp.float32) * s
    gain = lambda k, shape: 1.0 + 0.02 * jax.random.normal(k, shape, jnp.float32)
    f_bias = jnp.linspace(3.0, 6.0, M_HEADS, dtype=jnp.float32)
    z = jnp.zeros((M_HEADS,), jnp.float32)
    gate_base = jnp.concatenate([z, f_bias, z, f_bias])
    return {
        "x": nrm(ks[0], (BATCH, SEQ, D_MODEL), 1.0),
        "c": nrm(ks[1], (BATCH, D_MODEL), 1.0),
        "ctx": nrm(ks[2], (BATCH, CTX_LEN, D_MODEL), 1.0),
        "c_ctx": nrm(ks[3], (D_MODEL,), 1.0),
        "w_mod": nrm(ks[4], (DEPTH, D_MODEL, 6 * D_MODEL), 0.5 * D_MODEL ** -0.5),
        "b_mod": nrm(ks[5], (DEPTH, 6 * D_MODEL), 0.01),
        "g_norm1": gain(ks[6], (DEPTH, D_MODEL)),
        "g_norm2": gain(ks[7], (DEPTH, D_MODEL)),
        "w_in": nrm(ks[8], (DEPTH, D_MODEL, IN_WIDTH), D_MODEL ** -0.5),
        "b_gates": gate_base[None, :] + nrm(ks[9], (DEPTH, 4 * M_HEADS), 0.1),
        "conv_qk": nrm(ks[10], (DEPTH, K_CONV, 2 * M_WIDTH), K_CONV ** -0.5),
        "g_mlstm": gain(ks[11], (DEPTH, M_WIDTH)),
        "g_q_norm": gain(ks[12], (DEPTH, Q_LORA)),
        "g_kv_norm": gain(ks[13], (DEPTH, KV_LORA)),
        "w_uq": nrm(ks[14], (DEPTH, Q_LORA, A_HEADS * (A_NOPE + A_ROPE)), Q_LORA ** -0.5),
        "w_ukv": nrm(ks[15], (DEPTH, KV_LORA, A_HEADS * (A_NOPE + A_V)), KV_LORA ** -0.5),
        "w_out": nrm(ks[16], (DEPTH, MIX_WIDTH, D_MODEL), MIX_WIDTH ** -0.5),
        "w_up": nrm(ks[17], (DEPTH, D_MODEL, MLP_HIDDEN), D_MODEL ** -0.5),
        "w_down": nrm(ks[18], (DEPTH, MLP_HIDDEN, D_MODEL), MLP_HIDDEN ** -0.5),
        "g_final": gain(ks[19], (D_MODEL,)),
    }

def first_block(x, c, ctx, c_ctx, w_mod, b_mod, g_norm1, g_norm2, w_in, b_gates, conv_qk, g_mlstm,
              g_q_norm, g_kv_norm, w_uq, w_ukv, w_out, w_up, w_down, g_final):
    B, S, _ = x.shape
    rope_lat = axial_rope(S)
    xc = ctx
    for l in range(DEPTH):
        last = l == DEPTH - 1
        mod = (jax.nn.silu(c) @ w_mod[l] + b_mod[l])[:, None, :]
        mod_c = jax.nn.silu(c_ctx) @ w_mod[l] + b_mod[l]
        sh1, sc1, ga1, sh2, sc2, ga2 = jnp.split(mod, 6, axis=-1)
        sh1c, sc1c, ga1c, sh2c, sc2c, ga2c = jnp.split(mod_c, 6, axis=-1)

        h = modulate(rmsnorm(x, g_norm1[l]), sh1, sc1)
        hc = modulate(rmsnorm(xc, g_norm1[l]), sh1c, sc1c)
        pf, mq, mk, mv, mo, mg, cq, ckv, kr = split_proj(h @ w_in[l])
        pfc, mqc, mkc, mvc, moc, mgc, cqc, ckvc, krc = split_proj(hc @ w_in[l])

        y_f = fourier_mix(pf)

        fwd_c, bwd_c = mlstm_inputs(mqc, mkc, mvc, mgc, conv_qk[l], b_gates[l])
        fwd, bwd = mlstm_inputs(mq, mk, mv, mg, conv_qk[l], b_gates[l])
        zero = mlstm_zero_state(B)
        hcf, st_f = mlstm_direction(fwd_c, zero, False)
        hcb, st_b = mlstm_direction(bwd_c, zero, True)
        hf, _ = mlstm_direction(fwd, st_f, False)
        hb, _ = mlstm_direction(bwd, st_b, True)
        y_m = mlstm_output(hf, hb, mo, g_mlstm[l])

        ctx_keys = mla_keys(ckvc, krc, g_kv_norm[l], w_ukv[l], None)
        lat_keys = mla_keys(ckv, kr, g_kv_norm[l], w_ukv[l], rope_lat)
        qn, qr = mla_queries(cq, g_q_norm[l], w_uq[l], rope_lat)
        y_a = merge_heads(blocked_attend(qn, qr, (lat_keys, ctx_keys)))

        x = x + ga1 * (jnp.concatenate([y_f, y_m, y_a], axis=-1) @ w_out[l])
        x = x + ga2 * sqrelu_mlp(modulate(rmsnorm(x, g_norm2[l]), sh2, sc2), w_up[l], w_down[l])

        if not last:
            y_fc = fourier_mix(pfc)
            y_mc = mlstm_output(hcf, hcb, moc, g_mlstm[l])
            qn_c, qr_c = mla_queries(cqc, g_q_norm[l], w_uq[l], None)
            y_ac = merge_heads(softmax_attend(qn_c, qr_c, (ctx_keys,)))
            xc = xc + ga1c * (jnp.concatenate([y_fc, y_mc, y_ac], axis=-1) @ w_out[l])
            xc = xc + ga2c * sqrelu_mlp(modulate(rmsnorm(xc, g_norm2[l]), sh2c, sc2c), w_up[l], w_down[l])

    return rmsnorm(x, g_final)


N_META = 16
MIX_WIDTH_2 = D_MODEL
FOX_WIDTH = MIX_WIDTH_2 // 2
RET_WIDTH = MIX_WIDTH_2 - FOX_WIDTH
FOX_HEAD_DIM = 64
FOX_HEADS = FOX_WIDTH // FOX_HEAD_DIM
RET_HEADS = 4
RET_HEAD_DIM = RET_WIDTH // RET_HEADS
D_FF = -(-8 * D_MODEL // (3 * 256)) * 256
BLOCK_Q = 128
RET_CHUNK = 128
ROPE_BASE = 10000.0
FGATE_BIAS_MEAN = 3.0
RET_LOG_GAMMA = tuple(math.log(1.0 - 2.0 ** (-5 - h)) for h in range(RET_HEADS))
IN_SIZES = (FOX_WIDTH, FOX_WIDTH, FOX_WIDTH, FOX_HEADS, RET_WIDTH, RET_WIDTH, RET_WIDTH, RET_WIDTH)
IN_COLS = sum(IN_SIZES)
SPLIT_POINTS = tuple(int(v) for v in np.cumsum(IN_SIZES)[:-1])


def rmsnorm_2(x, g):
    x32 = x.astype(jnp.float32)
    y = x32 * lax.rsqrt(jnp.mean(x32 * x32, axis=-1, keepdims=True) + EPS)
    return (y * g.astype(jnp.float32)).astype(x.dtype)

def rotate(x, cos, sin):
    half = x.shape[-1] // 2
    x1, x2 = x[..., :half], x[..., half:]
    c = cos[None, :, None, :].astype(x.dtype)
    s = sin[None, :, None, :].astype(x.dtype)
    return jnp.concatenate([x1 * c - x2 * s, x1 * s + x2 * c], axis=-1)

def fox_attention(q, k, v, logf):
    B, L, H, Dh = q.shape
    scale = Dh ** -0.5
    c = jnp.cumsum(logf, axis=1).transpose(0, 2, 1)
    qh = q.transpose(0, 2, 1, 3)
    kh = k.transpose(0, 2, 1, 3)
    vh = v.transpose(0, 2, 1, 3)
    pos = jnp.arange(L)

    def attend(q_blk, c_q, q_pos, k_, v_, c_k, k_pos):
        s = jnp.einsum('bhqd,bhkd->bhqk', q_blk, k_).astype(jnp.float32) * scale
        s = s + c_q[..., :, None] - c_k[..., None, :]
        s = jnp.where(k_pos[None, :] <= q_pos[:, None], s, -jnp.inf)
        p = jax.nn.softmax(s, axis=-1)
        return jnp.einsum('bhqk,bhkd->bhqd', p.astype(v_.dtype), v_)

    meta_out = attend(qh[:, :, :N_META], c[:, :, :N_META], pos[:N_META],
                      kh[:, :, :N_META], vh[:, :, :N_META], c[:, :, :N_META], pos[:N_META])
    n_blk = (L - N_META) // BLOCK_Q
    q_real = qh[:, :, N_META:].reshape(B, H, n_blk, BLOCK_Q, Dh).transpose(2, 0, 1, 3, 4)
    c_real = c[:, :, N_META:].reshape(B, H, n_blk, BLOCK_Q).transpose(2, 0, 1, 3)
    pos_real = pos[N_META:].reshape(n_blk, BLOCK_Q)
    real_out = lax.map(lambda a: attend(a[0], a[1], a[2], kh, vh, c, pos),
                       (q_real, c_real, pos_real))
    real_out = real_out.transpose(1, 2, 0, 3, 4).reshape(B, H, L - N_META, Dh)
    out = jnp.concatenate([meta_out, real_out], axis=2)
    return out.transpose(0, 2, 1, 3)

def retention_chunkwise(q, k, v):
    B, L, H, Dh = q.shape
    log_g = jnp.array(RET_LOG_GAMMA, dtype=jnp.float32)

    def intra(qc, kc, vc, n):
        idx = jnp.arange(n)
        diff = idx[:, None] - idx[None, :]
        dec = jnp.where(diff >= 0,
                        jnp.exp(jnp.maximum(diff, 0)[None].astype(jnp.float32) * log_g[:, None, None]),
                        0.0)
        s = jnp.einsum('bnhd,bmhd->bhnm', qc, kc).astype(jnp.float32) * dec
        return jnp.einsum('bhnm,bmhd->bnhd', s, vc.astype(jnp.float32))

    qm, km, vm = q[:, :N_META], k[:, :N_META], v[:, :N_META]
    o_meta = intra(qm, km, vm, N_META)
    m_idx = jnp.arange(N_META, dtype=jnp.float32)
    k_dec_meta = jnp.exp((N_META - 1 - m_idx)[:, None] * log_g[None, :])
    state0 = jnp.einsum('bmhd,bmhe->bhde', km.astype(jnp.float32) * k_dec_meta[None, :, :, None],
                        vm.astype(jnp.float32))

    C = RET_CHUNK
    n_chunks = (L - N_META) // C
    j_idx = jnp.arange(C, dtype=jnp.float32)
    q_dec = jnp.exp((j_idx + 1.0)[:, None] * log_g[None, :])[None, :, :, None]
    k_dec = jnp.exp((C - 1.0 - j_idx)[:, None] * log_g[None, :])[None, :, :, None]
    chunk_dec = jnp.exp(C * log_g)[None, :, None, None]

    def to_chunks(t):
        return t[:, N_META:].reshape(B, n_chunks, C, H, Dh).transpose(1, 0, 2, 3, 4)

    def step(state, xs):
        qc, kc, vc = xs
        o = intra(qc, kc, vc, C) + jnp.einsum('bjhd,bhde->bjhe', qc.astype(jnp.float32) * q_dec, state)
        state = chunk_dec * state + jnp.einsum('bjhd,bjhe->bhde', kc.astype(jnp.float32) * k_dec,
                                               vc.astype(jnp.float32))
        return state, o

    _, o_real = lax.scan(step, state0, (to_chunks(q), to_chunks(k), to_chunks(v)))
    o_real = o_real.transpose(1, 0, 2, 3, 4).reshape(B, L - N_META, H, Dh)
    return jnp.concatenate([o_meta, o_real], axis=1)

def head_groupnorm(o, g):
    mu = jnp.mean(o, axis=-1, keepdims=True)
    var = jnp.mean(jnp.square(o - mu), axis=-1, keepdims=True)
    y = (o - mu) * lax.rsqrt(var + EPS)
    B, L, H, Dh = o.shape
    return y.reshape(B, L, H * Dh) * g.astype(jnp.float32)

def hybrid_layer(h, attn_norm_g, w_in, b_fgate, ret_gn_g, w_out,
                 ffn_norm_g, w_gate, w_up, w_down, cos, sin):
    B, L, _ = h.shape
    xn = rmsnorm_2(h, attn_norm_g)
    proj = jnp.einsum('bld,dc->blc', xn, w_in)
    fq, fk, fv, flog, rq, rk, rv, rg = jnp.split(proj, SPLIT_POINTS, axis=-1)

    logf = jax.nn.log_sigmoid(flog.astype(jnp.float32) + b_fgate.astype(jnp.float32))
    fshape = (B, L, FOX_HEADS, FOX_HEAD_DIM)
    fox_out = fox_attention(fq.reshape(fshape), fk.reshape(fshape), fv.reshape(fshape), logf)
    fox_out = fox_out.reshape(B, L, FOX_WIDTH)

    rshape = (B, L, RET_HEADS, RET_HEAD_DIM)
    rq_ = rotate(rq.reshape(rshape), cos, sin)
    rk_ = rotate(rk.reshape(rshape), cos, sin) * (RET_HEAD_DIM ** -0.5)
    ret = retention_chunkwise(rq_, rk_, rv.reshape(rshape))
    ret = head_groupnorm(ret, ret_gn_g).astype(h.dtype)
    ret_out = jax.nn.silu(rg) * ret

    mix = jnp.concatenate([fox_out, ret_out], axis=-1)
    h = h + jnp.einsum('blc,cd->bld', mix, w_out)

    hn = rmsnorm_2(h, ffn_norm_g)
    ff = jax.nn.silu(jnp.einsum('bld,df->blf', hn, w_gate)) * jnp.einsum('bld,df->blf', hn, w_up)
    return h + jnp.einsum('blf,fd->bld', ff, w_down)

def second_inputs(seed: int = 0) -> dict:
    key = jax.random.key(seed)
    ks = jax.random.split(key, 12)
    f32 = jnp.float32
    x = jax.random.normal(ks[0], (BATCH, SEQ, D_MODEL), f32)
    meta_tokens = jax.random.normal(ks[1], (N_META, D_MODEL), f32)
    attn_norm = 1.0 + 0.02 * jax.random.normal(ks[2], (DEPTH, D_MODEL), f32)
    w_in = jax.random.normal(ks[3], (DEPTH, D_MODEL, IN_COLS), f32) * D_MODEL ** -0.5
    b_fgate = FGATE_BIAS_MEAN + 0.5 * jax.random.normal(ks[4], (DEPTH, FOX_HEADS), f32)
    ret_gn = 1.0 + 0.02 * jax.random.normal(ks[5], (DEPTH, RET_WIDTH), f32)
    w_out = jax.random.normal(ks[6], (DEPTH, MIX_WIDTH_2, D_MODEL), f32) * MIX_WIDTH_2 ** -0.5
    ffn_norm = 1.0 + 0.02 * jax.random.normal(ks[7], (DEPTH, D_MODEL), f32)
    w_gate = jax.random.normal(ks[8], (DEPTH, D_MODEL, D_FF), f32) * D_MODEL ** -0.5
    w_up = jax.random.normal(ks[9], (DEPTH, D_MODEL, D_FF), f32) * D_MODEL ** -0.5
    w_down = jax.random.normal(ks[10], (DEPTH, D_FF, D_MODEL), f32) * D_FF ** -0.5
    final_norm = 1.0 + 0.02 * jax.random.normal(ks[11], (D_MODEL,), f32)
    return {"x": x, "meta_tokens": meta_tokens, "attn_norm": attn_norm, "w_in": w_in,
            "b_fgate": b_fgate, "ret_gn": ret_gn, "w_out": w_out, "ffn_norm": ffn_norm,
            "w_gate": w_gate, "w_up": w_up, "w_down": w_down, "final_norm": final_norm}

def second_block(x, meta_tokens, attn_norm, w_in, b_fgate, ret_gn, w_out, ffn_norm,
              w_gate, w_up, w_down, final_norm):
    B = x.shape[0]
    meta = jnp.broadcast_to(meta_tokens[None].astype(x.dtype), (B, N_META, D_MODEL))
    h = jnp.concatenate([meta, x], axis=1)
    L = h.shape[1]
    inv_freq = ROPE_BASE ** (-jnp.arange(0, RET_HEAD_DIM, 2, dtype=jnp.float32) / RET_HEAD_DIM)
    ang = jnp.arange(L, dtype=jnp.float32)[:, None] * inv_freq[None, :]
    cos, sin = jnp.cos(ang), jnp.sin(ang)
    for i in range(DEPTH):
        h = hybrid_layer(h, attn_norm[i], w_in[i], b_fgate[i], ret_gn[i], w_out[i],
                         ffn_norm[i], w_gate[i], w_up[i], w_down[i], cos, sin)
    h = rmsnorm_2(h, final_norm)
    return h[:, N_META:]


def setup_inputs(seed=0):
    out = dict(first_inputs(seed))
    for name, value in second_inputs(seed + 1).items():
        if name != "x":
            out[name + "_2"] = value
    return out


def reference(
    x, c, ctx, c_ctx, w_mod, b_mod, g_norm1, g_norm2, w_in, b_gates, conv_qk, g_mlstm, g_q_norm,
    g_kv_norm, w_uq, w_ukv, w_out, w_up, w_down, g_final, meta_tokens_2, attn_norm_2, w_in_2,
    b_fgate_2, ret_gn_2, w_out_2, ffn_norm_2, w_gate_2, w_up_2, w_down_2, final_norm_2,
):
    x = first_block(
        x, c, ctx, c_ctx, w_mod, b_mod, g_norm1, g_norm2, w_in, b_gates, conv_qk, g_mlstm,
        g_q_norm, g_kv_norm, w_uq, w_ukv, w_out, w_up, w_down, g_final,
    )
    return second_block(
        x, meta_tokens_2, attn_norm_2, w_in_2, b_fgate_2, ret_gn_2, w_out_2, ffn_norm_2,
        w_gate_2, w_up_2, w_down_2, final_norm_2,
    )


_drawn_inputs = setup_inputs


def setup_inputs(seed=0):
    import zlib

    import numpy as np

    out = dict(_drawn_inputs(seed))
    spreads = {}
    factors = {'g_norm1': 7.477,
     'g_norm2': 2.779,
     'g_mlstm': 8.0,
     'g_q_norm': 8.0,
     'g_kv_norm': 8.0,
     'ret_gn_2': 4.704,
     'ffn_norm_2': 2.848}
    for name, (base, spread) in spreads.items():
        noise = np.random.default_rng([zlib.crc32(name.encode()), seed]).standard_normal(out[name].shape)
        drawn = base * np.exp(spread * noise) if base else spread * noise
        out[name] = __import__('jax').numpy.asarray(drawn.astype(out[name].dtype))
    for name, factor in factors.items():
        out[name] = (out[name] * factor).astype(out[name].dtype)
    return out
```

```python
from contextlib import ExitStack, contextmanager

import numpy as np
import concourse.bass as bass
from concourse import mybir

F32 = mybir.dt.float32
F32R = mybir.dt.float32r
ALU = mybir.AluOpType
ACT = mybir.ActivationFunctionType
AX = mybir.AxisListType

P = 128
D = 1024
KT = D // P
DEPTH = 2
EPS = 1e-6
LAT, CTX = 512, 256
ALL = LAT + CTX
LT, CT = LAT // P, CTX // P
TT = LT + CT

F_GROUP = D // 16
M_HEADS, M_DIM = 4, 3 * D // 32
A_HEADS, A_NOPE, A_ROPE, A_V = 4, 64, 32, 3 * D // 32
A_QK = A_NOPE + A_ROPE
Q_LORA, KV_LORA = D // 4, D // 8
CONV = 5
GRID_W = 64
HID = 4 * D // P

META = 16
SEQ2 = LAT + META
FOX_HEADS, FOX_DIM = 8, 64
RET_HEADS, RET_DIM = 4, 128
FF = 2816 // P
LOG_GAMMA = [float(np.log(1.0 - 2.0 ** (-5 - h))) for h in range(RET_HEADS)]

BLOCK = 8 * P
RING = 4
SPLIT = 2
UNROLL = 4
BUFS = 2
ROWS = 36
FWD, BWD = 0, 32
F_ROW = 64
NEG = -1.0e30

MOD_BLOCKS, MOD_RING, MOD_FIRST = 6 * D // P, 4, 2 * D // P
FOURIER_BLOCKS, LATENT_BLOCKS = 2, 4
MLSTM_BLOCKS = 2 * M_HEADS + 3 + 3 + 1
OUT_BLOCKS = KT
QUARTERS, Q_TILES = 4, HID // 4
MLP_BLOCKS = QUARTERS * (Q_TILES + KT)
FOX_BLOCKS, RET_BLOCKS = 13, 16
HALVES, H_TILES, H_KT = 2, FF // 2, (6, 5)
FFN_BLOCKS = HALVES * (2 * H_TILES + 2 * KT)
NARROW = H_KT[0] * P
LAYER1 = FOURIER_BLOCKS + LATENT_BLOCKS + MLSTM_BLOCKS + OUT_BLOCKS + MLP_BLOCKS
LAYER2 = FOX_BLOCKS + RET_BLOCKS + OUT_BLOCKS + FFN_BLOCKS
BLOCKS = DEPTH * (LAYER1 + LAYER2) + SPLIT

C_IDENT, C_LOWER, C_UPPER, C_DFT, C_END = 0, P, 2 * P, 3 * P, 5 * P
P_C = 0
P_BMOD = P_C + 2 * KT
P_G1 = P_BMOD + DEPTH * MOD_BLOCKS
P_G2 = P_G1 + DEPTH * KT
P_CONV = P_G2 + DEPTH * KT
P_BG = P_CONV + DEPTH * 2 * M_HEADS * CONV
P_GQ = P_BG + DEPTH * 2
P_GKV = P_GQ + DEPTH * 2
P_ANORM = P_GKV + DEPTH
P_FNORM = P_ANORM + DEPTH * KT
P_BF = P_FNORM + DEPTH * KT
P_FINAL = P_BF + DEPTH
P_GFINAL = P_FINAL + KT
P_END = P_GFINAL + KT
ARENA = 24500


class Counter:

    def __init__(self, sem):
        self.sem, self.base = sem, 0

    def at(self, n):
        return self.base + n

    def close(self, n):
        self.base += n


class Steps:

    def __init__(self, eng, count):
        self.eng, self.count, self.n = eng, count, 0

    def __call__(self, ins):
        self.n += 1
        ins.then_inc(self.count.sem, 1)
        self.eng.wait_ge(self.count.sem, self.count.at(self.n))


def whole_turns(t, i, inner):
    return (0, t * inner + i) if isinstance(t, int) else (t, i)


class Core:

    def __init__(self, nc, ctx, dram):
        self.nc, self.ctx, self.dram = nc, ctx, dram
        self.counters = {}

        def sb(name, shape, dtype=F32):
            return ctx.enter_context(nc.sbuf_tensor(name, shape, dtype))

        self.x = sb("x", [P, KT, ALL])
        self.sumsq = sb("sumsq", [P, ALL])
        self.ring = sb("ring", [P, RING, BLOCK])
        self.hi_ring = sb("hi_ring", [P, SPLIT, BLOCK], F32R)
        self.lo_ring = sb("lo_ring", [P, SPLIT, BLOCK], F32R)
        self.const = sb("const", [P, C_END])
        self.param = sb("param", [P, P_END])
        self.ones = sb("ones", [P, P])
        self.eps = sb("eps", [P, 1])
        self.silu_c = sb("silu_c", [P, KT, 2])
        self.mod = sb("mod", [P, 6, KT, 2])
        self.gain = sb("gain", [P, 2, KT, 2])
        self.ps = ctx.enter_context(nc.psum_tensor("ps", [P, 8, 512], F32))
        self.landed = [ctx.enter_context(nc.semaphore(f"block_landed_{i}")) for i in range(RING)]
        self.done = ctx.enter_context(nc.semaphore("block_done"))
        self.block0 = 0
        self.loaded = 0
        self.free = self.counter("psum_free")
        self.hi = ctx.enter_context(nc.semaphore("block_hi"))
        self.lo = ctx.enter_context(nc.semaphore("block_lo"))
        self.narrow = []
        self.mod_landed = [ctx.enter_context(nc.semaphore(f"mod_landed_{i}")) for i in range(MOD_RING)]
        self.mod_done = ctx.enter_context(nc.semaphore("mod_block_done"))
        self.added = self.counter("squares_added")
        self.mod_used = 0
        self.names = 0

    @contextmanager
    def space(self, name, shape, dtype=F32):
        self.names += 1
        with self.nc.sbuf_tensor(f"{name}_{self.names}", shape, dtype) as t:
            yield t

    def counter(self, name):
        if name not in self.counters:
            self.counters[name] = Counter(self.ctx.enter_context(self.nc.semaphore(name)))
        return self.counters[name]

    def ident(self, n):
        return self.const[0:n, C_IDENT:C_IDENT + n]

    def buf(self, j):
        j %= BUFS
        return self.ps[:, 2 * j:2 * j + 2, :].rearrange("p b n -> p (b n)")

    def width(self, g):
        return NARROW if any(a <= g < b for a, b in self.narrow) else BLOCK

    def feed(self, sp, n):
        n = min(n, BLOCKS - self.loaded)
        while n > 0:
            g = self.loaded
            end = next((c for r in self.narrow for c in r if c > g), BLOCKS)
            run = min(n, end - g)
            width = self.width(g)

            def load(t, i):
                slot = (g + i) % RING
                if g + i >= RING:
                    sp.wait_ge(self.lo, t * UNROLL + (g + i - RING + 1))
                sp.dma_start(self.ring[:, slot, 0:width],
                             self.dram["weights"][t * UNROLL + (g + i), :, 0:width]).then_inc(self.landed[slot], 16)

            if g < RING:
                for i in range(run):
                    load(0, i)
            else:
                tiles(sp, run, UNROLL, load)
            self.loaded += run
            n -= run

    def part_hi(self, act, t, i, inner=UNROLL):
        t, i = whole_turns(t, i, inner)
        g = self.block0 + i
        w = self.width(g)
        if g < BLOCKS:
            act.wait_ge(self.landed[g % RING], t * (16 * inner // RING) + 16 * (g // RING + 1))
            if g >= SPLIT:
                act.wait_ge(self.done, t * inner + (g - SPLIT + 1))
            self.nc.scalar.activation(self.hi_ring[:, g % SPLIT, 0:w], self.ring[:, g % RING, 0:w],
                                      ACT.Copy).then_inc(self.hi, 1)

    def part_lo(self, dve, t, i, inner=UNROLL):
        t, i = whole_turns(t, i, inner)
        g = self.block0 + i
        w = self.width(g)
        if g < BLOCKS:
            dve.wait_ge(self.hi, t * inner + (g + 1))
            self.nc.vector.tensor_tensor(self.lo_ring[:, g % SPLIT, 0:w], self.ring[:, g % RING, 0:w],
                                         self.hi_ring[:, g % SPLIT, 0:w], ALU.subtract).then_inc(self.lo, 1)

    def arrived(self, pe, t, i, inner=UNROLL):
        g = self.block0 + i
        pe.wait_ge(self.lo, t * inner + (g + 1))
        return self.hi_ring[:, g % SPLIT, :], self.lo_ring[:, g % SPLIT, :]

    def mod_load(self, pool, ring, t, i, inner=MOD_RING):
        g = self.mod_used + i
        if g >= MOD_RING:
            pool.wait_ge(self.mod_done, t * inner + (g - MOD_RING + 1))
        pool.dma_start(ring[:, g % MOD_RING, :],
                       self.dram["w_mod"][t * inner + g]).then_inc(self.mod_landed[g % MOD_RING], 16)

    def mod_feed(self, pool, ring, n):
        first = max(0, MOD_RING - self.mod_used)
        for i in range(first):
            self.mod_load(pool, ring, 0, i)
        tiles(pool, n - first, MOD_RING, lambda t, i: self.mod_load(pool, ring, t, first + i))

    def mod_finish(self, dve, l, used, b0, b1):
        nc = self.nc
        step = Steps(dve, self.counter("mod_steps"))
        dve.wait_ge(self.mod_done, self.mod_used + used)
        src = self.ps[:, 7, 0:2 * MOD_BLOCKS].rearrange("p (m c) -> p m c", c=2)[:, b0:b1, :]
        b = self.param[:, P_BMOD + l * MOD_BLOCKS + b0:P_BMOD + l * MOD_BLOCKS + b1]
        mod = self.mod[:].rearrange("p s k c -> p (s k) c")[:, b0:b1, :]
        step(nc.vector.tensor_tensor(mod, src, b[:, :, None].to_broadcast([P, b1 - b0, 2]), ALU.add))
        for n, (g, scale) in enumerate(((P_G1, 1), (P_G2, 4))):
            if b0 <= scale * KT < b1:
                gn = self.param[:, g + l * KT:g + (l + 1) * KT]
                step(nc.vector.scalar_tensor_tensor(self.gain[:, n, :, :], self.mod[:, scale, :, :], 1.0,
                                                    gn[:, :, None].to_broadcast([P, KT, 2]), ALU.add, ALU.mult))
        step.count.close(step.n)

    def mod_product(self, pe, ring, first, t, i, inner):
        g = self.mod_used + i
        pe.wait_ge(self.mod_landed[g % MOD_RING], t * (16 * inner // MOD_RING) + 16 * (g // MOD_RING + 1))
        out = self.ps[:, 7, 0:2 * MOD_BLOCKS].rearrange("p (m c) -> p m c", c=2)
        for k, wk in enumerate(by_tile(ring[:, g % MOD_RING, :], KT)):
            last = self.nc.tensor.matmul(out[:, t * inner + (first + i), :], wk, self.silu_c[:, k, :],
                                         start=k == 0, stop=k == KT - 1)
        last.then_inc(self.mod_done, 1)

    def computed(self, eng, t, i, inner=UNROLL):
        eng.wait_ge(self.done, t * inner + (self.block0 + i + 1))

    def close(self, blocks, outputs):
        self.block0 += blocks
        self.free.close(outputs)


def tiles(eng, n, unroll, body):
    full = n // unroll
    if full > 1:
        with eng.Fori(0, full) as t:
            for i in range(unroll):
                body(t, i)
    elif full:
        for i in range(unroll):
            body(0, i)
    for i in range(n - full * unroll):
        body(full, i)


def segments(tokens):
    if tokens == SEQ2:
        return [(0, 0, SEQ2 // 2), (512, SEQ2 // 2, SEQ2 // 2)]
    return [(c, c, min(512, tokens - c)) for c in range(0, tokens, 512)]


def in_psum(buf, tokens):
    if tokens == SEQ2:
        return buf.rearrange("p (b n) -> p b n", b=2)[:, :, 0:SEQ2 // 2]
    return buf[:, 0:tokens]


def like_psum(ap, tokens):
    return ap.rearrange("p (b n) -> p b n", b=2) if tokens == SEQ2 else ap


def product(nc, out, weights, acts, tokens, m, row=0, first=True, last=True):
    for c, t0, n in segments(tokens):
        for k, (w, a) in enumerate(zip(weights, acts)):
            ins = nc.tensor.matmul(out[row:row + m, c:c + n], w, a[:, t0:t0 + n],
                                   start=first and k == 0, stop=last and k == len(weights) - 1)
    return ins


def product_parts(nc, out, slots, kts, acts, tokens, m=P, first=True, last=True, before=None):
    w_hi, w_lo = (by_tile(s, kts, m) for s in slots)
    for k in range(kts):
        if before is not None:
            before(k)
        a_hi, a_lo = acts(k)
        for c, t0, n in segments(tokens):
            for p, (w, a) in enumerate(((w_hi, a_hi), (w_hi, a_lo), (w_lo, a_hi))):
                ins = nc.tensor.matmul(out[0:m, c:c + n], w[k], a[:, t0:t0 + n], start=first and k == 0 and p == 0,
                                       stop=last and k == kts - 1 and p == 2)
    return ins


def by_tile(slot, n, width=P):
    return [slot[:, k * width:(k + 1) * width] for k in range(n)]


class Alloc:

    def __init__(self, tensor, start=0):
        self.arena, self.at = tensor, start
        self.size = tensor.shape[1]

    def __call__(self, *shape):
        n = int(np.prod(shape))
        ap = self.arena[:, self.at:self.at + n]
        self.at += n
        assert self.at <= self.size, (self.at, self.size)
        if len(shape) == 2:
            ap = ap.rearrange("p (a b) -> p a b", a=shape[0])
        elif len(shape) == 3:
            ap = ap.rearrange("p (a b c) -> p a b c", a=shape[0], b=shape[1])
        return ap


def setup(core):
    nc, dram = core.nc, core.dram
    inputs = core.counter("inputs_in")
    ready = core.counter("setup_steps")
    sig = core.counter("sigmoid_c")
    made = core.counter("silu_c_ready")
    squares = core.counter("x_squared")
    sq = Squares(core, ALL)
    with core.space("mod_ring", [P, MOD_RING, BLOCK]) as ring, core.space("sq", [P, 2, ALL]) as tmp:
        with nc.Block(no_gpsimd_drain=True) as block:
            @block.sync
            def _(sp):
                sp.dma_start(core.param[:], dram["param"]).then_inc(inputs.sem, 16)
                sp.dma_start(core.x[:], dram["x"]).then_inc(inputs.sem, 16)
                core.feed(sp, RING)

            @block.gpsimd
            def _(pool):
                core.mod_feed(pool, ring, MOD_FIRST)
                for m in range(KT):
                    sq.add(pool, tmp, m)

            @block.tensor
            def _(pe):
                pe.wait_ge(made.sem, made.at(1))
                tiles(pe, MOD_FIRST, MOD_RING, lambda t, i: core.mod_product(pe, ring, 0, t, i, MOD_RING))

            @block.scalar
            def _(act):
                act.dma_start(core.const[:], dram["const"]).then_inc(inputs.sem, 16)
                act.wait_ge(inputs.sem, 48)
                nc.scalar.activation(core.silu_c[:], core.param[:, P_C:P_C + 2 * KT].rearrange("p (k c) -> p k c", c=2),
                                     ACT.Sigmoid).then_inc(sig.sem, 1)
                for i in range(SPLIT):
                    core.part_hi(act, 0, i)
                for m in range(KT):
                    sq.square(act, tmp, m)

            @block.vector
            def _(dve):
                step = Steps(dve, ready)
                step(nc.vector.memset(core.ones[:], 1.0))
                for n in range(BUFS):
                    nc.vector.memset(core.eps[:], EPS).then_inc(core.free.sem, 1)
                    dve.wait_ge(core.free.sem, n + 1)
                dve.wait_ge(inputs.sem, 48)
                dve.wait_ge(sig.sem, 1)
                nc.vector.tensor_tensor(core.silu_c[:], core.silu_c[:],
                                        core.param[:, P_C:P_C + 2 * KT].rearrange("p (k c) -> p k c", c=2),
                                        ALU.mult).then_inc(made.sem, 1)
                for i in range(SPLIT):
                    core.part_lo(dve, 0, i)
                core.mod_finish(dve, 0, MOD_FIRST, 0, MOD_FIRST)
    ready.close(1)
    inputs.close(48)
    core.mod_used += MOD_FIRST
    sq.close(KT)


class Squares:

    def __init__(self, core, tokens):
        self.core, self.tokens = core, tokens
        self.squared = core.counter("tile_squared")

    def square(self, act, tmp, m, i=None, t=0, inner=0):
        core, n = self.core, self.tokens
        i = m if i is None else i
        act.wait_ge(core.added.sem, t * inner + core.added.at(max(i - 1, 0)))
        core.nc.scalar.activation(tmp[:, i % 2, 0:n], core.x[:, m, 0:n], ACT.Square).then_inc(self.squared.sem, 1)

    def add(self, pool, tmp, m, i=None, t=0, inner=0, fresh=None):
        core, n = self.core, self.tokens
        i = m if i is None else i
        pool.wait_ge(self.squared.sem, t * inner + self.squared.at(i + 1))
        pool.wait_ge(core.added.sem, t * inner + core.added.at(i))
        dst, src = core.sumsq[:, 0:n], tmp[:, i % 2, 0:n]
        if m == 0 if fresh is None else fresh:
            if isinstance(t, int):
                ins = core.nc.gpsimd.tensor_copy(dst, src)
            else:
                ins = core.nc.gpsimd.tensor_tensor(dst, src, core.ones[:, 0:1].to_broadcast([P, n]), ALU.mult)
            ins.then_inc(core.added.sem, 1)
        else:
            core.nc.gpsimd.tensor_tensor(dst, dst, src, ALU.add).then_inc(core.added.sem, 1)

    def close(self, n):
        self.squared.close(n)
        self.core.added.close(n)


class Norm:

    def __init__(self, core, tokens, gains, shifts, groups, h):
        self.core, self.tokens, self.gains, self.shifts, self.groups = core, tokens, gains, shifts, groups
        self.h_hi, self.h_lo = h
        self.summed, self.root, self.inverse, self.made, self.hi, self.ready = (
            core.counter("norm_" + n) for n in ("summed", "root", "inverse", "made", "hi", "ready"))
        self.acc = core.ps[:, 4:6, :].rearrange("p b n -> p (b n)")

    def on_pe(self, pe):
        core = self.core
        pe.wait_ge(core.added.sem, core.added.at(0))
        product(core.nc, self.acc, [core.ones[:]], [core.sumsq[:]], self.tokens, P).then_inc(self.summed.sem, 1)

    def on_act(self, act):
        core, n, groups = self.core, self.tokens, self.groups
        act.wait_ge(self.summed.sem, self.summed.at(1))
        core.nc.scalar.activation(like_psum(core.sumsq[:, 0:n], n), in_psum(self.acc, n), ACT.Sqrt,
                                  bias=core.eps[:, 0:1], scale=1.0 / D).then_inc(self.root.sem, 1)
        for k in range(KT):
            act.wait_ge(self.made.sem, self.made.at(k + 1))
            for t0, t1, c in groups:
                src = self.tmp[:, k % 2, t0:t1]
                if self.shifts is None:
                    ins = core.nc.scalar.activation(self.h_hi[:, k, t0:t1], src, ACT.Copy)
                else:
                    ins = core.nc.scalar.activation(self.h_hi[:, k, t0:t1], src, ACT.Identity,
                                                    bias=self.shifts(k, c))
            ins.then_inc(self.hi.sem, 1)

    def on_dve(self, dve, tmp):
        core, n, groups, v = self.core, self.tokens, self.groups, self.core.nc.vector
        dve.wait_ge(self.root.sem, self.root.at(1))
        v.reciprocal(core.sumsq[:, 0:n], core.sumsq[:, 0:n]).then_inc(self.inverse.sem, 1)
        dve.wait_ge(self.inverse.sem, self.inverse.at(1))

        def rest(k):
            dve.wait_ge(self.hi.sem, self.hi.at(k + 1))
            for t0, t1, c in groups:
                src, hi, lo = tmp[:, k % 2, t0:t1], self.h_hi[:, k, t0:t1], self.h_lo[:, k, t0:t1]
                if self.shifts is None:
                    ins = v.tensor_tensor(lo, src, hi, ALU.subtract)
                else:
                    ins = v.scalar_tensor_tensor(lo, src, self.shifts(k, c), hi, ALU.add, ALU.subtract)
            ins.then_inc(self.ready.sem, 1)

        for k in range(KT):
            if k >= 2:
                dve.wait_ge(self.ready.sem, self.ready.at(k - 1))
            for t0, t1, c in groups:
                ins = v.scalar_tensor_tensor(tmp[:, k % 2, t0:t1], core.x[:, k, t0:t1], self.gains(k, c),
                                             core.sumsq[:, t0:t1], ALU.mult, ALU.mult)
            ins.then_inc(self.made.sem, 1)
            if k:
                rest(k - 1)
        dve.wait_ge(self.made.sem, self.made.at(KT))
        rest(KT - 1)

    def wait_tile(self, pe):
        return lambda k: pe.wait_ge(self.ready.sem, self.ready.at(k + 1))

    def close(self):
        for c, n in ((self.summed, 1), (self.root, 1), (self.inverse, 1), (self.made, KT), (self.hi, KT),
                     (self.ready, KT)):
            c.close(n)


def plain_norm(core, tokens, gain, to):
    nc = core.nc
    summed, root, steps = core.counter("norm_summed"), core.counter("norm_root"), core.counter("norm_steps")
    acc = core.ps[:, 4:6, :].rearrange("p b n -> p (b n)")
    s = core.sumsq[:, 0:tokens]
    with nc.Block(no_gpsimd_drain=True) as block:
        @block.tensor
        def _(pe):
            pe.wait_ge(core.added.sem, core.added.at(0))
            product(nc, acc, [core.ones[:]], [core.sumsq[:]], tokens, P).then_inc(summed.sem, 1)

        @block.scalar
        def _(act):
            act.wait_ge(summed.sem, summed.at(1))
            nc.scalar.activation(s, acc[:, 0:tokens], ACT.Sqrt, bias=core.eps[:, 0:1],
                                 scale=1.0 / D).then_inc(root.sem, 1)

        @block.vector
        def _(dve):
            step = Steps(dve, steps)
            dve.wait_ge(root.sem, root.at(1))
            step(nc.vector.reciprocal(s, s))
            for k in range(KT):
                last = nc.vector.scalar_tensor_tensor(to[:, k, 0:tokens], core.x[:, k, 0:tokens],
                                                      core.param[:, gain + k:gain + k + 1], s, ALU.mult, ALU.mult)
            step(last)
    summed.close(1)
    root.close(1)
    steps.close(2)


def add_output(core, dve, dst_tile, src, tokens, groups, gate):
    v = core.nc.vector
    for t0, t1, c in groups:
        dst = like_psum(dst_tile[:, t0:t1], tokens)
        s = in_psum(src, tokens) if tokens == SEQ2 else src[:, t0:t1]
        if gate is None:
            ins = v.tensor_tensor(dst, s, dst, ALU.add)
        else:
            ins = v.scalar_tensor_tensor(dst, s, gate(c), dst, ALU.mult, ALU.add)
    return ins


def out_projection(core, h, mix, tokens, gates, groups, tmp):
    nc = core.nc
    h_hi, h_lo = h
    hi, ready = core.counter("mix_hi"), core.counter("mix_ready")
    sq = Squares(core, tokens)
    with nc.Block(no_gpsimd_drain=True) as block:
        @block.sync
        def _(sp):
            core.feed(sp, OUT_BLOCKS)

        @block.gpsimd
        def _(pool):
            for m in range(KT):
                sq.add(pool, tmp, m)

        @block.tensor
        def _(pe):
            for i in range(OUT_BLOCKS):
                w = core.arrived(pe, 0, i)
                pe.wait_ge(core.free.sem, core.free.at(i + 1))
                product_parts(nc, core.buf(i), w, KT, lambda k: (h_hi[:, k, :], h_lo[:, k, :]), tokens,
                              before=None if mix is None else lambda k: pe.wait_ge(ready.sem, ready.at(k + 1))
                              ).then_inc(core.done, 1)

        @block.scalar
        def _(act):
            if mix is not None:
                for k in range(KT):
                    nc.scalar.activation(h_hi[:, k, 0:tokens], mix[:, k, 0:tokens], ACT.Copy).then_inc(hi.sem, 1)
            for i in range(OUT_BLOCKS):
                core.part_hi(act, 0, i + SPLIT)
                act.wait_ge(core.free.sem, core.free.at(BUFS + i + 1))
                sq.square(act, tmp, i)

        @block.vector
        def _(dve):
            if mix is not None:
                for k in range(KT):
                    dve.wait_ge(hi.sem, hi.at(k + 1))
                    nc.vector.tensor_tensor(h_lo[:, k, 0:tokens], mix[:, k, 0:tokens], h_hi[:, k, 0:tokens],
                                            ALU.subtract).then_inc(ready.sem, 1)
            for i in range(OUT_BLOCKS):
                core.part_lo(dve, 0, i + SPLIT)
                core.computed(dve, 0, i)
                add_output(core, dve, core.x[:, i, :], core.buf(i), tokens, groups,
                           None if gates is None else lambda c: gates(i, c)).then_inc(core.free.sem, 1)
    core.close(OUT_BLOCKS, OUT_BLOCKS)
    sq.close(KT)
    if mix is not None:
        hi.close(KT)
        ready.close(KT)


def squared_relu_mlp(core, norm, acts, tokens, gates, groups, mods):
    nc = core.nc
    per = Q_TILES + KT
    per_mod = MOD_BLOCKS // QUARTERS
    squared = core.counter("hidden_squared")
    hi, ready = core.counter("hidden_hi"), core.counter("hidden_ready")
    sq = Squares(core, tokens)
    with ExitStack() as ctx:
        hid_hi, hid_lo = (ctx.enter_context(core.space(n, [P, Q_TILES, ALL], F32R)) for n in ("hid_hi", "hid_lo"))
        tmp = ctx.enter_context(core.space("tmp", [P, 2, ALL]))
        sqt = ctx.enter_context(core.space("sq", [P, 2, ALL]))
        ring = ctx.enter_context(core.space("mod_ring", [P, MOD_RING, BLOCK])) if mods else None
        norm.tmp = tmp
        with nc.Block(no_gpsimd_drain=True) as block:
            @block.sync
            def _(sp):
                core.feed(sp, MLP_BLOCKS)

            @block.gpsimd
            def _(pool):
                pool.wait_ge(norm.ready.sem, norm.ready.at(KT))
                with pool.Fori(0, QUARTERS) as t:
                    if mods:
                        for i in range(per_mod):
                            core.mod_load(pool, ring, t, i, per_mod)
                    for m in range(KT):
                        sq.add(pool, sqt, m, t=t, inner=KT)

            @block.tensor
            def _(pe):
                norm.on_pe(pe)
                with pe.Fori(0, QUARTERS) as t:
                    for i in range(per):
                        up = i < Q_TILES
                        w = core.arrived(pe, t, i, per)
                        pe.wait_ge(core.free.sem, t * per + core.free.at(i + 1))
                        if up:
                            product_parts(nc, core.buf(i), w, KT, acts, tokens,
                                          before=norm.wait_tile(pe) if i == 0 else None).then_inc(core.done, 1)
                        else:
                            before = lambda k: pe.wait_ge(ready.sem, t * Q_TILES + ready.at(k + 1))
                            product_parts(nc, core.buf(i), w, Q_TILES, lambda k: (hid_hi[:, k, :], hid_lo[:, k, :]),
                                          tokens, before=before if i == Q_TILES else None).then_inc(core.done, 1)
                        if mods and i < per_mod:
                            core.mod_product(pe, ring, 0, t, i, per_mod)

            @block.scalar
            def _(act):
                norm.on_act(act)
                with act.Fori(0, QUARTERS) as t:
                    for i in range(per):
                        core.part_hi(act, t, i + SPLIT, per)
                        if i < Q_TILES:
                            core.computed(act, t, i, per)
                            if i == 0:
                                act.wait_ge(core.free.sem, t * per + core.free.at(BUFS))
                            act.wait_ge(ready.sem, t * Q_TILES + ready.at(max(i - 1, 0)))
                            r = tmp[:, i % 2, 0:tokens]
                            nc.scalar.activation(r, core.buf(i)[:, 0:tokens], ACT.Relu).then_inc(core.free.sem, 1)
                            act.wait_ge(core.free.sem, t * per + core.free.at(BUFS + i + 1))
                            nc.scalar.activation(r, r, ACT.Square).then_inc(squared.sem, 1)
                        else:
                            act.wait_ge(core.free.sem, t * per + core.free.at(BUFS + i + 1))
                            sq.square(act, sqt, i - Q_TILES, t=t, inner=KT)

            @block.vector
            def _(dve):
                norm.on_dve(dve, tmp)
                with dve.Fori(0, QUARTERS) as t:
                    for i in range(per):
                        core.part_lo(dve, t, i + SPLIT, per)
                        if i < Q_TILES:
                            r = tmp[:, i % 2, 0:tokens]
                            dve.wait_ge(squared.sem, t * Q_TILES + squared.at(i + 1))
                            nc.vector.tensor_copy(hid_hi[:, i, 0:tokens], r).then_inc(hi.sem, 1)
                            dve.wait_ge(hi.sem, t * Q_TILES + hi.at(i + 1))
                            nc.vector.tensor_tensor(hid_lo[:, i, 0:tokens], r, hid_hi[:, i, 0:tokens],
                                                    ALU.subtract).then_inc(ready.sem, 1)
                        else:
                            m = i - Q_TILES
                            core.computed(dve, t, i, per)
                            if m == 0:
                                dve.wait_ge(core.free.sem, t * per + core.free.at(BUFS + Q_TILES))
                            add_output(core, dve, core.x[:, m, :], core.buf(i), tokens, groups,
                                       lambda c: gates(m, c)).then_inc(core.free.sem, 1)
                if mods:
                    dve.wait_ge(core.free.sem, core.free.at(BUFS + QUARTERS * per))
                    core.mod_finish(dve, 1, MOD_BLOCKS, 0, MOD_BLOCKS)
    core.close(MLP_BLOCKS, QUARTERS * per)
    for c, n in ((squared, Q_TILES), (hi, Q_TILES), (ready, Q_TILES)):
        c.close(n * QUARTERS)
    sq.close(KT * QUARTERS)
    norm.close()
    if mods:
        core.mod_used += MOD_BLOCKS


def swiglu_mlp(core, norm, acts):
    nc = core.nc
    n_up, n_down = 2 * H_TILES, 2 * KT
    outs = n_up + KT
    sigmoid = core.counter("gate_sigmoid")
    product_ready = core.counter("hidden_product")
    hi, ready = core.counter("hidden_hi"), core.counter("hidden_ready")
    cleared = core.counter("sumsq_cleared")
    sq = Squares(core, SEQ2)
    with ExitStack() as ctx:
        hid_hi, hid_lo = (ctx.enter_context(core.space(n, [P, H_TILES, SEQ2], F32R)) for n in ("hid_hi", "hid_lo"))
        tmp = ctx.enter_context(core.space("tmp", [P, 2, SEQ2]))
        sqt = ctx.enter_context(core.space("sq", [P, 2, SEQ2]))
        norm.tmp = tmp
        with nc.Block(no_gpsimd_drain=True) as block:
            @block.sync
            def _(sp):
                core.feed(sp, FFN_BLOCKS)

            @block.gpsimd
            def _(pool):
                pool.wait_ge(norm.ready.sem, norm.ready.at(KT))
                for half in range(HALVES):
                    if half:
                        pool.wait_ge(core.added.sem, core.added.at(half * KT))
                    nc.gpsimd.memset(core.sumsq[:, 0:SEQ2], 0.0).then_inc(cleared.sem, 1)
                    pool.wait_ge(cleared.sem, cleared.at(half + 1))
                    with pool.Fori(0, KT // 2) as t:
                        for o in range(2):
                            sq.add(pool, sqt, o, i=half * KT + o, t=t, inner=2, fresh=False)

            @block.tensor
            def _(pe):
                norm.on_pe(pe)
                for half in range(HALVES):
                    b0, f0 = half * (n_up + n_down), half * outs

                    def up(t, i):
                        w = core.arrived(pe, t, b0 + i)
                        pe.wait_ge(core.free.sem, t * UNROLL + core.free.at(f0 + i + 1))
                        product_parts(nc, core.buf(i), w, KT, acts, SEQ2,
                                      before=norm.wait_tile(pe) if i == 0 and half == 0 else None
                                      ).then_inc(core.done, 1)

                    def down(t, i):
                        o, p = divmod(i, 2)
                        w = core.arrived(pe, t, b0 + n_up + i)
                        if p == 0:
                            pe.wait_ge(core.free.sem, t * 2 + core.free.at(f0 + n_up + o + 1))
                        k0 = p * H_KT[0]
                        product_parts(nc, core.buf(o), w, H_KT[p], lambda k: (hid_hi[:, k0 + k, :], hid_lo[:, k0 + k, :]),
                                      SEQ2, first=p == 0, last=p == 1,
                                      before=lambda k: pe.wait_ge(ready.sem, ready.at(half * H_TILES + k0 + k + 1))
                                      ).then_inc(core.done, 1)

                    tiles(pe, n_up, UNROLL, up)
                    tiles(pe, n_down, UNROLL, down)

            @block.scalar
            def _(act):
                norm.on_act(act)
                for half in range(HALVES):
                    b0, f0 = half * (n_up + n_down), half * outs

                    def pair(t, i):
                        core.part_hi(act, t, b0 + 2 * i + SPLIT)
                        core.computed(act, t, b0 + 2 * i)
                        act.wait_ge(ready.sem, t * 2 + ready.at(half * H_TILES + max(i - 1, 0)))
                        nc.scalar.activation(like_psum(tmp[:, i % 2, :], SEQ2), in_psum(core.buf(0), SEQ2),
                                             ACT.Sigmoid).then_inc(sigmoid.sem, 1)
                        core.part_hi(act, t, b0 + 2 * i + 1 + SPLIT)

                    def out(t, i):
                        o, p = divmod(i, 2)
                        core.part_hi(act, t, b0 + n_up + i + SPLIT)
                        if p:
                            act.wait_ge(core.free.sem, t * 2 + core.free.at(f0 + n_up + BUFS + o + 1))
                            sq.square(act, sqt, t * 2 + o, i=half * KT + o, t=t, inner=2)

                    tiles(act, H_TILES, 2, pair)
                    tiles(act, n_down - UNROLL, UNROLL, out)
                    for i in range(UNROLL):
                        out((n_down - UNROLL) // UNROLL, i)

            @block.vector
            def _(dve):
                v = nc.vector
                norm.on_dve(dve, tmp)
                for half in range(HALVES):
                    b0, f0 = half * (n_up + n_down), half * outs

                    def pair(t, i):
                        s = tmp[:, i % 2, :]
                        n = half * H_TILES + i + 1
                        core.part_lo(dve, t, b0 + 2 * i + SPLIT)
                        dve.wait_ge(sigmoid.sem, t * 2 + sigmoid.at(n))
                        v.tensor_tensor(like_psum(s, SEQ2), in_psum(core.buf(0), SEQ2), like_psum(s, SEQ2),
                                        ALU.mult).then_inc(core.free.sem, 1)
                        core.part_lo(dve, t, b0 + 2 * i + 1 + SPLIT)
                        dve.wait_ge(core.free.sem, t * UNROLL + core.free.at(f0 + BUFS + 2 * i + 1))
                        core.computed(dve, t, b0 + 2 * i + 1)
                        v.tensor_tensor(like_psum(s, SEQ2), in_psum(core.buf(1), SEQ2), like_psum(s, SEQ2),
                                        ALU.mult).then_inc(core.free.sem, 1)
                        dve.wait_ge(core.free.sem, t * UNROLL + core.free.at(f0 + BUFS + 2 * i + 2))
                        v.tensor_copy(hid_hi[:, t * 2 + i, :], s).then_inc(hi.sem, 1)
                        dve.wait_ge(hi.sem, t * 2 + hi.at(n))
                        v.tensor_tensor(hid_lo[:, t * 2 + i, :], s, hid_hi[:, t * 2 + i, :],
                                        ALU.subtract).then_inc(ready.sem, 1)

                    def out(t, i):
                        o, p = divmod(i, 2)
                        core.part_lo(dve, t, b0 + n_up + i + SPLIT)
                        if p:
                            core.computed(dve, t, b0 + n_up + i)
                            add_output(core, dve, core.x[:, t * 2 + o, :], core.buf(o), SEQ2, [(0, SEQ2, 0)],
                                       None).then_inc(core.free.sem, 1)

                    tiles(dve, H_TILES, 2, pair)
                    tiles(dve, n_down - UNROLL, UNROLL, out)
                    for i in range(UNROLL):
                        out((n_down - UNROLL) // UNROLL, i)
    core.close(FFN_BLOCKS, HALVES * outs)
    for c, n in ((sigmoid, H_TILES), (hi, H_TILES), (ready, H_TILES), (cleared, 1)):
        c.close(n * HALVES)
    sq.close(KT * HALVES)
    norm.close()


def fourier(core, arena, acts, mix, tokens, norm, mods):
    nc, dram = core.nc, core.dram
    tiles_of = [(0, LT, 0, LAT)] + ([(LT, TT, LAT, ALL)] if tokens == ALL else [])
    a = Alloc(arena, KT * ALL)
    u, spec = a(2, ALL), a(TT, 4 * P)
    cos = [a(LT, LAT), a(CT, CTX)]
    sin = [a(LT, LAT), a(CT, CTX)]
    mod_ring = a(MOD_RING, BLOCK) if mods else None
    norm.tmp = a(2, ALL)
    tables = core.counter("tables_in")
    evacuated = core.counter("fourier_evacuated")
    feature = core.counter("fourier_features")
    token = core.counter("fourier_tokens")
    nt = tokens // P
    with nc.Block(no_gpsimd_drain=True) as block:
        @block.sync
        def _(sp):
            core.feed(sp, FOURIER_BLOCKS)

        @block.gpsimd
        def _(pool):
            for name, dst in (("cos_lat", cos[0]), ("sin_lat", sin[0]), ("cos_ctx", cos[1]), ("sin_ctx", sin[1])):
                pool.dma_start(dst, dram[name]).then_inc(tables.sem, 16)
            if mods:
                core.mod_feed(pool, mod_ring, mods)

        @block.tensor
        def _(pe):
            norm.on_pe(pe)
            for j in range(FOURIER_BLOCKS):
                w = core.arrived(pe, 0, j)
                pe.wait_ge(core.free.sem, core.free.at(j + 1))
                product_parts(nc, core.buf(j), w, KT, acts, tokens,
                              before=norm.wait_tile(pe)).then_inc(core.done, 1)
            pe.wait_ge(core.free.sem, core.free.at(BUFS + FOURIER_BLOCKS))
            for t in range(nt):
                if t >= 2:
                    pe.wait_ge(evacuated.sem, evacuated.at(t - 1))
                for j in range(2):
                    last = nc.tensor.matmul(core.ps[:, 4 + t % 2, j * 2 * P:(j + 1) * 2 * P],
                                            u[:, j, t * P:(t + 1) * P], core.const[:, C_DFT:C_END],
                                            start=True, stop=True)
                last.then_inc(feature.sem, 1)
            pe.wait_ge(evacuated.sem, evacuated.at(nt))
            pe.wait_ge(tables.sem, tables.at(64))
            for j in range(2):
                for n, (t0, t1, c0, c1) in enumerate(tiles_of):
                    for t in range(t0, t1):
                        for part, table in enumerate((cos[n], sin[n])):
                            last = nc.tensor.matmul(core.buf(j)[:, c0:c1],
                                                    spec[:, t, (2 * j + part) * P:(2 * j + part + 1) * P],
                                                    table[:, t - t0, :], start=t == t0 and part == 0,
                                                    stop=t == t1 - 1 and part == 1)
                last.then_inc(token.sem, 1)
            if mods:
                tiles(pe, mods, MOD_RING,
                      lambda t, i: core.mod_product(pe, mod_ring, MOD_BLOCKS - mods, t, i, MOD_RING))

        @block.scalar
        def _(act):
            norm.on_act(act)
            for j in range(FOURIER_BLOCKS):
                core.part_hi(act, 0, j + SPLIT)
                core.computed(act, 0, j)
                nc.scalar.activation(u[:, j, 0:tokens], core.buf(j)[:, 0:tokens], ACT.Copy).then_inc(core.free.sem, 1)
            for j in range(2):
                act.wait_ge(token.sem, token.at(j + 1))
                nc.scalar.activation(mix[:, j, 0:tokens], core.buf(j)[:, 0:tokens], ACT.Copy)

        @block.vector
        def _(dve):
            norm.on_dve(dve, norm.tmp)
            for j in range(FOURIER_BLOCKS):
                core.part_lo(dve, 0, j + SPLIT)
            for t in range(nt):
                dve.wait_ge(feature.sem, feature.at(t + 1))
                nc.vector.tensor_copy(spec[:, t, :], core.ps[:, 4 + t % 2, :]).then_inc(evacuated.sem, 1)
            if mods:
                core.mod_finish(dve, 0, mods, MOD_FIRST, MOD_BLOCKS)
    core.close(FOURIER_BLOCKS, FOURIER_BLOCKS)
    core.mod_used += mods
    norm.close()
    tables.close(64)
    evacuated.close(nt)
    feature.close(nt)
    token.close(2)


def latent_attention(core, arena, acts, l, mix, ctx_queries):
    nc, dram = core.nc, core.dram
    a = Alloc(arena, KT * ALL)
    qt = a(A_HEADS, ALL)
    first, second = a(3, ALL), a(4, ALL)
    cq, ckv = first[:, 0:2, :], first[:, 2:3, :]
    work, rstd = second[:, 0:2, :], second[:, 2:4, :]
    kt, kr = a(A_HEADS, ALL), a(1, ALL)[:, 0, :]
    v = a(TT, A_HEADS * A_V)
    cos, sin = a(1, LAT)[:, 0, :], a(1, LAT)[:, 0, :]
    w_ukv = a(1, A_HEADS * (A_NOPE + A_V))[:, 0, :]
    y = first.rearrange("p a b -> p (a b)").rearrange("p (t n) -> p t n", t=TT)
    probs = second[:, 0:3, :]
    probs_t = a(2, ALL)
    w_uq = probs_t.rearrange("p a b -> p (a b)")[:, 0:BLOCK]
    top, total, inv = a(1, 32)[:, 0, :], a(1, 32)[:, 0, :], a(1, 32)[:, 0, :]
    scale = float(A_QK) ** -0.5
    rot = slice(A_NOPE, A_QK)
    gq, gkv = P_GQ + l * 2, P_GKV + l
    units = [(h, t, 0, TT) for t in range(LT) for h in range(A_HEADS)]
    if ctx_queries:
        units += [(h, t, LT, TT) for t in range(LT, TT) for h in range(A_HEADS)]
    qtiles = TT if ctx_queries else LT

    tables = core.counter("tables_in")
    steps = core.counter("latent_steps")
    squared = core.counter("latent_squared")
    summed = core.counter("latent_summed")
    root = core.counter("latent_root")
    lora_in = core.counter("lora_weights_in")
    normed = core.counter("latent_normed")
    qk_psum = core.counter("qk_products")
    qk_copied = core.counter("qk_copied")
    scored = core.counter("scores_ready")
    peak = core.counter("row_max_ready")
    expd = core.counter("probs_ready")
    turned = core.counter("probs_turned")
    turned_in = core.counter("turned_probs_copied")
    summed_v = core.counter("attention_ready")
    written = core.counter("attention_written")
    y_turned = core.counter("y_turned")
    y_copied = core.counter("y_copied")

    with nc.Block(no_gpsimd_drain=True) as block:
        @block.sync
        def _(sp):
            core.feed(sp, LATENT_BLOCKS)

        @block.gpsimd
        def _(pool):
            pool.dma_start(cos[rot, :], dram["rope_cos"]).then_inc(tables.sem, 16)
            pool.dma_start(sin[rot, :], dram["rope_sin"]).then_inc(tables.sem, 16)
            pool.dma_start(sin[A_QK:P, :], dram["rope_sin"]).then_inc(tables.sem, 16)
            pool.dma_start(w_uq, dram["w_uq"][l]).then_inc(lora_in.sem, 16)
            pool.dma_start(w_ukv, dram["w_ukv"][l]).then_inc(lora_in.sem, 16)

        @block.tensor
        def _(pe):
            for j in range(LATENT_BLOCKS):
                w = core.arrived(pe, 0, j)
                pe.wait_ge(core.free.sem, core.free.at(j + 1))
                product_parts(nc, core.buf(j), w, KT, acts, ALL).then_inc(core.done, 1)
            pe.wait_ge(core.free.sem, core.free.at(BUFS + 4))
            pe.wait_ge(squared.sem, squared.at(2))
            product(nc, core.buf(0), [core.ones[:]] * 2, [work[:, 0, :], work[:, 1, :]], ALL, P).then_inc(summed.sem, 1)
            pe.wait_ge(squared.sem, squared.at(3))
            product(nc, core.buf(1), [core.ones[:]], [work[:, 0, :]], ALL, P).then_inc(summed.sem, 1)
            pe.wait_ge(normed.sem, normed.at(2))
            pe.wait_ge(lora_in.sem, lora_in.at(32))
            wq, wkv = w_uq, w_ukv
            main = wq[:, 0:2 * A_HEADS * A_QK].rearrange("p (k n) -> p k n", k=2)
            swap = wq[:, 2 * A_HEADS * A_QK:BLOCK].rearrange("p (k n) -> p k n", k=2)
            for h in range(A_HEADS):
                if h:
                    pe.wait_ge(qk_copied.sem, qk_copied.at(h))
                product(nc, core.buf(0), [main[:, k, h * A_QK:(h + 1) * A_QK] for k in range(2)],
                        [cq[:, k, :] for k in range(2)], ALL, A_QK)
                last = product(nc, core.buf(1), [swap[:, k, h * A_ROPE:(h + 1) * A_ROPE] for k in range(2)],
                               [cq[:, k, :] for k in range(2)], LAT, A_ROPE, row=A_NOPE)
                last.then_inc(qk_psum.sem, 1)
            for h in range(A_HEADS):
                pe.wait_ge(qk_copied.sem, qk_copied.at(A_HEADS + h))
                product(nc, core.buf(h), [wkv[:, h * A_NOPE:(h + 1) * A_NOPE]], [ckv[:, 0, :]], ALL,
                        A_NOPE).then_inc(qk_psum.sem, 1)
            for t in range(TT):
                if t >= 4:
                    pe.wait_ge(qk_copied.sem, qk_copied.at(2 * A_HEADS + t - 3))
                last = nc.tensor.matmul(core.ps[:, 4 + t % 4, 0:A_HEADS * A_V], ckv[:, 0, t * P:(t + 1) * P],
                                        wkv[:, A_HEADS * A_NOPE:A_HEADS * (A_NOPE + A_V)], start=True, stop=True)
                last.then_inc(qk_psum.sem, 1)
            pe.wait_ge(qk_copied.sem, qk_copied.at(2 * A_HEADS + TT))
            pe.wait_ge(steps.sem, steps.at(3 + A_HEADS))

            def scores(u):
                h, t, s0, s1 = units[u]
                if u >= 2:
                    pe.wait_ge(expd.sem, expd.at(u - 1))
                out = core.buf(u)
                for c0 in range(s0 * P, s1 * P, 512):
                    c1 = min(c0 + 512, s1 * P)
                    last = nc.tensor.matmul(out[:, c0 - s0 * P:c1 - s0 * P], qt[0:A_QK, h, t * P:(t + 1) * P],
                                            kt[0:A_QK, h, c0:c1], start=True, stop=True)
                last.then_inc(scored.sem, 1)

            def turn(u):
                h, t, s0, s1 = units[u]
                pe.wait_ge(expd.sem, expd.at(u + 1))
                if u >= 1:
                    pe.wait_ge(turned_in.sem, turned_in.at(u))
                for s in range(s1 - s0):
                    last = nc.tensor.transpose(core.ps[:, 4 + s // 4, (s % 4) * P:(s % 4 + 1) * P],
                                               probs[:, u % 3, s * P:(s + 1) * P], core.ident(P))
                last.then_inc(turned.sem, 1)

            def weigh(u):
                h, t, s0, s1 = units[u]
                pe.wait_ge(turned_in.sem, turned_in.at(u + 1))
                if u >= 2:
                    pe.wait_ge(written.sem, written.at(u - 1))
                for s in range(s0, s1):
                    last = nc.tensor.matmul(core.ps[:, 6 + u % 2, 0:A_V],
                                            probs_t[:, u % 2, (s - s0) * P:(s - s0 + 1) * P],
                                            v[:, s, h * A_V:(h + 1) * A_V], start=s == s0, stop=s == s1 - 1)
                last.then_inc(summed_v.sem, 1)

            scores(0)
            for u in range(len(units)):
                if u + 1 < len(units):
                    scores(u + 1)
                if u:
                    weigh(u - 1)
                turn(u)
            weigh(len(units) - 1)
            pe.wait_ge(written.sem, written.at(len(units)))
            for t in range(qtiles):
                if t >= 2:
                    pe.wait_ge(y_copied.sem, y_copied.at(t - 1))
                for j in range(3):
                    last = nc.tensor.transpose(core.ps[:, t % 2, j * P:(j + 1) * P], y[:, t, j * P:(j + 1) * P],
                                               core.ident(P))
                last.then_inc(y_turned.sem, 1)

        @block.scalar
        def _(act):
            for j in range(3):
                core.part_hi(act, 0, j + SPLIT)
                core.computed(act, 0, j)
                nc.scalar.activation(first[:, j, :], core.buf(j)[:, 0:ALL], ACT.Copy).then_inc(core.free.sem, 1)
            core.part_hi(act, 0, 3 + SPLIT)
            core.computed(act, 0, 3)
            nc.scalar.activation(kr[A_NOPE:P, :], core.buf(3)[A_NOPE:P, 0:ALL], ACT.Copy).then_inc(core.free.sem, 1)
            act.wait_ge(core.free.sem, core.free.at(BUFS + 3))
            for j in range(2):
                nc.scalar.activation(work[:, j, :], cq[:, j, :], ACT.Square).then_inc(squared.sem, 1)
            act.wait_ge(summed.sem, summed.at(1))
            nc.scalar.activation(rstd[:, 0, :], core.buf(0)[:, 0:ALL], ACT.Sqrt, bias=core.eps[:, 0:1],
                                 scale=1.0 / Q_LORA).then_inc(root.sem, 1)
            nc.scalar.activation(work[:, 0, :], ckv[:, 0, :], ACT.Square).then_inc(squared.sem, 1)
            act.wait_ge(summed.sem, summed.at(2))
            nc.scalar.activation(rstd[:, 1, :], core.buf(1)[:, 0:ALL], ACT.Sqrt, bias=core.eps[:, 0:1],
                                 scale=1.0 / KV_LORA).then_inc(root.sem, 1)
            for h in range(A_HEADS):
                act.wait_ge(qk_psum.sem, qk_psum.at(A_HEADS + h + 1))
                nc.scalar.activation(kt[0:A_NOPE, h, :], core.buf(h)[0:A_NOPE, 0:ALL],
                                     ACT.Copy).then_inc(qk_copied.sem, 1)
            for t in range(TT):
                act.wait_ge(qk_psum.sem, qk_psum.at(2 * A_HEADS + t + 1))
                nc.scalar.activation(v[:, t, :], core.ps[:, 4 + t % 4, 0:A_HEADS * A_V],
                                     ACT.Copy).then_inc(qk_copied.sem, 1)
            for u, (h, t, s0, s1) in enumerate(units):
                act.wait_ge(peak.sem, peak.at(u + 1))
                if u >= 3:
                    act.wait_ge(turned.sem, turned.at(u - 2))
                nc.scalar.activation(probs[:, u % 3, 0:(s1 - s0) * P], core.buf(u)[:, 0:(s1 - s0) * P], ACT.Exp,
                                     bias=top[:, u:u + 1], accum_out=total[:, u:u + 1]).then_inc(expd.sem, 1)
            for t in range(qtiles):
                act.wait_ge(y_turned.sem, y_turned.at(t + 1))
                nc.scalar.activation(mix[:, 5:8, t * P:(t + 1) * P],
                                     core.ps[:, t % 2, 0:3 * P].rearrange("p (j n) -> p j n", j=3),
                                     ACT.Copy).then_inc(y_copied.sem, 1)

        @block.vector
        def _(dve):
            step = Steps(dve, steps)
            for j in range(LATENT_BLOCKS):
                core.part_lo(dve, 0, j + SPLIT)
            dve.wait_ge(tables.sem, tables.at(48))
            dve.wait_ge(core.free.sem, core.free.at(BUFS + 4))
            swapped = slice(A_QK, P)
            step(nc.vector.tensor_tensor(kt[rot, 0, 0:LAT], kr[rot, 0:LAT], cos[rot, :], ALU.mult))
            step(nc.vector.tensor_tensor(kt[rot, 1, 0:LAT], kr[swapped, 0:LAT], sin[swapped, :], ALU.mult))
            step(nc.vector.tensor_tensor(kr[rot, 0:LAT], kt[rot, 0, 0:LAT], kt[rot, 1, 0:LAT], ALU.add))
            for h in range(A_HEADS):
                step(nc.vector.tensor_copy(kt[rot, h, :], kr[rot, :]))
            dve.wait_ge(root.sem, root.at(1))
            step(nc.vector.reciprocal(rstd[:, 0, :], rstd[:, 0, :]))
            for j in range(2):
                last = nc.vector.scalar_tensor_tensor(cq[:, j, :], cq[:, j, :], core.param[:, gq + j:gq + j + 1],
                                                      rstd[:, 0, :], ALU.mult, ALU.mult)
                if j:
                    last.then_inc(normed.sem, 1)
                else:
                    step(last)
            dve.wait_ge(root.sem, root.at(2))
            step(nc.vector.reciprocal(rstd[:, 1, :], rstd[:, 1, :]))
            nc.vector.scalar_tensor_tensor(ckv[:, 0, :], ckv[:, 0, :], core.param[:, gkv:gkv + 1],
                                           rstd[:, 1, :], ALU.mult, ALU.mult).then_inc(normed.sem, 1)
            for h in range(A_HEADS):
                dve.wait_ge(qk_psum.sem, qk_psum.at(h + 1))
                step(nc.vector.tensor_scalar(qt[0:A_QK, h, :], core.buf(0)[0:A_QK, 0:ALL], scale, None, ALU.mult))
                step(nc.vector.scalar_tensor_tensor(work[rot, 0, 0:LAT], core.buf(1)[rot, 0:LAT], scale, sin[rot, :],
                                                    ALU.mult, ALU.mult))
                step(nc.vector.tensor_tensor(work[rot, 1, 0:LAT], qt[rot, h, 0:LAT], cos[rot, :], ALU.mult))
                nc.vector.tensor_tensor(qt[rot, h, 0:LAT], work[rot, 0, 0:LAT], work[rot, 1, 0:LAT],
                                        ALU.add).then_inc(qk_copied.sem, 1)

            def peak_of(u):
                h, t, s0, s1 = units[u]
                dve.wait_ge(scored.sem, scored.at(u + 1))
                nc.vector.tensor_reduce(top[:, u:u + 1], core.buf(u)[:, 0:(s1 - s0) * P], AX.X, ALU.max,
                                        negate=True).then_inc(peak.sem, 1)

            def finish(u):
                h, t, s0, s1 = units[u]
                dve.wait_ge(summed_v.sem, summed_v.at(u + 1))
                nc.vector.tensor_scalar(y[:, t, h * A_V:(h + 1) * A_V], core.ps[:, 6 + u % 2, 0:A_V],
                                        inv[:, u:u + 1], None, ALU.mult).then_inc(written.sem, 1)

            peak_of(0)
            for u in range(len(units)):
                h, t, s0, s1 = units[u]
                if u + 1 < len(units):
                    peak_of(u + 1)
                if u:
                    finish(u - 1)
                dve.wait_ge(expd.sem, expd.at(u + 1))
                step(nc.vector.reciprocal(inv[:, u:u + 1], total[:, u:u + 1]))
                dve.wait_ge(turned.sem, turned.at(u + 1))
                nc.vector.tensor_copy(probs_t[:, u % 2, 0:(s1 - s0) * P],
                                      core.ps[:, 4:6, :].rearrange("p b n -> p (b n)")[:, 0:(s1 - s0) * P]
                                      ).then_inc(turned_in.sem, 1)
            finish(len(units) - 1)
            steps.close(step.n)
    core.close(LATENT_BLOCKS, 4)
    n = len(units)
    for s, k in ((tables, 48), (lora_in, 32), (squared, 3), (summed, 2), (root, 2), (normed, 2), (qk_psum, 2 * A_HEADS + TT),
                 (qk_copied, 2 * A_HEADS + TT), (scored, n), (peak, n), (expd, n), (turned, n), (turned_in, n),
                 (summed_v, n), (written, n), (y_turned, qtiles), (y_copied, qtiles)):
        s.close(k)


class Mlstm:

    def __init__(self, arena):
        a = self.alloc = Alloc(arena, KT * ALL)
        self.q, self.k = a(M_HEADS, ALL), a(M_HEADS, ALL)
        self.k_tok, self.v = a(TT, M_HEADS * M_DIM), a(TT, M_HEADS, M_DIM + 1)
        self.out_gate = a(TT, M_HEADS * M_DIM)
        self.rows_i, self.rows_f = a(1, ALL)[:, 0, :], a(1, ALL)[:, 0, :]
        self.gain_row = a(1, M_HEADS * M_DIM)[:, 0, :]


def mlstm_inputs(core, arena, acts, l, m, acc):
    nc, dram = core.nc, core.dram
    a = Alloc(arena, m.alloc.at)
    width = LAT + 4 + CTX + 4
    conv_n = width - 4
    raw, sig = a(2, width), a(2, conv_n)
    flat = raw
    heads2 = 2 * M_HEADS
    mw = M_HEADS * M_DIM
    turns = 6
    copied = core.counter("conv_input_copied")
    taps = core.counter("conv_steps")
    gate = core.counter("conv_sigmoid")
    made = core.counter("conv_made")
    turned = core.counter("values_turned")
    turned_in = core.counter("values_copied")
    k_turned = core.counter("keys_turned")
    small = core.counter("mlstm_gain_in")
    ones_in = core.counter("mlstm_ones_in")
    rows_in = core.counter("gate_rows_in")
    bias = P_BG + l * 2
    cv = P_CONV + l * heads2 * CONV
    outs = MLSTM_BLOCKS
    out_t = core.ps[:, 4:6, :].rearrange("p b n -> p (b n)")
    with nc.Block(no_gpsimd_drain=True) as block:
        @block.sync
        def _(sp):
            core.feed(sp, MLSTM_BLOCKS)

        @block.gpsimd
        def _(pool):
            pool.dma_start(m.gain_row, dram["g_mlstm"][l]).then_inc(small.sem, 16)
            pool.memset(m.v[:, :, :, M_DIM:M_DIM + 1], 1.0).then_inc(ones_in.sem, 1)

        @block.tensor
        def _(pe):
            def turn(n):
                pe.wait_ge(core.free.sem, core.free.at(BUFS + heads2 + n + 1))
                if n:
                    pe.wait_ge(turned_in.sem, turned_in.at(n))
                for t in range(TT):
                    last = nc.tensor.transpose(out_t[:, t * P:(t + 1) * P], flat[:, n % 2, t * P:(t + 1) * P],
                                               core.ident(P))
                last.then_inc(turned.sem, 1)

            for j in range(MLSTM_BLOCKS):
                w = core.arrived(pe, 0, j)
                pe.wait_ge(core.free.sem, core.free.at(j + 1))
                product_parts(nc, core.buf(j), w, KT, acts, ALL, M_DIM if j < heads2 else P).then_inc(core.done, 1)
                if j > heads2:
                    turn(j - heads2 - 1)
            pe.wait_ge(turned_in.sem, turned_in.at(turns))
            pe.wait_ge(small.sem, small.at(16))
            pe.wait_ge(ones_in.sem, ones_in.at(1))
            for t in range(TT):
                if t >= 4:
                    pe.wait_ge(made.sem, made.at(heads2 + t - 3))
                for h in range(M_HEADS):
                    last = nc.tensor.transpose(core.ps[:, 4 + t % 4, h * M_DIM:(h + 1) * M_DIM],
                                               m.k[0:M_DIM, h, t * P:(t + 1) * P], core.ident(M_DIM))
                last.then_inc(k_turned.sem, 1)

        @block.scalar
        def _(act):
            for j in range(heads2):
                core.part_hi(act, 0, j + SPLIT)
                core.computed(act, 0, j)
                if j == 0:
                    act.wait_ge(taps.sem, taps.at(1))
                if j >= 2:
                    act.wait_ge(made.sem, made.at(j - 1))
                r = raw[0:M_DIM, j % 2, :]
                nc.scalar.activation(r[:, 2:2 + LAT], core.buf(j)[0:M_DIM, 0:LAT], ACT.Copy)
                nc.scalar.activation(r[:, LAT + 6:LAT + 6 + CTX], core.buf(j)[0:M_DIM, LAT:ALL],
                                     ACT.Copy).then_inc(core.free.sem, 1)
                if j >= 1:
                    act.wait_ge(copied.sem, copied.at(j))
                    nc.scalar.activation(sig[0:M_DIM, (j - 1) % 2, :], acc[0:M_DIM, (j - 1) % 2, :],
                                         ACT.Sigmoid).then_inc(gate.sem, 1)
            act.wait_ge(copied.sem, copied.at(heads2))
            nc.scalar.activation(sig[0:M_DIM, 1, :], acc[0:M_DIM, 1, :], ACT.Sigmoid).then_inc(gate.sem, 1)
            for n in range(turns):
                core.part_hi(act, 0, heads2 + n + SPLIT)
                core.computed(act, 0, heads2 + n)
                if n >= 2:
                    act.wait_ge(turned.sem, turned.at(n - 1))
                dst, src = flat[:, n % 2, 0:ALL], core.buf(heads2 + n)[:, 0:ALL]
                nc.scalar.activation(dst, src, ACT.Copy if n < 3 else ACT.Sigmoid).then_inc(core.free.sem, 1)
            core.part_hi(act, 0, MLSTM_BLOCKS - 1 + SPLIT)
            core.computed(act, 0, MLSTM_BLOCKS - 1)
            last = core.buf(outs - 1)
            nc.scalar.activation(m.rows_i[0:ROWS, :], last[0:ROWS, 0:ALL], ACT.Identity,
                                 bias=core.param[0:ROWS, bias:bias + 1]).then_inc(rows_in.sem, 1)
            nc.scalar.activation(m.rows_f[0:ROWS, :], last[F_ROW:F_ROW + ROWS, 0:ALL], ACT.Copy).then_inc(core.free.sem, 1)
            act.wait_ge(core.free.sem, core.free.at(BUFS + outs))
            nc.scalar.activation(m.rows_f[0:ROWS, :], m.rows_f[0:ROWS, :], ACT.Identity,
                                 bias=core.param[0:ROWS, bias + 1:bias + 2]).then_inc(rows_in.sem, 1)
            act.wait_ge(rows_in.sem, rows_in.at(2))

        @block.vector
        def _(dve):
            step = Steps(dve, taps)
            step(nc.vector.memset(raw, 0.0))

            def silu(j):
                dst = (m.q if j < M_HEADS else m.k)[0:M_DIM, j % M_HEADS, :]
                dve.wait_ge(gate.sem, gate.at(j + 1))
                for n, (t0, t1, c) in enumerate(((0, LAT, 0), (LAT, ALL, LAT + 4))):
                    s = slice(c, c + t1 - t0)
                    last = nc.vector.tensor_tensor(dst[:, t0:t1], acc[0:M_DIM, j % 2, s], sig[0:M_DIM, j % 2, s],
                                                   ALU.mult)
                last.then_inc(made.sem, 1)

            for j in range(heads2):
                core.part_lo(dve, 0, j + SPLIT)
                dve.wait_ge(core.free.sem, core.free.at(BUFS + j + 1))
                r, o = raw[0:M_DIM, j % 2, :], acc[0:M_DIM, j % 2, :]
                tap = lambda i: core.param[0:M_DIM, cv + j * CONV + i:cv + j * CONV + i + 1]
                if j >= 2:
                    dve.wait_ge(made.sem, made.at(j - 1))
                step(nc.vector.tensor_scalar(o, r[:, 0:conv_n], tap(0), None, ALU.mult))
                for i in range(1, CONV - 1):
                    step(nc.vector.scalar_tensor_tensor(o, r[:, i:i + conv_n], tap(i), o, ALU.mult, ALU.add))
                nc.vector.scalar_tensor_tensor(o, r[:, CONV - 1:CONV - 1 + conv_n], tap(CONV - 1), o, ALU.mult,
                                               ALU.add).then_inc(copied.sem, 1)
                if j >= 1:
                    silu(j - 1)
            core.part_lo(dve, 0, heads2 + SPLIT)
            silu(heads2 - 1)
            for n in range(turns):
                if n < turns:
                    core.part_lo(dve, 0, heads2 + n + 1 + SPLIT)
                dve.wait_ge(turned.sem, turned.at(n + 1))
                by_t = out_t[:, 0:ALL].rearrange("p (t n) -> p t n", t=TT)
                if n >= 3:
                    c = (n - 3) * P
                    nc.vector.tensor_copy(m.out_gate[:, :, c:c + P], by_t).then_inc(turned_in.sem, 1)
                    continue
                f = n * P
                while f < (n + 1) * P:
                    h, d = divmod(f, M_DIM)
                    e = min((h + 1) * M_DIM, (n + 1) * P)
                    last = nc.vector.tensor_copy(m.v[:, :, h, d:d + e - f], by_t[:, :, f - n * P:e - n * P])
                    f = e
                last.then_inc(turned_in.sem, 1)
            for t in range(TT):
                dve.wait_ge(k_turned.sem, k_turned.at(t + 1))
                nc.vector.tensor_copy(m.k_tok[:, t, :], core.ps[:, 4 + t % 4, 0:mw]).then_inc(made.sem, 1)
            taps.close(step.n)
    core.close(MLSTM_BLOCKS, outs)
    small.close(16)
    ones_in.close(1)
    rows_in.close(2)
    copied.close(heads2)
    gate.close(heads2)
    made.close(heads2 + TT)
    turned.close(turns)
    turned_in.close(turns)
    k_turned.close(TT)


def mlstm(core, arena, scratch, m, mix, ctx_out):
    nc, dram = core.nc, core.dram
    a = Alloc(arena, m.alloc.at)
    hflat = scratch
    hid = M_HEADS * M_DIM
    out = hflat[:, 0:TT * hid].rearrange("p (t n) -> p t n", t=TT)
    select = hflat[:, 2304:2304 + 8 * P].rearrange("p (r n) -> p r n", r=8)
    per_token = hflat[:, 3328:3328 + 24 * ROWS].rearrange("p (n r) -> p n r", r=ROWS)
    decay = hflat[:, 4192:4192 + ROWS * TT].rearrange("p (r t) -> p r t", t=TT)
    decay_rows = hflat[0:ROWS, 4408:4408 + ROWS * TT].rearrange("p (r t) -> p r t", t=TT)
    a = Alloc(scratch, 4700)
    b, peak, w_state, floor_, w_key, tmp = (a(1, ALL)[0:ROWS, 0, :] for _ in range(6))
    state_m, last_m, dec = (a(1, TT)[0:ROWS, 0, :] for _ in range(3))
    weight, score = a(2, M_HEADS * P), a(2, M_HEADS * P)
    a = Alloc(arena, m.alloc.at)
    keyed = a(2, hid)
    part, both = a(1, M_HEADS * (M_DIM + 1)), a(2, M_HEADS * (M_DIM + 1))
    state = a(2, M_HEADS * (M_DIM + 1))
    den, ms = a(2, M_HEADS), a(1, TT * M_HEADS)[:, 0, :]
    sq = m.k.rearrange("p h n -> p (h n)")[:, 0:TT * hid]
    lf, ai = m.rows_f[0:ROWS, :], m.rows_i[0:ROWS, :]
    tile = lambda ap, t: ap[:, t * P:(t + 1) * P]
    by_t = lambda ap: ap.rearrange("p (t n) -> p t n", t=TT)
    order = (tuple(range(LT, TT)) + tuple(range(LT)), tuple(reversed(range(TT))))
    row0 = (FWD, BWD)
    scale = float(M_DIM) ** -0.5
    nt = TT if ctx_out else LT

    steps_all = [(d, i, order[d][i]) for i in range(TT) for d in range(2)]
    outs = [u for u, (d, i, t) in enumerate(steps_all) if t < nt]
    upds = [u for u, (d, i, t) in enumerate(steps_all) if i < TT - 1]
    n_out = lambda u: sum(v < u for v in outs)
    n_upd = lambda u: sum(v < u for v in upds)

    chain = core.counter("gate_steps")
    exponents = core.counter("gate_exponents")
    mean_sq = core.counter("mean_squares")
    act_chain = core.counter("gate_act_steps")
    rows_ready = core.counter("gate_rows_ready")
    turned = core.counter("gate_rows_turned")
    select_in = core.counter("select_in")
    weights_p = core.counter("weight_exponents")
    scores_p = core.counter("mlstm_scores")
    w_exp = core.counter("weights_ready")
    scored = core.counter("weighted_scores")
    summed = core.counter("mlstm_sums")
    keys = core.counter("weighted_keys")
    grown = core.counter("state_products")
    passed = core.counter("state_ready")
    written = core.counter("mlstm_written")
    token_rows = core.counter("token_rows_copied")
    y_turned = core.counter("y_turned")

    with nc.Block(no_gpsimd_drain=True) as block:
        @block.gpsimd
        def _(pool):
            pool.dma_start(select[0:ROWS, :, :], dram["select"]).then_inc(select_in.sem, 16)
            pool.wait_ge(token_rows.sem, token_rows.at(2))
            for u in upds:
                d, i, t = steps_all[u]
                n = n_upd(u)
                if n >= 2:
                    pool.wait_ge(grown.sem, grown.at(n - 1))
                wk = per_token[:, 3 * TT + t, row0[d]:row0[d] + M_HEADS]
                nc.gpsimd.tensor_tensor(keyed[:, n % 2, :].rearrange("p (h d) -> p h d", h=M_HEADS),
                                        m.k_tok[:, t, :].rearrange("p (h d) -> p h d", h=M_HEADS),
                                        wk[:, :, None].to_broadcast([P, M_HEADS, M_DIM]),
                                        ALU.mult).then_inc(keys.sem, 1)

        @block.tensor
        def _(pe):
            pe.wait_ge(rows_ready.sem, rows_ready.at(1))
            for q, rows in enumerate((ai, w_state, floor_, w_key)):
                for t in range(TT):
                    n = q * TT + t
                    last = nc.tensor.transpose(core.ps[:, 4 + n // 12, n % 12 * ROWS:(n % 12 + 1) * ROWS],
                                               tile(rows, t), core.ident(ROWS))
            last = nc.tensor.matmul(core.ps[:, 6, 0:ROWS * TT], core.ones[0:ROWS, :],
                                    decay_rows.rearrange("p r t -> p (r t)"), start=True, stop=True)
            last.then_inc(turned.sem, 1)
            pe.wait_ge(select_in.sem, select_in.at(16))

            def weigh(u):
                d, i, t = steps_all[u]
                n = n_out(u)
                if n >= 2:
                    pe.wait_ge(w_exp.sem, w_exp.at(n - 1))
                mask = core.const[:, C_UPPER:C_UPPER + P] if d == 0 else core.const[:, C_LOWER:C_LOWER + P]
                nc.tensor.matmul(core.ps[:, n % 2, :], core.ident(P), mask[:, None, :].to_broadcast([P, M_HEADS, P]),
                                 start=True, stop=False)
                for h in range(M_HEADS):
                    last = nc.tensor.matmul(core.ps[:, n % 2, h * P:(h + 1) * P], select[0:ROWS, d * M_HEADS + h, :],
                                            tile(tmp, t), start=False, stop=h == M_HEADS - 1)
                last.then_inc(weights_p.sem, 1)
                if n >= 2:
                    pe.wait_ge(scored.sem, scored.at(n - 1))
                for h in range(M_HEADS):
                    last = nc.tensor.matmul(core.ps[:, 2 + n % 2, h * P:(h + 1) * P], tile(m.k[0:M_DIM, h, :], t),
                                            tile(m.q[0:M_DIM, h, :], t), start=True, stop=True)
                last.then_inc(scores_p.sem, 1)

            def sums(u):
                d, i, t = steps_all[u]
                n = n_out(u)
                pe.wait_ge(scored.sem, scored.at(n + 1))
                if n >= 1:
                    pe.wait_ge(written.sem, written.at(n))
                for h in range(M_HEADS):
                    c = slice(h * (M_DIM + 1), (h + 1) * (M_DIM + 1))
                    last = nc.tensor.matmul(core.ps[:, 4 + n % 2, c], score[:, n % 2, h * P:(h + 1) * P],
                                            m.v[:, t, h, :], start=True, stop=True)
                if i:
                    pe.wait_ge(passed.sem, passed.at(n_upd(2 * (i - 1) + d) + 1))
                    for h in range(M_HEADS):
                        c = slice(h * (M_DIM + 1), (h + 1) * (M_DIM + 1))
                        last = nc.tensor.matmul(core.ps[:, 6, c], tile(m.q[0:M_DIM, h, :], t), state[0:M_DIM, d, c],
                                                start=True, stop=True)
                last.then_inc(summed.sem, 1)

            def grow(u):
                d, i, t = steps_all[u]
                n = n_upd(u)
                pe.wait_ge(keys.sem, keys.at(n + 1))
                if n >= 1:
                    pe.wait_ge(passed.sem, passed.at(n))
                for h in range(M_HEADS):
                    last = nc.tensor.matmul(core.ps[0:M_DIM, 7, h * (M_DIM + 1):(h + 1) * (M_DIM + 1)],
                                            keyed[:, n % 2, h * M_DIM:(h + 1) * M_DIM], m.v[:, t, h, :],
                                            start=True, stop=True)
                last.then_inc(grown.sem, 1)

            pe.wait_ge(token_rows.sem, token_rows.at(3))
            weigh(outs[0])
            for u in range(len(steps_all)):
                n = n_out(u)
                if u in outs and n + 1 < len(outs):
                    weigh(outs[n + 1])
                if u in outs:
                    sums(u)
                if u in upds:
                    grow(u)
            pe.wait_ge(written.sem, written.at(len(outs) + 1))
            for t in range(nt):
                for j in range(3):
                    last = nc.tensor.transpose(core.ps[:, t, j * P:(j + 1) * P], out[:, t, j * P:(j + 1) * P],
                                               core.ident(P))
                last.then_inc(y_turned.sem, 1)

        @block.scalar
        def _(act):
            step = Steps(act, act_chain)
            step(nc.scalar.activation(tmp, lf, ACT.Abs))
            step(nc.scalar.activation(tmp, tmp, ACT.Exp, scale=-1.0))
            step(nc.scalar.activation(tmp, tmp, ACT.Ln, bias=core.ones[0:ROWS, 0:1]))
            act.wait_ge(exponents.sem, exponents.at(1))
            for ap, s in ((dec, 1.0), (w_state, 1.0), (floor_, -1.0), (w_key, 1.0)):
                step(nc.scalar.activation(ap, ap, ACT.Exp, scale=s))
            for u in outs:
                d, i, t = steps_all[u]
                n = n_out(u)
                if n == 0:
                    act.wait_ge(token_rows.sem, token_rows.at(2))
                act.wait_ge(weights_p.sem, weights_p.at(n + 1))
                if n >= 2:
                    act.wait_ge(scored.sem, scored.at(n - 1))
                for h in range(M_HEADS):
                    last = nc.scalar.activation(weight[:, n % 2, h * P:(h + 1) * P],
                                                core.ps[:, n % 2, h * P:(h + 1) * P], ACT.Exp,
                                                bias=per_token[:, t, row0[d] + h:row0[d] + h + 1])
                last.then_inc(w_exp.sem, 1)
            act.wait_ge(mean_sq.sem, mean_sq.at(1))
            step(nc.scalar.activation(ms[:, 0:nt * M_HEADS], ms[:, 0:nt * M_HEADS], ACT.Sqrt, bias=core.eps[:, 0:1],
                                      scale=1.0 / M_DIM))
            for t in range(nt):
                act.wait_ge(y_turned.sem, y_turned.at(t + 1))
                nc.scalar.activation(mix[:, 2:5, t * P:(t + 1) * P],
                                     core.ps[:, t, 0:3 * P].rearrange("p (j n) -> p j n", j=3), ACT.Copy)

        @block.vector
        def _(dve):
            step = Steps(dve, chain)
            v = nc.vector
            step(v.memset(b, 0.0))
            step(v.memset(peak, 0.0))
            step(v.memset(state_m, 0.0))
            step(v.memset(last_m, 0.0))
            dve.wait_ge(act_chain.sem, act_chain.at(3))
            step(v.scalar_tensor_tensor(lf, lf, 0.0, tmp, ALU.min, ALU.subtract))

            def run(d, dst, src, t, initial, op):
                r = slice(row0[d], row0[d] + M_HEADS)
                o, s = tile(dst[r, :], t), tile(src[r, :], t)
                if d:
                    o, s = o[:, ::-1], s[:, ::-1]
                return v.tensor_tensor_scan(o, s, s, initial, op, op if op == ALU.max else ALU.bypass)

            for t in range(TT):
                for d in range(2):
                    last = run(d, b, lf, t, 0.0, ALU.add)
            step(last)
            step(v.tensor_tensor(ai, ai, b, ALU.subtract))
            for i in range(TT):
                for d in range(2):
                    r = slice(row0[d], row0[d] + M_HEADS)
                    last = run(d, peak, ai, order[d][i], state_m[r, order[d][i]:order[d][i] + 1], ALU.max)
                step(last)
                for d in range(2):
                    t = order[d][i]
                    r = slice(row0[d], row0[d] + M_HEADS)
                    c = t * P + (P - 1 if d == 0 else 0)
                    last = v.tensor_copy(last_m[r, t:t + 1], peak[r, c:c + 1])
                    if i < TT - 1:
                        n = order[d][i + 1]
                        last = v.tensor_tensor(state_m[r, n:n + 1], b[r, c:c + 1], peak[r, c:c + 1], ALU.add)
                step(last)
            bc = lambda ap: ap[:, :, None].to_broadcast([ROWS, TT, P])
            v.tensor_tensor(dec, state_m, last_m, ALU.subtract)
            v.tensor_tensor(by_t(w_state), bc(state_m), by_t(peak), ALU.subtract)
            v.tensor_tensor(floor_, b, peak, ALU.add)
            v.tensor_tensor(by_t(w_key), by_t(ai), bc(last_m), ALU.subtract)
            v.tensor_scalar(tmp, peak, -1.0, None, ALU.mult).then_inc(exponents.sem, 1)
            dve.wait_ge(act_chain.sem, act_chain.at(7))
            step(v.tensor_scalar(w_state, w_state, scale, None, ALU.mult))
            v.tensor_tensor(decay_rows, core.const[0:ROWS, C_IDENT:C_IDENT + ROWS][:, :, None].to_broadcast(
                [ROWS, ROWS, TT]), dec[:, None, :].to_broadcast([ROWS, ROWS, TT]), ALU.mult).then_inc(rows_ready.sem, 1)
            dve.wait_ge(turned.sem, turned.at(1))
            for n in range(2):
                v.tensor_copy(per_token[:, 12 * n:12 * (n + 1), :].rearrange("p n r -> p (n r)"),
                              core.ps[:, 4 + n, 0:12 * ROWS]).then_inc(token_rows.sem, 1)
            v.tensor_copy(decay.rearrange("p r t -> p (r t)"), core.ps[:, 6, 0:ROWS * TT]).then_inc(token_rows.sem, 1)
            dve.wait_ge(token_rows.sem, token_rows.at(3))
            heads = lambda ap: ap.rearrange("p (h d) -> p h d", h=M_HEADS)

            def scored_step(u):
                n = n_out(u)
                dve.wait_ge(w_exp.sem, w_exp.at(n + 1))
                dve.wait_ge(scores_p.sem, scores_p.at(n + 1))
                if n >= 2:
                    dve.wait_ge(summed.sem, summed.at(n - 1))
                v.scalar_tensor_tensor(score[:, n % 2, :], core.ps[:, 2 + n % 2, :], scale, weight[:, n % 2, :],
                                       ALU.mult, ALU.mult).then_inc(scored.sem, 1)

            def combine(u):
                d, i, t = steps_all[u]
                n = n_out(u)
                r = slice(row0[d], row0[d] + M_HEADS)
                nd, pt, dn = both[:, n % 2, :], part[:, 0, :], den[:, n % 2, :]
                w1 = M_HEADS * (M_DIM + 1)
                dve.wait_ge(summed.sem, summed.at(n + 1))
                if i:
                    step(v.tensor_tensor(heads(pt), heads(core.ps[:, 6, 0:w1]), per_token[:, TT + t, r][:, :, None]
                                         .to_broadcast([P, M_HEADS, M_DIM + 1]), ALU.mult))
                    step(v.tensor_tensor(nd, core.ps[:, 4 + n % 2, 0:w1], pt, ALU.add))
                else:
                    step(v.tensor_copy(nd, core.ps[:, 4 + n % 2, 0:w1]))
                q = heads(nd)[:, :, M_DIM]
                step(v.scalar_tensor_tensor(dn, q, -1.0, q, ALU.mult, ALU.max))
                step(v.tensor_tensor(dn, dn, per_token[:, 2 * TT + t, r], ALU.max))
                step(v.reciprocal(dn, dn))
                rb = dn[:, :, None].to_broadcast([P, M_HEADS, M_DIM])
                o = heads(out[:, t, :])
                if t not in seen:
                    seen.add(t)
                    v.tensor_tensor(o, heads(nd)[:, :, 0:M_DIM], rb, ALU.mult).then_inc(written.sem, 1)
                else:
                    step(v.tensor_tensor(heads(nd)[:, :, 0:M_DIM], heads(nd)[:, :, 0:M_DIM], rb, ALU.mult))
                    v.tensor_tensor(o, o, heads(nd)[:, :, 0:M_DIM], ALU.add).then_inc(written.sem, 1)

            def pass_on(u):
                d, i, t = steps_all[u]
                n = n_upd(u)
                st, w1 = state[0:M_DIM, d, :], M_HEADS * (M_DIM + 1)
                dve.wait_ge(grown.sem, grown.at(n + 1))
                if i == 0:
                    v.tensor_copy(st, core.ps[0:M_DIM, 7, 0:w1]).then_inc(passed.sem, 1)
                else:
                    dc = decay[0:M_DIM, row0[d]:row0[d] + M_HEADS, t]
                    dve.wait_ge(passed.sem, passed.at(n))
                    step(v.tensor_tensor(heads(st), heads(st), dc[:, :, None].to_broadcast(
                        [M_DIM, M_HEADS, M_DIM + 1]), ALU.mult))
                    v.tensor_tensor(st, st, core.ps[0:M_DIM, 7, 0:w1], ALU.add).then_inc(passed.sem, 1)

            seen = set()
            scored_step(outs[0])
            for u in range(len(steps_all)):
                n = n_out(u)
                if u in outs and n + 1 < len(outs):
                    scored_step(outs[n + 1])
                if u in outs:
                    combine(u)
                if u in upds:
                    pass_on(u)
            dve.wait_ge(written.sem, written.at(len(outs)))
            o3 = out[:, 0:nt, :].rearrange("p t (h d) -> p (t h) d", h=M_HEADS)
            s3 = sq[:, 0:nt * hid]
            step(v.tensor_tensor(s3.rearrange("p (t n) -> p t n", t=nt), out[:, 0:nt, :], out[:, 0:nt, :], ALU.mult))
            v.tensor_reduce(ms[:, 0:nt * M_HEADS], s3.rearrange("p (g d) -> p g d", d=M_DIM), AX.X,
                            ALU.add).then_inc(mean_sq.sem, 1)
            dve.wait_ge(act_chain.sem, act_chain.at(8))
            step(v.reciprocal(ms[:, 0:nt * M_HEADS], ms[:, 0:nt * M_HEADS]))
            step(v.tensor_tensor(o3, o3, ms[:, 0:nt * M_HEADS][:, :, None].to_broadcast([P, nt * M_HEADS, M_DIM]),
                                 ALU.mult))
            step(v.tensor_tensor(out[:, 0:nt, :], out[:, 0:nt, :], m.gain_row[:, None, :].to_broadcast([P, nt, hid]),
                                 ALU.mult))
            v.tensor_tensor(out[:, 0:nt, :], out[:, 0:nt, :], m.out_gate[:, 0:nt, :], ALU.mult).then_inc(written.sem, 1)
            chain.close(step.n)
    act_chain.close(8)
    no, nu = len(outs), len(upds)
    for s, k in ((exponents, 1), (mean_sq, 1), (rows_ready, 1), (turned, 1), (select_in, 16), (weights_p, no),
                 (scores_p, no), (w_exp, no), (scored, no), (summed, no), (keys, nu), (grown, nu), (passed, nu),
                 (written, no + 1), (token_rows, 3), (y_turned, nt)):
        s.close(k)


TOKEN_TILES = [(t * P, P) for t in range(LT)] + [(LAT, META)]


def turn_tokens(core, src, out):
    for t, (c, n) in enumerate(TOKEN_TILES):
        last = core.nc.tensor.transpose(out[0:n, t * P:(t + 1) * P], src[:, c:c + n], core.ident(P))
    return last


def token_major_copies(eng_op, out, dst):
    eng_op(dst[:, 0:LT, :], out[:, 0:LT * P].rearrange("p (t n) -> p t n", t=LT))
    return eng_op(dst[0:META, LT, :], out[0:META, LT * P:(LT + 1) * P])


def forgetting_attention(core, arena, acts, norm, l, y):
    nc = core.nc
    a = Alloc(arena, (LT + 1) * D)
    norm.tmp = a(2, SEQ2)
    flat = a(2, SEQ2)
    q, k, v = a(FOX_HEADS, SEQ2), a(FOX_HEADS, SEQ2), a(LT + 1, FOX_HEADS * FOX_DIM)
    lf, c_row, tmp = (a(1, SEQ2)[0:FOX_HEADS, 0, :] for _ in range(3))
    probs, probs_t = a(3, SEQ2), a(2, 5 * P)
    n_units = FOX_HEADS * (LT + 1)
    top, total, inv = (a(1, n_units)[:, 0, :] for _ in range(3))
    units = [(h, t) for t in range(LT + 1) for h in range(FOX_HEADS)]
    rows = lambda u: TOKEN_TILES[units[u][1]][1]
    real = lambda u: (units[u][1] + 1) * P if units[u][1] < LT else 0

    chain = core.counter("fox_steps")
    act_chain = core.counter("fox_act_steps")
    c_in = core.counter("c_in_keys")
    ones_in = core.counter("fox_ones_in")
    scored = core.counter("scores_ready")
    peak = core.counter("row_max_ready")
    expd = core.counter("probs_ready")
    turned = core.counter("probs_turned")
    turned_in = core.counter("turned_probs_copied")
    summed_v = core.counter("attention_ready")
    written = core.counter("attention_written")
    summed_c = core.counter("c_ready")
    v_turned = core.counter("values_turned")
    v_copied = core.counter("values_copied")
    out_t = core.ps[:, 4:6, :].rearrange("p b n -> p (b n)")

    with nc.Block(no_gpsimd_drain=True) as block:
        @block.sync
        def _(sp):
            core.feed(sp, FOX_BLOCKS)
            sp.wait_ge(summed_c.sem, summed_c.at(1))
            for h in range(FOX_HEADS):
                sp.dma_start(k[FOX_DIM:FOX_DIM + 1, h, :], c_row[h:h + 1, :]).then_inc(c_in.sem, 16)

        @block.gpsimd
        def _(pool):
            pool.wait_ge(core.added.sem, core.added.at(0))
            pool.memset(q[FOX_DIM:FOX_DIM + 1, :, :], 1.0).then_inc(ones_in.sem, 1)

        @block.tensor
        def _(pe):
            norm.on_pe(pe)

            def turn_values(n):
                pe.wait_ge(core.free.sem, core.free.at(BUFS + FOX_HEADS + 2 + n))
                if n:
                    pe.wait_ge(v_copied.sem, v_copied.at(n))
                turn_tokens(core, flat[:, n % 2, :], out_t).then_inc(v_turned.sem, 1)

            for j in range(FOX_BLOCKS):
                w = core.arrived(pe, 0, j)
                pe.wait_ge(core.free.sem, core.free.at(j + 1))
                product_parts(nc, core.buf(j), w, KT, acts, SEQ2,
                              before=norm.wait_tile(pe)).then_inc(core.done, 1)
                if j > FOX_HEADS + 1:
                    turn_values(j - FOX_HEADS - 2)
            turn_values(3)
            pe.wait_ge(v_copied.sem, v_copied.at(4))
            pe.wait_ge(core.free.sem, core.free.at(BUFS + FOX_BLOCKS))
            pe.wait_ge(c_in.sem, c_in.at(16 * FOX_HEADS))
            pe.wait_ge(ones_in.sem, ones_in.at(1))

            def scores(u):
                h, t = units[u]
                c, n = TOKEN_TILES[t]
                if u >= 2:
                    pe.wait_ge(expd.sem, expd.at(u - 1))
                out, r = core.buf(u), real(u)
                qs = q[0:FOX_DIM + 1, h, c:c + n]
                mask = core.const[:, C_LOWER:C_LOWER + P]
                if r:
                    nc.tensor.matmul(out[:, 0:r], qs, k[0:FOX_DIM + 1, h, 0:r], start=True, stop=False)
                    nc.tensor.matmul(out[:, r - P:r], core.ident(P), mask, start=False, stop=True)
                last = nc.tensor.matmul(out[0:n, r:r + META], qs, k[0:FOX_DIM + 1, h, LAT:SEQ2], start=True,
                                        stop=r > 0)
                if not r:
                    last = nc.tensor.matmul(out[0:n, 0:META], core.ident(META), mask[0:META, 0:META], start=False,
                                            stop=True)
                last.then_inc(scored.sem, 1)

            def turn(u):
                n, r = rows(u), real(u)
                pe.wait_ge(expd.sem, expd.at(u + 1))
                if u >= 1:
                    pe.wait_ge(turned_in.sem, turned_in.at(u))
                for s in range(r // P):
                    nc.tensor.transpose(core.ps[:, 4, s * P:(s + 1) * P], probs[:, u % 3, s * P:(s + 1) * P],
                                        core.ident(P))
                nc.tensor.transpose(core.ps[0:META, 5, 0:n], probs[0:n, u % 3, r:r + META],
                                    core.ident(n)).then_inc(turned.sem, 1)

            def weigh(u):
                h, t = units[u]
                n, r = rows(u), real(u)
                pe.wait_ge(turned_in.sem, turned_in.at(u + 1))
                if u >= 2:
                    pe.wait_ge(written.sem, written.at(u - 1))
                out = core.ps[0:n, 6 + u % 2, 0:FOX_DIM]
                hc = slice(h * FOX_DIM, (h + 1) * FOX_DIM)
                for s in range(r // P):
                    nc.tensor.matmul(out, probs_t[:, u % 2, s * P:(s + 1) * P], v[:, s, hc], start=s == 0, stop=False)
                nc.tensor.matmul(out, probs_t[0:META, u % 2, LAT:LAT + n], v[0:META, LT, hc], start=r == 0,
                                 stop=True).then_inc(summed_v.sem, 1)

            scores(0)
            for u in range(n_units):
                if u + 1 < n_units:
                    scores(u + 1)
                if u:
                    weigh(u - 1)
                turn(u)
            weigh(n_units - 1)

        @block.scalar
        def _(act):
            norm.on_act(act)
            step = Steps(act, act_chain)
            core.part_hi(act, 0, SPLIT)
            core.computed(act, 0, 0)
            bias = core.param[0:FOX_HEADS, P_BF + l:P_BF + l + 1]
            g = core.buf(0)[0:FOX_HEADS, :]
            step(nc.scalar.activation(like_psum(lf, SEQ2), in_psum(g, SEQ2), ACT.Identity, bias=bias))
            nc.scalar.activation(like_psum(tmp, SEQ2), in_psum(g, SEQ2), ACT.Abs, bias=bias).then_inc(core.free.sem, 1)
            act.wait_ge(core.free.sem, core.free.at(BUFS + 1))
            step(nc.scalar.activation(tmp, tmp, ACT.Exp, scale=-1.0))
            step(nc.scalar.activation(tmp, tmp, ACT.Ln, bias=core.ones[0:FOX_HEADS, 0:1]))
            for j in range(1, FOX_HEADS + 1):
                core.part_hi(act, 0, j + SPLIT)
                core.computed(act, 0, j)
                dst, h = (q, 2 * (j - 1)) if j <= FOX_HEADS // 2 else (k, 2 * (j - 1) - FOX_HEADS)
                s = float(FOX_DIM) ** -0.5 if j <= FOX_HEADS // 2 else 1.0
                for e in range(2):
                    last = nc.scalar.activation(like_psum(dst[0:FOX_DIM, h + e, :], SEQ2),
                                                in_psum(core.buf(j)[e * FOX_DIM:(e + 1) * FOX_DIM, :], SEQ2), ACT.Copy,
                                                scale=s)
                last.then_inc(core.free.sem, 1)
            for j in range(4):
                core.part_hi(act, 0, FOX_HEADS + 1 + j + SPLIT)
                core.computed(act, 0, FOX_HEADS + 1 + j)
                if j >= 2:
                    act.wait_ge(v_turned.sem, v_turned.at(j - 1))
                nc.scalar.activation(like_psum(flat[:, j % 2, :], SEQ2), in_psum(core.buf(FOX_HEADS + 1 + j), SEQ2),
                                     ACT.Copy).then_inc(core.free.sem, 1)
            for u, (h, t) in enumerate(units):
                n, w = rows(u), real(u) + META
                act.wait_ge(peak.sem, peak.at(u + 1))
                if u >= 3:
                    act.wait_ge(turned.sem, turned.at(u - 2))
                nc.scalar.activation(probs[0:n, u % 3, 0:w], core.buf(u)[0:n, 0:w], ACT.Exp, bias=top[0:n, u:u + 1],
                                     accum_out=total[0:n, u:u + 1]).then_inc(expd.sem, 1)

        @block.vector
        def _(dve):
            norm.on_dve(dve, norm.tmp)
            core.part_lo(dve, 0, SPLIT)
            core.part_lo(dve, 0, SPLIT + 1)
            step = Steps(dve, chain)
            dve.wait_ge(act_chain.sem, act_chain.at(3))
            step(nc.vector.scalar_tensor_tensor(lf, lf, 0.0, tmp, ALU.min, ALU.subtract))
            meta, reals = slice(LAT, SEQ2), slice(0, LAT)
            step(nc.vector.tensor_tensor_scan(tmp[:, meta], lf[:, meta], lf[:, meta], 0.0, ALU.add, ALU.bypass))
            step(nc.vector.tensor_tensor_scan(tmp[:, reals], lf[:, reals], lf[:, reals], tmp[:, SEQ2 - 1:SEQ2], ALU.add,
                                              ALU.bypass))
            nc.vector.tensor_scalar(c_row, tmp, -1.0, None, ALU.mult).then_inc(summed_c.sem, 1)
            for j in range(2, FOX_BLOCKS):
                core.part_lo(dve, 0, j + SPLIT)
                if j > FOX_HEADS + 1:
                    n = j - FOX_HEADS - 2
                    dve.wait_ge(v_turned.sem, v_turned.at(n + 1))
                    token_major_copies(nc.vector.tensor_copy, out_t,
                                       v[:, :, n * P:(n + 1) * P]).then_inc(v_copied.sem, 1)
            dve.wait_ge(v_turned.sem, v_turned.at(4))
            token_major_copies(nc.vector.tensor_copy, out_t, v[:, :, 3 * P:4 * P]).then_inc(v_copied.sem, 1)

            def peak_of(u):
                n, w = rows(u), real(u) + META
                dve.wait_ge(scored.sem, scored.at(u + 1))
                nc.vector.tensor_reduce(top[0:n, u:u + 1], core.buf(u)[0:n, 0:w], AX.X, ALU.max,
                                        negate=True).then_inc(peak.sem, 1)

            def finish(u):
                h, t = units[u]
                n = rows(u)
                dve.wait_ge(summed_v.sem, summed_v.at(u + 1))
                nc.vector.tensor_scalar(y[0:n, t, h * FOX_DIM:(h + 1) * FOX_DIM], core.ps[0:n, 6 + u % 2, 0:FOX_DIM],
                                        inv[0:n, u:u + 1], None, ALU.mult).then_inc(written.sem, 1)

            peak_of(0)
            for u in range(n_units):
                n, r = rows(u), real(u)
                if u + 1 < n_units:
                    peak_of(u + 1)
                if u:
                    finish(u - 1)
                dve.wait_ge(expd.sem, expd.at(u + 1))
                step(nc.vector.reciprocal(inv[0:n, u:u + 1], total[0:n, u:u + 1]))
                dve.wait_ge(turned.sem, turned.at(u + 1))
                if r:
                    nc.vector.tensor_copy(probs_t[:, u % 2, 0:r], core.ps[:, 4, 0:r])
                nc.vector.tensor_copy(probs_t[0:META, u % 2, LAT:LAT + n], core.ps[0:META, 5, 0:n]
                                      ).then_inc(turned_in.sem, 1)
            finish(n_units - 1)
            chain.close(step.n)
    core.close(FOX_BLOCKS, FOX_BLOCKS)
    norm.close()
    v_turned.close(4)
    v_copied.close(4)
    act_chain.close(3)
    for s in (scored, peak, expd, turned, turned_in, summed_v, written):
        s.close(n_units)
    c_in.close(16 * FOX_HEADS)
    ones_in.close(1)
    summed_c.close(1)


def retention(core, arena, acts, l, y, h_hi, h_lo):
    nc, dram = core.nc, core.dram
    a = Alloc(arena, (LT + 1) * D)
    qk = a(2 * RET_HEADS, SEQ2)
    cos, sin = a(1, SEQ2)[:, 0, :], a(1, SEQ2)[:, 0, :]
    decay = a(RET_HEADS, SEQ2)
    v, gate = a(LT + 1, RET_HEADS * RET_DIM), a(LT + 1, RET_HEADS * RET_DIM)
    work = a(2, SEQ2)
    score = a(LT + 1, SEQ2)
    gain = a(1, RET_HEADS * RET_DIM)[:, 0, :]
    groups = (LT + 1) * RET_HEADS
    mean, var = a(1, groups)[:, 0, :], a(1, groups)[:, 0, :]
    gate_sig = v
    sq_buf = qk.rearrange("p a b -> p (a b)")[:, 0:(LT + 1) * RET_HEADS * RET_DIM].rearrange(
        "p (t n) -> p t n", t=LT + 1)
    half = RET_DIM // 2
    scale = float(RET_DIM) ** -0.5
    outs = RET_BLOCKS
    fox = FOX_HEADS * FOX_DIM
    width = RET_HEADS * RET_DIM

    tables = core.counter("tables_in")
    chain = core.counter("ret_steps")
    rotated = core.counter("ret_rotated")
    gate_in = core.counter("ret_gate_in")
    scores_p = core.counter("ret_scores")
    scored = core.counter("ret_weighted")
    summed = core.counter("ret_sums")
    copied = core.counter("ret_copied")
    moment = core.counter("ret_variance")
    root = core.counter("ret_root")
    ready = core.counter("ret_ready")
    y_turned = core.counter("y_turned")
    y_copied = core.counter("y_copied")
    tail = core.counter("ret_tail_cleared")
    turned = core.counter("values_turned")
    t_copied = core.counter("values_copied")
    hi_done = core.counter("y_hi_ready")
    out_t = core.ps[:, 4:6, :].rearrange("p b n -> p (b n)")
    flat = score[:, 0:2, :]

    pairs = [(LT, 0, LAT, META), (LT, LAT, META, 0)] + [(s, s * P, LAT - s * P, 0) for s in range(LT)]

    with nc.Block(no_gpsimd_drain=True) as block:
        @block.sync
        def _(sp):
            core.feed(sp, RET_BLOCKS)

        @block.gpsimd
        def _(pool):
            pool.dma_start(cos, dram["ret_cos"]).then_inc(tables.sem, 16)
            pool.dma_start(sin, dram["ret_sin"]).then_inc(tables.sem, 16)
            pool.dma_start(decay, dram["ret_decay"]).then_inc(tables.sem, 16)
            pool.dma_start(gain, dram["ret_gn"][l]).then_inc(tables.sem, 16)
            pool.memset(y[:, LT, fox:D], 0.0).then_inc(tail.sem, 1)
            pool.memset(gate[:, LT, :], 0.0).then_inc(tail.sem, 1)

        @block.tensor
        def _(pe):
            two = 2 * RET_HEADS

            def turn_block(n):
                pe.wait_ge(core.free.sem, core.free.at(BUFS + two + n + 1))
                if n:
                    pe.wait_ge(t_copied.sem, t_copied.at(n))
                turn_tokens(core, flat[:, n % 2, :], out_t).then_inc(turned.sem, 1)

            for j in range(RET_BLOCKS):
                w = core.arrived(pe, 0, j)
                pe.wait_ge(core.free.sem, core.free.at(j + 1))
                product_parts(nc, core.buf(j), w, KT, acts, SEQ2).then_inc(core.done, 1)
                if j > two:
                    turn_block(j - two - 1)
            turn_block(two - 1)
            pe.wait_ge(t_copied.sem, t_copied.at(two))
            pe.wait_ge(core.free.sem, core.free.at(BUFS + RET_BLOCKS))
            pe.wait_ge(rotated.sem, rotated.at(2 * RET_HEADS))
            n = 0
            for h in range(RET_HEADS):
                for s, q0, nq, _ in pairs:
                    c, rows = TOKEN_TILES[s]
                    if n >= 4:
                        pe.wait_ge(scored.sem, scored.at(n - 3))
                    nc.tensor.matmul(core.ps[0:rows, n % 4, 0:nq], qk[:, RET_HEADS + h, c:c + rows],
                                     qk[:, h, q0:q0 + nq], start=True, stop=True).then_inc(scores_p.sem, 1)
                    n += 1
                pe.wait_ge(scored.sem, scored.at(n))
                if h:
                    pe.wait_ge(copied.sem, copied.at(h))
                for t, (c, rows) in enumerate(TOKEN_TILES):
                    keys = [LT] + (list(range(t + 1)) if t < LT else [])
                    for i, s in enumerate(keys):
                        kr = TOKEN_TILES[s][1]
                        last = nc.tensor.matmul(core.ps[0:rows, 4 + t // 4, t % 4 * P:(t % 4 + 1) * P],
                                                score[0:kr, s, c:c + rows], v[0:kr, s, h * RET_DIM:(h + 1) * RET_DIM],
                                                start=i == 0, stop=i == len(keys) - 1)
                last.then_inc(summed.sem, 1)
            pe.wait_ge(ready.sem, ready.at(1))
            for t, (c, rows) in enumerate(TOKEN_TILES):
                for j in range(2):
                    n = 2 * t + j
                    if n >= 4:
                        pe.wait_ge(y_copied.sem, y_copied.at(n - 3))
                    for i in range(4):
                        f = (4 * j + i) * P
                        last = nc.tensor.transpose(core.ps[:, n % 4, i * P:i * P + rows], y[0:rows, t, f:f + P],
                                                   core.ident(rows))
                    last.then_inc(y_turned.sem, 1)

        @block.scalar
        def _(act):
            two = 2 * RET_HEADS
            for j in range(RET_BLOCKS):
                core.part_hi(act, 0, j + SPLIT)
                if j >= two:
                    n = j - two
                    core.computed(act, 0, j)
                    if n == 0:
                        act.wait_ge(core.free.sem, core.free.at(BUFS + two))
                    if n >= 2:
                        act.wait_ge(turned.sem, turned.at(n - 1))
                    nc.scalar.activation(like_psum(flat[:, n % 2, :], SEQ2), in_psum(core.buf(j), SEQ2),
                                         ACT.Copy).then_inc(core.free.sem, 1)
            act.wait_ge(core.free.sem, core.free.at(BUFS + RET_BLOCKS))
            for h in range(RET_HEADS):
                act.wait_ge(summed.sem, summed.at(h + 1))
                c = fox + h * RET_DIM
                if h == 0:
                    act.wait_ge(tail.sem, tail.at(1))
                token_major_copies(lambda o, i: nc.scalar.activation(o, i, ACT.Copy),
                                   core.ps[:, 4:6, :].rearrange("p b n -> p (b n)"),
                                   y[:, :, c:c + RET_DIM]).then_inc(copied.sem, 1)
            nc.scalar.activation(gate_sig, gate, ACT.Sigmoid).then_inc(gate_in.sem, 1)
            act.wait_ge(moment.sem, moment.at(1))
            nc.scalar.activation(var, var, ACT.Sqrt, bias=core.eps[:, 0:1], scale=1.0 / RET_DIM).then_inc(root.sem, 1)
            for n in range(2 * (LT + 1)):
                t, j = divmod(n, 2)
                c, rows = TOKEN_TILES[t]
                act.wait_ge(y_turned.sem, y_turned.at(n + 1))
                nc.scalar.activation(h_hi[:, 4 * j:4 * j + 4, c:c + rows],
                                     core.ps[:, n % 4, :].rearrange("p (i n) -> p i n", i=4)[:, :, 0:rows],
                                     ACT.Copy).then_inc(hi_done.sem, 1)

        @block.vector
        def _(dve):
            step = Steps(dve, chain)
            v_ = nc.vector
            dve.wait_ge(tables.sem, tables.at(64))
            pv = lambda j, r: in_psum(core.buf(j)[r, :], SEQ2)
            lo, hi = slice(0, half), slice(half, RET_DIM)
            for j in range(2 * RET_HEADS):
                core.part_lo(dve, 0, j + SPLIT)
                core.computed(dve, 0, j)
                step(v_.tensor_tensor(like_psum(work[:, 0, :], SEQ2), pv(j, slice(0, P)), like_psum(cos, SEQ2),
                                      ALU.mult))
                for dst, src in ((lo, hi), (hi, lo)):
                    last = v_.tensor_tensor(like_psum(work[dst, 1, :], SEQ2), pv(j, src), like_psum(sin[src, :], SEQ2),
                                            ALU.mult)
                last.then_inc(core.free.sem, 1)
                dve.wait_ge(core.free.sem, core.free.at(BUFS + j + 1))
                v_.tensor_tensor(qk[:, j, :], work[:, 0, :], work[:, 1, :], ALU.add).then_inc(rotated.sem, 1)
                dve.wait_ge(rotated.sem, rotated.at(j + 1))
            dve.wait_ge(tail.sem, tail.at(2))
            for n in range(2 * RET_HEADS + 1):
                if n < 2 * RET_HEADS:
                    core.part_lo(dve, 0, 2 * RET_HEADS + n + SPLIT)
                if n:
                    b = n - 1
                    dst = v if b < RET_HEADS else gate
                    dve.wait_ge(turned.sem, turned.at(n))
                    c = b % RET_HEADS * P
                    token_major_copies(v_.tensor_copy, out_t, dst[:, :, c:c + P]).then_inc(t_copied.sem, 1)
            dve.wait_ge(t_copied.sem, t_copied.at(2 * RET_HEADS))
            n = 0
            for h in range(RET_HEADS):
                if h:
                    dve.wait_ge(summed.sem, summed.at(h))
                for s, q0, nq, c in pairs:
                    rows = TOKEN_TILES[s][1]
                    dve.wait_ge(scores_p.sem, scores_p.at(n + 1))
                    v_.scalar_tensor_tensor(score[0:rows, s, q0:q0 + nq], core.ps[0:rows, n % 4, 0:nq], scale,
                                            decay[0:rows, h, c:c + nq], ALU.mult, ALU.mult).then_inc(scored.sem, 1)
                    n += 1
            dve.wait_ge(copied.sem, copied.at(RET_HEADS))
            o = y[:, :, fox:D]
            og = [o[:, t, :].rearrange("p (h d) -> p h d", h=RET_HEADS) for t in range(LT + 1)]
            sq = [sq_buf[:, t, :].rearrange("p (h d) -> p h d", h=RET_HEADS) for t in range(LT + 1)]
            per = lambda ap, t: ap[:, t * RET_HEADS:(t + 1) * RET_HEADS]
            bc = lambda ap: ap[:, :, None].to_broadcast([P, RET_HEADS, RET_DIM])
            for t in range(LT + 1):
                last = v_.tensor_reduce(per(mean, t), og[t], AX.X, ALU.add)
            step(last)
            step(v_.tensor_scalar(mean, mean, 1.0 / RET_DIM, None, ALU.mult))
            for t in range(LT + 1):
                last = v_.tensor_tensor(og[t], og[t], bc(per(mean, t)), ALU.subtract)
            step(last)
            step(v_.tensor_tensor(sq_buf, o, o, ALU.mult))
            for t in range(LT + 1):
                last = v_.tensor_reduce(per(var, t), sq[t], AX.X, ALU.add)
            last.then_inc(moment.sem, 1)
            dve.wait_ge(gate_in.sem, gate_in.at(1))
            step(v_.tensor_tensor(gate, gate, gate_sig, ALU.mult))
            step(v_.tensor_tensor(gate, gate, gain[:, None, :].to_broadcast([P, LT + 1, width]), ALU.mult))
            dve.wait_ge(root.sem, root.at(1))
            step(v_.reciprocal(var, var))
            for t in range(LT + 1):
                last = v_.tensor_tensor(og[t], og[t], bc(per(var, t)), ALU.mult)
            step(last)
            v_.tensor_tensor(o, o, gate, ALU.mult).then_inc(ready.sem, 1)
            for n in range(2 * (LT + 1)):
                t, j = divmod(n, 2)
                c, rows = TOKEN_TILES[t]
                dve.wait_ge(hi_done.sem, hi_done.at(n + 1))
                v_.tensor_tensor(h_lo[:, 4 * j:4 * j + 4, c:c + rows],
                                 core.ps[:, n % 4, :].rearrange("p (i n) -> p i n", i=4)[:, :, 0:rows],
                                 h_hi[:, 4 * j:4 * j + 4, c:c + rows], ALU.subtract).then_inc(y_copied.sem, 1)
            chain.close(step.n)
    core.close(RET_BLOCKS, outs)
    for s, k in ((tables, 64), (tail, 2), (rotated, 2 * RET_HEADS), (gate_in, 1), (scores_p, RET_HEADS * len(pairs)),
                 (scored, RET_HEADS * len(pairs)), (summed, RET_HEADS), (copied, RET_HEADS), (moment, 1), (root, 1),
                 (ready, 1), (y_turned, 2 * (LT + 1)), (y_copied, 2 * (LT + 1)),
                 (turned, 2 * RET_HEADS), (t_copied, 2 * RET_HEADS), (hi_done, 2 * (LT + 1))):
        s.close(k)


def load_meta(core):
    nc = core.nc
    meta = core.counter("meta_in")
    sq = Squares(core, SEQ2)
    with core.space("sq", [P, 2, ALL]) as tmp:
        with nc.Block(no_gpsimd_drain=True) as block:
            @block.sync
            def _(sp):
                sp.dma_start(core.x[:, :, LAT:SEQ2], core.dram["meta"]).then_inc(meta.sem, 16)

            @block.scalar
            def _(act):
                act.wait_ge(meta.sem, meta.at(16))
                for m in range(KT):
                    sq.square(act, tmp, m)

            @block.gpsimd
            def _(pool):
                for m in range(KT):
                    sq.add(pool, tmp, m)
    sq.close(KT)
    meta.close(16)


def store(core, result):
    stored = core.counter("result_stored")
    with core.nc.Block(no_gpsimd_drain=True) as block:
        @block.sync
        def _(sp):
            sp.dma_start(core.dram["out"], result[:, :, 0:LAT]).then_inc(stored.sem, 16)
            sp.wait_ge(stored.sem, 16)


def build(nc, dram, stop=None):
    with ExitStack() as ctx:
        core = Core(nc, ctx, dram)
        for l in range(DEPTH):
            for half in range(HALVES):
                end = DEPTH * LAYER1 + (l + 1) * LAYER2 - (HALVES - 1 - half) * FFN_BLOCKS // HALVES
                core.narrow.append((end - 2 * KT, end))
        param = core.param
        setup(core)

        @contextmanager
        def parts(width):
            with core.space("h_hi", [P, KT, width], F32R) as hi, core.space("h_lo", [P, KT, width], F32R) as lo:
                yield (hi, lo), lambda k: (hi[:, k, :], lo[:, k, :])

        for l in range(DEPTH):
            last = l == DEPTH - 1
            whole = [(0, LAT, 0), (LAT, ALL, 1)]
            some, tokens = (whole[:1], LAT) if last else (whole, ALL)
            with core.space("arena", [P, ARENA]) as arena:
                mix = arena[:, 0:KT * ALL].rearrange("p (k n) -> p k n", k=KT)
                with parts(ALL) as (h, acts):
                    norm = Norm(core, ALL, lambda k, c: core.gain[:, 0, k, c:c + 1],
                                lambda k, c: core.mod[:, 0, k, c:c + 1], whole, h)
                    fourier(core, arena, acts, mix, tokens, norm, 0 if l else MOD_BLOCKS - MOD_FIRST)
                    latent_attention(core, arena, acts, l, mix, not last)
                    m = Mlstm(arena)
                    conv_n = ALL + 4
                    acc = arena[:, 2 * ALL:2 * ALL + 2 * conv_n].rearrange("p (a n) -> p a n", a=2)
                    mlstm_inputs(core, arena, acts, l, m, acc)
                with core.space("scratch", [P, 2 * KT * ALL]) as scratch:
                    mlstm(core, arena, scratch, m, mix, not last)
                with parts(ALL) as (h, acts):
                    tmp = arena[:, KT * ALL:(KT + 2) * ALL].rearrange("p (a n) -> p a n", a=2)
                    out_projection(core, h, mix, tokens, lambda j, c: core.mod[:, 2, j, c:c + 1], some, tmp)
            with parts(ALL) as (h, acts):
                norm = Norm(core, tokens, lambda k, c: core.gain[:, 1, k, c:c + 1],
                            lambda k, c: core.mod[:, 3, k, c:c + 1], some, h)
                squared_relu_mlp(core, norm, acts, tokens, lambda j, c: core.mod[:, 5, j, c:c + 1], some, not last)
            if stop == l:
                break
        if stop is None or stop > 1:
            plain_norm(core, LAT, P_GFINAL, core.x)
            load_meta(core)
            every = [(0, SEQ2, 0)]
            for l in range(DEPTH):
                with parts(SEQ2) as (h, acts):
                    with core.space("arena", [P, ARENA]) as arena:
                        y = arena[:, 0:(LT + 1) * D].rearrange("p (t n) -> p t n", t=LT + 1)
                        norm = Norm(core, SEQ2, lambda k, c: param[:, P_ANORM + l * KT + k:P_ANORM + l * KT + k + 1],
                                    None, every, h)
                        forgetting_attention(core, arena, acts, norm, l, y)
                        retention(core, arena, acts, l, y, *h)
                    with core.space("sq", [P, 2, SEQ2]) as tmp:
                        out_projection(core, h, None, SEQ2, None, every, tmp)
                    norm = Norm(core, SEQ2, lambda k, c: param[:, P_FNORM + l * KT + k:P_FNORM + l * KT + k + 1],
                                None, every, h)
                    swiglu_mlp(core, norm, acts)
            with core.space("result", [P, KT, LAT]) as result:
                plain_norm(core, LAT, P_FINAL, result)
                store(core, result)
        else:
            store(core, core.x)



def _blocks(w, cols):
    parts = w[:, cols].reshape(-1, P, len(cols)).transpose(1, 0, 2).reshape(P, -1)
    out = np.zeros((P, BLOCK), np.float32)
    out[:, :parts.shape[1]] = parts
    return out[None]


def _stream(i):
    r = np.arange
    out = []

    def by_cols(w, start, stop, width=P):
        out.extend(_blocks(w, r(c, c + width)) for c in range(start, stop, width))

    def padded(w, groups, width):
        z = np.zeros((w.shape[0], width * len(groups)), np.float32)
        for n, g in enumerate(groups):
            for at, cols in g:
                z[:, n * width + at:n * width + at + len(cols)] = w[:, cols]
        zz = np.zeros((w.shape[0], P), np.float32)
        zz[:, :z.shape[1]] = z
        out.append(_blocks(zz, r(P)))

    f = 4 * F_GROUP
    mw = M_HEADS * M_DIM
    rot = A_ROPE // 4
    swap = np.concatenate([r(rot, 2 * rot), r(rot), r(3 * rot, 4 * rot), r(2 * rot, 3 * rot)])
    for l in range(DEPTH):
        w = i["w_in"][l]
        g0 = f + 4 * mw
        q0 = g0 + 4 * M_HEADS
        kr0 = q0 + Q_LORA + KV_LORA
        by_cols(w, 0, f)
        by_cols(w, q0, kr0)
        padded(w, [[(A_NOPE, kr0 + r(A_ROPE)), (A_QK, kr0 + swap)]], P)
        by_cols(w, f, f + 2 * mw, M_DIM)
        by_cols(w, f + 2 * mw, f + 4 * mw)
        gate = lambda n: g0 + n * M_HEADS + r(M_HEADS)
        padded(w, [[(FWD, gate(0)), (BWD, gate(2)), (F_ROW + FWD, gate(1)), (F_ROW + BWD, gate(3))]], P)
        by_cols(i["w_out"][l], 0, D)
        for q in range(QUARTERS):
            by_cols(i["w_up"][l], q * D, (q + 1) * D)
            by_cols(i["w_down"][l][q * D:(q + 1) * D], 0, D)
    fw = FOX_HEADS * FOX_DIM
    for l in range(DEPTH):
        w = i["w_in_2"][l]
        padded(w, [[(0, 3 * fw + r(FOX_HEADS))]], P)
        by_cols(w, 0, 3 * fw)
        by_cols(w, 3 * fw + FOX_HEADS, w.shape[1])
        by_cols(i["w_out_2"][l], 0, D)
        half = H_TILES * P
        for n in range(HALVES):
            for c in range(n * half, (n + 1) * half, P):
                by_cols(i["w_gate_2"][l], c, c + P)
                by_cols(i["w_up_2"][l], c, c + P)
            for c in range(0, D, P):
                k = n * half
                for kts in H_KT:
                    out.append(_blocks(i["w_down_2"][l][k:k + kts * P], r(c, c + P)))
                    k += kts * P
    out.append(np.zeros((SPLIT, P, BLOCK), np.float32))
    return np.concatenate(out)


def _modulation(i):
    return np.concatenate([_blocks(i["w_mod"][l], np.arange(c, c + P)) for l in range(DEPTH) for c in range(0, 6 * D, P)])


def _lora(i):
    rot = A_ROPE // 4
    r = np.arange
    swap = np.concatenate([r(rot, 2 * rot), r(rot), r(3 * rot, 4 * rot), r(2 * rot, 3 * rot)])
    rows = lambda v: v.reshape(2, P, -1).transpose(1, 0, 2).reshape(P, -1)
    q, kv = [], []
    for l in range(DEPTH):
        uq = i["w_uq"][l].reshape(2, P, A_HEADS, A_QK)
        q.append(np.concatenate([rows(uq), rows(uq[:, :, :, A_NOPE + swap])], 1))
        ukv = i["w_ukv"][l].reshape(P, A_HEADS, A_NOPE + A_V)
        kv.append(np.concatenate([ukv[:, :, :A_NOPE].reshape(P, -1), ukv[:, :, A_NOPE:].reshape(P, -1)], 1))
    return np.stack(q), np.stack(kv)


def _params(i):
    p = np.zeros((P, P_END), np.float32)
    tiled = lambda v: v.reshape(-1, P).T

    def put(at, v):
        p[:v.shape[0], at:at + v.shape[1]] = v

    c = np.stack([i["c"].reshape(-1), i["c_ctx"]], 1).reshape(KT, P, 2).transpose(1, 0, 2).reshape(P, -1)
    put(P_C, c)
    for l in range(DEPTH):
        put(P_BMOD + l * MOD_BLOCKS, tiled(i["b_mod"][l]))
        put(P_G1 + l * KT, tiled(i["g_norm1"][l]))
        put(P_G2 + l * KT, tiled(i["g_norm2"][l]))
        conv = i["conv_qk"][l].reshape(CONV, 2 * M_HEADS, M_DIM).transpose(2, 1, 0).reshape(M_DIM, -1)
        put(P_CONV + l * 2 * M_HEADS * CONV, conv)
        bg = i["b_gates"][l].reshape(4, M_HEADS)
        for n in range(2):
            p[FWD:FWD + M_HEADS, P_BG + 2 * l + n] = bg[n]
            p[BWD:BWD + M_HEADS, P_BG + 2 * l + n] = bg[2 + n]
        put(P_GQ + 2 * l, tiled(i["g_q_norm"][l]))
        put(P_GKV + l, tiled(i["g_kv_norm"][l]))
        put(P_ANORM + l * KT, tiled(i["attn_norm_2"][l]))
        put(P_FNORM + l * KT, tiled(i["ffn_norm_2"][l]))
        put(P_BF + l, i["b_fgate_2"][l].reshape(-1, 1))
    put(P_FINAL, tiled(i["final_norm_2"]))
    put(P_GFINAL, tiled(i["g_final"]))
    return p


def _tables():
    t = {}
    p, f = np.arange(P)[:, None], np.arange(P)[None, :]
    const = np.zeros((P, C_END))
    const[:, C_IDENT:C_IDENT + P] = np.eye(P)
    const[:, C_LOWER:C_LOWER + P] = np.where(f <= p, 0.0, NEG)
    const[:, C_UPPER:C_UPPER + P] = np.where(f >= p, 0.0, NEG)
    same = (p // F_GROUP) == (f // F_GROUP)
    ang = 2 * np.pi * ((p % F_GROUP) * (f % F_GROUP) % F_GROUP) / F_GROUP
    const[:, C_DFT:C_DFT + P] = np.cos(ang) * same
    const[:, C_DFT + P:C_END] = np.sin(ang) * same
    t["const"] = const
    for name, n in (("lat", LAT), ("ctx", CTX)):
        ang = 2 * np.pi * (np.outer(np.arange(n), np.arange(n)) % n) / n
        norm = 1.0 / np.sqrt(n * F_GROUP)
        t["cos_" + name] = (np.cos(ang) * norm).reshape(n // P, P, n).transpose(1, 0, 2)
        t["sin_" + name] = (-np.sin(ang) * norm).reshape(n // P, P, n).transpose(1, 0, 2)
    nf = A_ROPE // 4
    freqs = (10000.0 ** (-np.arange(nf, dtype=np.float32) / np.float32(nf))).astype(np.float32)
    pos = np.arange(LAT)
    axes = [(pos // GRID_W).astype(np.float32), (pos % GRID_W).astype(np.float32)]
    cos, sin = np.zeros((A_ROPE, LAT)), np.zeros((A_ROPE, LAT))
    for axis in range(2):
        a = freqs[:, None] * axes[axis][None, :]
        for part in range(2):
            rows = slice((2 * axis + part) * nf, (2 * axis + part + 1) * nf)
            cos[rows] = np.cos(a)
            sin[rows] = np.sin(a) * (-1.0 if part == 0 else 1.0)
    t["rope_cos"], t["rope_sin"] = cos, sin
    select = np.zeros((ROWS, 2 * M_HEADS, P))
    for d, row in enumerate((FWD, BWD)):
        for h in range(M_HEADS):
            select[row + h, d * M_HEADS + h] = 1.0
    t["select"] = select
    inv = (10000.0 ** (-np.arange(0, RET_DIM, 2, dtype=np.float32) / np.float32(RET_DIM))).astype(np.float32)
    place = np.concatenate([META + np.arange(LAT), np.arange(META)]).astype(np.float32)
    a = inv[:, None] * place[None, :]
    t["ret_cos"] = np.concatenate([np.cos(a), np.cos(a)])
    t["ret_sin"] = np.concatenate([np.sin(a), -np.sin(a)])
    j = np.arange(SEQ2)[None, :] - np.arange(P)[:, None]
    t["ret_decay"] = np.stack([np.where(j >= 0, np.exp(np.maximum(j, 0) * g), 0.0) for g in LOG_GAMMA], 1)
    return {k: np.ascontiguousarray(v, np.float32) for k, v in t.items()}


def _arrays(i):
    to_features = lambda v: v.reshape(v.shape[-2], KT, P).transpose(2, 1, 0)
    rows = lambda v: np.broadcast_to(v[:, None, :], (DEPTH, P, v.shape[-1]))
    arrays = {
        "weights": _stream(i),
        "w_mod": _modulation(i),
        "param": _params(i),
        "x": np.concatenate([to_features(i["x"]), to_features(i["ctx"])], 2),
        "meta": to_features(i["meta_tokens_2"]),
        "g_mlstm": rows(i["g_mlstm"]),
        "ret_gn": rows(i["ret_gn_2"]),
    }
    arrays["w_uq"], arrays["w_ukv"] = _lora(i)
    arrays.update(_tables())
    return {k: np.ascontiguousarray(v) for k, v in arrays.items()}


def kernel(**inputs):
    import concourse.bacc as bacc
    from concourse.bass_utils import run_bass_kernel_spmd

    nc = bacc.Bacc("TRN2", target_bir_lowering=False, num_devices=1)
    arrays = _arrays({k: np.asarray(v) for k, v in inputs.items()})
    dram = {k: nc.dram_tensor(k + "_dram", v.shape, mybir.dt.from_np(v.dtype), kind="ExternalInput").ap()
            for k, v in arrays.items()}
    dram["out"] = nc.dram_tensor("out_dram", (P, KT, LAT), F32, kind="ExternalOutput").ap()
    build(nc, dram)
    r = run_bass_kernel_spmd(nc, [{k + "_dram": v for k, v in arrays.items()}], core_ids=[0])
    out = r.results[0]["out_dram"]
    return np.ascontiguousarray(out.transpose(2, 1, 0).reshape(1, LAT, D))
```

```python
from contextlib import ExitStack, contextmanager

import numpy as np
import concourse.bass as bass
from concourse import mybir

F32 = mybir.dt.float32
F32R = mybir.dt.float32r
ALU = mybir.AluOpType
ACT = mybir.ActivationFunctionType
AX = mybir.AxisListType

P = 128
D = 1024
KT = D // P
DEPTH = 2
EPS = 1e-6
LAT, CTX = 512, 256
ALL = LAT + CTX
LT, CT = LAT // P, CTX // P
TT = LT + CT

F_GROUP = D // 16
M_HEADS, M_DIM = 4, 3 * D // 32
A_HEADS, A_NOPE, A_ROPE, A_V = 4, 64, 32, 3 * D // 32
A_QK = A_NOPE + A_ROPE
Q_LORA, KV_LORA = D // 4, D // 8
CONV = 5
GRID_W = 64
HID = 4 * D // P

META = 16
SEQ2 = LAT + META
FOX_HEADS, FOX_DIM = 8, 64
RET_HEADS, RET_DIM = 4, 128
FF = 2816 // P
LOG_GAMMA = [float(np.log(1.0 - 2.0 ** (-5 - h))) for h in range(RET_HEADS)]

BLOCK = 8 * P
RING = 4
SPLIT = 2
UNROLL = 4
CONV_IN = LAT + 4 + CTX + 4
LAG = 3
BUFS = 2
ROWS = 36
FWD, BWD = 0, 32
ROW0 = (FWD, BWD)
F_ROW = 64
NEG = -1.0e30

MOD_BLOCKS, MOD_RING, MOD_FIRST = 6 * D // P, 4, 2 * D // P
MOD_FOURIER = KT
FOURIER_BLOCKS, LATENT_BLOCKS = 2, 4
MLSTM_BLOCKS = 2 * M_HEADS + 3 + 3 + 1
OUT_BLOCKS = KT
QUARTERS, Q_TILES = 4, HID // 4
MLP_BLOCKS = QUARTERS * (Q_TILES + KT)
FOX_BLOCKS, RET_BLOCKS = 13, 16
HALVES, H_TILES, H_KT = 2, FF // 2, (6, 5)
FFN_BLOCKS = HALVES * (2 * H_TILES + 2 * KT)
NARROW = H_KT[0] * P
LAYER1 = FOURIER_BLOCKS + LATENT_BLOCKS + MLSTM_BLOCKS + OUT_BLOCKS + MLP_BLOCKS
LAYER2 = FOX_BLOCKS + RET_BLOCKS + OUT_BLOCKS + FFN_BLOCKS
BLOCKS = DEPTH * (LAYER1 + LAYER2) + SPLIT

C_IDENT, C_LOWER, C_UPPER, C_DFT, C_END = 0, P, 2 * P, 3 * P, 5 * P
P_BMOD = 0
P_G1 = P_BMOD + DEPTH * MOD_BLOCKS
P_G2 = P_G1 + DEPTH * KT
P_CONV = P_G2 + DEPTH * KT
P_BG = P_CONV + DEPTH * 2 * M_HEADS * CONV
P_GQ = P_BG + DEPTH * 2
P_GKV = P_GQ + DEPTH * 2
P_ANORM = P_GKV + DEPTH
P_FNORM = P_ANORM + DEPTH * KT
P_BF = P_FNORM + DEPTH * KT
P_FINAL = P_BF + DEPTH
P_GFINAL = P_FINAL + KT
P_END = P_GFINAL + KT
ARENA = 24500


class Counter:

    def __init__(self, sem):
        self.sem, self.base = sem, 0

    def at(self, n):
        return self.base + n

    def close(self, n):
        self.base += n


class Steps:

    def __init__(self, eng, count):
        self.eng, self.count, self.n = eng, count, 0

    def __call__(self, ins):
        self.n += 1
        ins.then_inc(self.count.sem, 1)
        self.eng.wait_ge(self.count.sem, self.count.at(self.n))


def whole_turns(t, i, inner):
    return (0, t * inner + i) if isinstance(t, int) else (t, i)


class Core:

    def __init__(self, nc, ctx, dram):
        self.nc, self.ctx, self.dram = nc, ctx, dram
        self.counters = {}

        def sb(name, shape, dtype=F32):
            return ctx.enter_context(nc.sbuf_tensor(name, shape, dtype))

        self.x = sb("x", [P, KT, ALL])
        self.sumsq = sb("sumsq", [P, ALL])
        self.ring = sb("ring", [P, RING, BLOCK])
        self.hi_ring = sb("hi_ring", [P, SPLIT, BLOCK], F32R)
        self.lo_ring = sb("lo_ring", [P, SPLIT, BLOCK], F32R)
        self.const = sb("const", [P, C_END])
        self.param = sb("param", [P, P_END])
        self.ones = sb("ones", [P, P])
        self.eps = sb("eps", [P, 1])
        self.mod_sum = sb("mod_sum", [P, MOD_BLOCKS, 2])
        self.mod = sb("mod", [P, 6, KT, 2])
        self.gain = sb("gain", [P, 2, KT, 2])
        self.ps = ctx.enter_context(nc.psum_tensor("ps", [P, 8, 512], F32))
        self.landed = [ctx.enter_context(nc.semaphore(f"block_landed_{i}")) for i in range(RING)]
        self.done = ctx.enter_context(nc.semaphore("block_done"))
        self.block0 = 0
        self.loaded = 0
        self.free = self.counter("psum_free")
        self.hi = ctx.enter_context(nc.semaphore("block_hi"))
        self.lo = ctx.enter_context(nc.semaphore("block_lo"))
        self.narrow = []
        self.mod_landed = [ctx.enter_context(nc.semaphore(f"mod_landed_{i}")) for i in range(MOD_RING)]
        self.mod_done = ctx.enter_context(nc.semaphore("mod_sum_done"))
        self.added = self.counter("squares_added")
        self.mod_used = 0
        self.names = 0

    @contextmanager
    def space(self, name, shape, dtype=F32):
        self.names += 1
        with self.nc.sbuf_tensor(f"{name}_{self.names}", shape, dtype) as t:
            yield t

    def counter(self, name):
        if name not in self.counters:
            self.counters[name] = Counter(self.ctx.enter_context(self.nc.semaphore(name)))
        return self.counters[name]

    def ident(self, n):
        return self.const[0:n, C_IDENT:C_IDENT + n]

    def buf(self, j):
        j %= BUFS
        return self.ps[:, 2 * j:2 * j + 2, :].rearrange("p b n -> p (b n)")

    def width(self, g):
        return NARROW if any(a <= g < b for a, b in self.narrow) else BLOCK

    def load(self, sp, g, t=0, inner=0):
        w = self.width(g)
        if g >= RING:
            sp.wait_ge(self.lo, t * inner + (g - RING + 1))
        sp.dma_start(self.ring[:, g % RING, 0:w],
                     self.dram["weights"][t * inner + g, :, 0:w]).then_inc(self.landed[g % RING], 16)

    def feed(self, sp, n):
        n = min(n, BLOCKS - self.loaded)
        while n > 0:
            g = self.loaded
            end = next((c for r in self.narrow for c in r if c > g), BLOCKS)
            run = min(n, end - g)

            if g < RING:
                for i in range(run):
                    self.load(sp, g + i)
            else:
                tiles(sp, run, UNROLL, lambda t, i: self.load(sp, g + i, t, UNROLL))
            self.loaded += run
            n -= run

    def part_hi(self, act, t, i, inner=UNROLL):
        t, i = whole_turns(t, i, inner)
        g = self.block0 + i
        w = self.width(g)
        if g < BLOCKS:
            act.wait_ge(self.landed[g % RING], t * (16 * inner // RING) + 16 * (g // RING + 1))
            if g >= SPLIT:
                act.wait_ge(self.done, t * inner + (g - SPLIT + 1))
            self.nc.scalar.activation(self.hi_ring[:, g % SPLIT, 0:w], self.ring[:, g % RING, 0:w],
                                      ACT.Copy).then_inc(self.hi, 1)

    def part_lo(self, dve, t, i, inner=UNROLL):
        t, i = whole_turns(t, i, inner)
        g = self.block0 + i
        w = self.width(g)
        if g < BLOCKS:
            dve.wait_ge(self.hi, t * inner + (g + 1))
            self.nc.vector.tensor_tensor(self.lo_ring[:, g % SPLIT, 0:w], self.ring[:, g % RING, 0:w],
                                         self.hi_ring[:, g % SPLIT, 0:w], ALU.subtract).then_inc(self.lo, 1)

    def arrived(self, pe, t, i, inner=UNROLL):
        g = self.block0 + i
        pe.wait_ge(self.lo, t * inner + (g + 1))
        return self.hi_ring[:, g % SPLIT, :], self.lo_ring[:, g % SPLIT, :]

    def buf4(self, j):
        j %= 4
        return self.ps[:, 2 * j:2 * j + 2, :].rearrange("p b n -> p (b n)")

    def computed(self, eng, t, i, inner=UNROLL):
        eng.wait_ge(self.done, t * inner + (self.block0 + i + 1))

    def close(self, blocks, outputs):
        self.block0 += blocks
        self.free.close(outputs)


def tiles(eng, n, unroll, body):
    full = n // unroll
    if full > 1:
        with eng.Fori(0, full) as t:
            for i in range(unroll):
                body(t, i)
    elif full:
        for i in range(unroll):
            body(0, i)
    for i in range(n - full * unroll):
        body(full, i)


def segments(tokens):
    if tokens == SEQ2:
        return [(0, 0, SEQ2 // 2), (512, SEQ2 // 2, SEQ2 // 2)]
    return [(c, c, min(512, tokens - c)) for c in range(0, tokens, 512)]


def in_psum(buf, tokens):
    if tokens == SEQ2:
        return buf.rearrange("p (b n) -> p b n", b=2)[:, :, 0:SEQ2 // 2]
    return buf[:, 0:tokens]


def like_psum(ap, tokens):
    return ap.rearrange("p (b n) -> p b n", b=2) if tokens == SEQ2 else ap


def product(nc, out, weights, acts, tokens, m, row=0, first=True, last=True):
    for c, t0, n in segments(tokens):
        for k, (w, a) in enumerate(zip(weights, acts)):
            ins = nc.tensor.matmul(out[row:row + m, c:c + n], w, a[:, t0:t0 + n],
                                   start=first and k == 0, stop=last and k == len(weights) - 1)
    return ins


def tile_product(nc, out, slots, k, kts, acts, tokens, m=P, first=True, last=True):
    w_hi, w_lo = (by_tile(s, kts, m)[k] for s in slots)
    a_hi, a_lo = acts(k)
    for c, t0, n in segments(tokens):
        for p, (w, a) in enumerate(((w_hi, a_hi), (w_hi, a_lo), (w_lo, a_hi))):
            ins = nc.tensor.matmul(out[0:m, c:c + n], w, a[:, t0:t0 + n], start=first and k == 0 and p == 0,
                                   stop=last and k == kts - 1 and p == 2)
    return ins


def product_parts(nc, out, slots, kts, acts, tokens, m=P, first=True, last=True, before=None):
    for k in range(kts):
        if before is not None:
            before(k)
        ins = tile_product(nc, out, slots, k, kts, acts, tokens, m, first, last)
    return ins


def product_pair(core, pe, t, i, inner, kts, acts, tokens, free, before):
    slots = []
    for k in range(kts + LAG):
        if k in (0, LAG):
            slots.append(core.arrived(pe, t, i + len(slots), inner))
            free(i + len(slots) - 1)
        if k < kts:
            before(k)
            last = tile_product(core.nc, core.buf(i), slots[0], k, kts, acts, tokens)
            if k == kts - 1:
                last.then_inc(core.done, 1)
        if k >= LAG:
            last = tile_product(core.nc, core.buf(i + 1), slots[1], k - LAG, kts, acts, tokens)
    last.then_inc(core.done, 1)


def by_tile(slot, n, width=P):
    return [slot[:, k * width:(k + 1) * width] for k in range(n)]


class Alloc:

    def __init__(self, tensor, start=0):
        self.arena, self.at = tensor, start
        self.size = tensor.shape[1]

    def __call__(self, *shape):
        n = int(np.prod(shape))
        ap = self.arena[:, self.at:self.at + n]
        self.at += n
        assert self.at <= self.size, (self.at, self.size)
        if len(shape) == 2:
            ap = ap.rearrange("p (a b) -> p a b", a=shape[0])
        elif len(shape) == 3:
            ap = ap.rearrange("p (a b c) -> p a b c", a=shape[0], b=shape[1])
        return ap


class Modulation:

    def __init__(self, core, l, first, count, ring, rows, lead=0):
        self.core, self.l, self.first, self.count, self.lead = core, l, first, count, lead
        self.lead_made = core.counter("last_gate_ready")
        self.ring = ring.rearrange("p (r n) -> p r n", r=MOD_RING)
        self.rows, self.scratch = rows[:, 0:2, :], rows[:, 2:4, :]
        self.base, self.fed = core.mod_used, 0
        self.rows_in, self.gates, self.made = (core.counter("silu_" + n) for n in ("rows_in", "gates", "made"))
        self.steps, self.n = core.counter("mod_steps"), 0

    def load(self, sp, t, i, inner=MOD_RING):
        core, g = self.core, self.base + i
        if g >= MOD_RING:
            sp.wait_ge(core.mod_done, t * (2 * inner) + 2 * (g - MOD_RING + 1))
        sp.dma_start(self.ring[:, g % MOD_RING, :],
                     core.dram["w_mod"][t * inner + g]).then_inc(core.mod_landed[g % MOD_RING], 16)

    def feed(self, sp, n=None):
        n, first = self.count if n is None else n, self.fed
        self.fed += n
        if self.base + first < MOD_RING:
            for i in range(n):
                self.load(sp, 0, first + i)
        else:
            tiles(sp, n, MOD_RING, lambda t, i: self.load(sp, t, first + i))

    def load_rows(self, act):
        act.dma_start(self.rows.rearrange("p c n -> p (c n)"),
                      self.core.dram["c_rows"].to_broadcast([P, 2 * D])).then_inc(self.rows_in.sem, 16)

    def sigmoid(self, act):
        act.wait_ge(self.rows_in.sem, self.rows_in.at(16))
        self.core.nc.scalar.activation(self.scratch, self.rows, ACT.Sigmoid).then_inc(self.gates.sem, 1)

    def begin(self, dve):
        dve.wait_ge(self.gates.sem, self.gates.at(1))
        self.core.nc.vector.tensor_tensor(self.rows, self.rows, self.scratch, ALU.mult).then_inc(self.made.sem, 1)
        dve.wait_ge(self.made.sem, self.made.at(1))

    def sums(self, dve, t, i, inner=MOD_RING):
        core, g = self.core, self.base + i
        dve.wait_ge(core.mod_landed[g % MOD_RING], t * (16 * inner // MOD_RING) + 16 * (g // MOD_RING + 1))
        for c in range(2):
            if g:
                dve.wait_ge(core.mod_done, t * (2 * inner) + 2 * g + c - 1)
            core.nc.vector.scalar_tensor_tensor(self.scratch[:, c, :], self.ring[:, g % MOD_RING, :], 1.0,
                                                self.rows[:, c, :], ALU.mult, ALU.mult,
                                                accum_out=core.mod_sum[:, t * inner + (self.first + i), c:c + 1]
                                                ).then_inc(core.mod_done, 1)

    def all_sums(self, dve):
        head = max(0, MOD_RING - self.base)
        for i in range(head):
            self.sums(dve, 0, i)
        tiles(dve, self.count - head, MOD_RING, lambda t, i: self.sums(dve, t, head + i))

    def finish(self, dve):
        core, v, l = self.core, self.core.nc.vector, self.l
        step = Steps(dve, self.steps)
        b0, b1 = self.first, self.first + self.count - self.lead
        dve.wait_ge(core.mod_done, 2 * (self.base + self.count))
        b = core.param[:, P_BMOD + l * MOD_BLOCKS + b0:P_BMOD + l * MOD_BLOCKS + b1]
        mod = core.mod[:].rearrange("p s k c -> p (s k) c")[:, b0:b1, :]
        step(v.tensor_tensor(mod, core.mod_sum[:, b0 + self.lead:b1 + self.lead, :],
                             b[:, :, None].to_broadcast([P, b1 - b0, 2]), ALU.add))
        for n, (g, scale) in enumerate(((P_G1, 1), (P_G2, 4))):
            if b0 <= scale * KT < b1:
                gn = core.param[:, g + l * KT:g + (l + 1) * KT]
                step(v.scalar_tensor_tensor(core.gain[:, n, :, :], core.mod[:, scale, :, :], 1.0,
                                            gn[:, :, None].to_broadcast([P, KT, 2]), ALU.add, ALU.mult))
        self.n = step.n

    def finish_lead(self, dve, t, inner):
        core, n = self.core, self.lead
        dve.wait_ge(core.mod_done, t * (2 * inner) + 2 * (self.base + n))
        b = core.param[:, P_BMOD + self.l * MOD_BLOCKS - n:P_BMOD + self.l * MOD_BLOCKS]
        mod = core.mod[:].rearrange("p s k c -> p (s k) c")[:, MOD_BLOCKS - n:MOD_BLOCKS, :]
        core.nc.vector.tensor_tensor(mod, core.mod_sum[:, 0:n, :], b[:, :, None].to_broadcast([P, n, 2]),
                                     ALU.add).then_inc(self.lead_made.sem, 1)
        dve.wait_ge(self.lead_made.sem, t + self.lead_made.at(1))

    def close(self, leads=0):
        self.lead_made.close(leads)
        self.core.mod_used += self.count
        self.rows_in.close(16)
        self.gates.close(1)
        self.made.close(1)
        self.steps.close(self.n)


def setup(core):
    nc, dram = core.nc, core.dram
    inputs, x_in = core.counter("inputs_in"), core.counter("x_in")
    ready = core.counter("setup_steps")
    sq = Squares(core, ALL)
    with core.space("mod_ring", [P, MOD_RING * BLOCK]) as ring, core.space("silu_rows", [P, 4, D]) as rows, \
            core.space("sq", [P, 2, ALL]) as tmp:
        mod = Modulation(core, 0, 0, MOD_FIRST, ring[:], rows[:])
        with nc.Block(no_gpsimd_drain=True) as block:
            @block.sync
            def _(sp):
                sp.dma_start(core.param[:], dram["param"]).then_inc(inputs.sem, 16)
                mod.feed(sp, MOD_RING)
                sp.dma_start(core.x[:], dram["x"]).then_inc(x_in.sem, 16)
                mod.feed(sp, MOD_FIRST - MOD_RING)
                core.feed(sp, RING)

            @block.gpsimd
            def _(pool):
                for m in range(KT):
                    sq.add(pool, tmp, m)

            @block.scalar
            def _(act):
                mod.load_rows(act)
                act.dma_start(core.const[:], dram["const"]).then_inc(inputs.sem, 16)
                mod.sigmoid(act)
                act.wait_ge(x_in.sem, 16)
                for m in range(KT):
                    sq.square(act, tmp, m)
                for i in range(SPLIT):
                    core.part_hi(act, 0, i)

            @block.vector
            def _(dve):
                step = Steps(dve, ready)
                step(nc.vector.memset(core.ones[:], 1.0))
                for n in range(BUFS):
                    nc.vector.memset(core.eps[:], EPS).then_inc(core.free.sem, 1)
                    dve.wait_ge(core.free.sem, n + 1)
                dve.wait_ge(inputs.sem, 32)
                mod.begin(dve)
                mod.all_sums(dve)
                for i in range(SPLIT):
                    core.part_lo(dve, 0, i)
                mod.finish(dve)
    ready.close(1)
    inputs.close(32)
    x_in.close(16)
    mod.close()
    sq.close(KT)


class Squares:

    def __init__(self, core, tokens):
        self.core, self.tokens = core, tokens
        self.squared = core.counter("tile_squared")

    def square(self, act, tmp, m, i=None, t=0, inner=0):
        core, n = self.core, self.tokens
        i = m if i is None else i
        act.wait_ge(core.added.sem, t * inner + core.added.at(max(i - 1, 0)))
        core.nc.scalar.activation(tmp[:, i % 2, 0:n], core.x[:, m, 0:n], ACT.Square).then_inc(self.squared.sem, 1)

    def add(self, pool, tmp, m, i=None, t=0, inner=0, fresh=None):
        core, n = self.core, self.tokens
        i = m if i is None else i
        pool.wait_ge(self.squared.sem, t * inner + self.squared.at(i + 1))
        pool.wait_ge(core.added.sem, t * inner + core.added.at(i))
        dst, src = core.sumsq[:, 0:n], tmp[:, i % 2, 0:n]
        if m == 0 if fresh is None else fresh:
            if isinstance(t, int):
                ins = core.nc.gpsimd.tensor_copy(dst, src)
            else:
                ins = core.nc.gpsimd.tensor_tensor(dst, src, core.ones[:, 0:1].to_broadcast([P, n]), ALU.mult)
            ins.then_inc(core.added.sem, 1)
        else:
            core.nc.gpsimd.tensor_tensor(dst, dst, src, ALU.add).then_inc(core.added.sem, 1)

    def close(self, n):
        self.squared.close(n)
        self.core.added.close(n)


class Norm:

    def __init__(self, core, tokens, gains, shifts, groups, h):
        self.core, self.tokens, self.gains, self.shifts, self.groups = core, tokens, gains, shifts, groups
        self.h_hi, self.h_lo = h
        self.summed, self.root, self.inverse, self.made, self.hi, self.ready = (
            core.counter("norm_" + n) for n in ("summed", "root", "inverse", "made", "hi", "ready"))
        self.acc = core.ps[:, 4:6, :].rearrange("p b n -> p (b n)")

    def on_pe(self, pe):
        core = self.core
        pe.wait_ge(core.added.sem, core.added.at(0))
        product(core.nc, self.acc, [core.ones[:]], [core.sumsq[:]], self.tokens, P).then_inc(self.summed.sem, 1)

    def on_act(self, act):
        core, n, groups = self.core, self.tokens, self.groups
        act.wait_ge(self.summed.sem, self.summed.at(1))
        core.nc.scalar.activation(like_psum(core.sumsq[:, 0:n], n), in_psum(self.acc, n), ACT.Sqrt,
                                  bias=core.eps[:, 0:1], scale=1.0 / D).then_inc(self.root.sem, 1)
        for k in range(KT):
            act.wait_ge(self.made.sem, self.made.at(k + 1))
            for t0, t1, c in groups:
                src = self.tmp[:, k % 2, t0:t1]
                if self.shifts is None:
                    ins = core.nc.scalar.activation(self.h_hi[:, k, t0:t1], src, ACT.Copy)
                else:
                    ins = core.nc.scalar.activation(self.h_hi[:, k, t0:t1], src, ACT.Identity,
                                                    bias=self.shifts(k, c))
            ins.then_inc(self.hi.sem, 1)

    def on_dve(self, dve, tmp):
        core, n, groups, v = self.core, self.tokens, self.groups, self.core.nc.vector
        dve.wait_ge(self.root.sem, self.root.at(1))
        v.reciprocal(core.sumsq[:, 0:n], core.sumsq[:, 0:n]).then_inc(self.inverse.sem, 1)
        dve.wait_ge(self.inverse.sem, self.inverse.at(1))

        def rest(k):
            dve.wait_ge(self.hi.sem, self.hi.at(k + 1))
            for t0, t1, c in groups:
                src, hi, lo = tmp[:, k % 2, t0:t1], self.h_hi[:, k, t0:t1], self.h_lo[:, k, t0:t1]
                if self.shifts is None:
                    ins = v.tensor_tensor(lo, src, hi, ALU.subtract)
                else:
                    ins = v.scalar_tensor_tensor(lo, src, self.shifts(k, c), hi, ALU.add, ALU.subtract)
            ins.then_inc(self.ready.sem, 1)

        for k in range(KT):
            if k >= 2:
                dve.wait_ge(self.ready.sem, self.ready.at(k - 1))
            for t0, t1, c in groups:
                ins = v.scalar_tensor_tensor(tmp[:, k % 2, t0:t1], core.x[:, k, t0:t1], self.gains(k, c),
                                             core.sumsq[:, t0:t1], ALU.mult, ALU.mult)
            ins.then_inc(self.made.sem, 1)
            if k:
                rest(k - 1)
        dve.wait_ge(self.made.sem, self.made.at(KT))
        rest(KT - 1)

    def wait_tile(self, pe):
        return lambda k: pe.wait_ge(self.ready.sem, self.ready.at(k + 1))

    def close(self):
        for c, n in ((self.summed, 1), (self.root, 1), (self.inverse, 1), (self.made, KT), (self.hi, KT),
                     (self.ready, KT)):
            c.close(n)


def plain_norm(core, tokens, gain, to):
    nc = core.nc
    summed, root, steps = core.counter("norm_summed"), core.counter("norm_root"), core.counter("norm_steps")
    acc = core.ps[:, 4:6, :].rearrange("p b n -> p (b n)")
    s = core.sumsq[:, 0:tokens]
    with nc.Block(no_gpsimd_drain=True) as block:
        @block.tensor
        def _(pe):
            pe.wait_ge(core.added.sem, core.added.at(0))
            product(nc, acc, [core.ones[:]], [core.sumsq[:]], tokens, P).then_inc(summed.sem, 1)

        @block.scalar
        def _(act):
            act.wait_ge(summed.sem, summed.at(1))
            nc.scalar.activation(s, acc[:, 0:tokens], ACT.Sqrt, bias=core.eps[:, 0:1],
                                 scale=1.0 / D).then_inc(root.sem, 1)

        @block.vector
        def _(dve):
            step = Steps(dve, steps)
            dve.wait_ge(root.sem, root.at(1))
            step(nc.vector.reciprocal(s, s))
            for k in range(KT):
                last = nc.vector.scalar_tensor_tensor(to[:, k, 0:tokens], core.x[:, k, 0:tokens],
                                                      core.param[:, gain + k:gain + k + 1], s, ALU.mult, ALU.mult)
            step(last)
    summed.close(1)
    root.close(1)
    steps.close(2)


def add_output(core, dve, dst_tile, src, tokens, groups, gate):
    v = core.nc.vector
    for t0, t1, c in groups:
        dst = like_psum(dst_tile[:, t0:t1], tokens)
        s = in_psum(src, tokens) if tokens == SEQ2 else src[:, t0:t1]
        if gate is None:
            ins = v.tensor_tensor(dst, s, dst, ALU.add)
        else:
            ins = v.scalar_tensor_tensor(dst, s, gate(c), dst, ALU.mult, ALU.add)
    return ins


def out_projection(core, h, mix, tokens, gates, groups, tmp, mod=None):
    nc = core.nc
    h_hi, h_lo = h
    hi, ready = core.counter("mix_hi"), core.counter("mix_ready")
    sq = Squares(core, tokens)
    with nc.Block(no_gpsimd_drain=True) as block:
        @block.sync
        def _(sp):
            if mod:
                for i in range(OUT_BLOCKS):
                    for n in range(i * mod.count // OUT_BLOCKS, (i + 1) * mod.count // OUT_BLOCKS):
                        mod.load(sp, 0, n)
                    core.feed(sp, 1)
            else:
                core.feed(sp, OUT_BLOCKS)

        @block.gpsimd
        def _(pool):
            for m in range(KT):
                sq.add(pool, tmp, m)

        @block.tensor
        def _(pe):
            free = lambda i: pe.wait_ge(core.free.sem, core.free.at(i + 1))
            acts = lambda k: (h_hi[:, k, :], h_lo[:, k, :])
            if mix is not None:
                product_pair(core, pe, 0, 0, UNROLL, KT, acts, tokens, free,
                             lambda k: pe.wait_ge(ready.sem, ready.at(k + 1)))
            for i in range(0 if mix is None else 2, OUT_BLOCKS):
                w = core.arrived(pe, 0, i)
                free(i)
                product_parts(nc, core.buf(i), w, KT, acts, tokens).then_inc(core.done, 1)

        @block.scalar
        def _(act):
            if mod:
                mod.load_rows(act)
            if mix is not None:
                for k in range(KT):
                    nc.scalar.activation(h_hi[:, k, 0:tokens], mix[:, k, 0:tokens], ACT.Copy).then_inc(hi.sem, 1)
            if mod:
                mod.sigmoid(act)
            for i in range(OUT_BLOCKS):
                core.part_hi(act, 0, i + SPLIT)
                act.wait_ge(core.free.sem, core.free.at(BUFS + i + 1))
                sq.square(act, tmp, i)

        @block.vector
        def _(dve):
            if mix is not None:
                for k in range(KT):
                    dve.wait_ge(hi.sem, hi.at(k + 1))
                    nc.vector.tensor_tensor(h_lo[:, k, 0:tokens], mix[:, k, 0:tokens], h_hi[:, k, 0:tokens],
                                            ALU.subtract).then_inc(ready.sem, 1)
            for i in range(OUT_BLOCKS):
                core.part_lo(dve, 0, i + SPLIT)
                core.computed(dve, 0, i)
                add_output(core, dve, core.x[:, i, :], core.buf(i), tokens, groups,
                           None if gates is None else lambda c: gates(i, c)).then_inc(core.free.sem, 1)
                if mod:
                    if i == 0:
                        mod.begin(dve)
                    for n in range(i * mod.count // OUT_BLOCKS, (i + 1) * mod.count // OUT_BLOCKS):
                        mod.sums(dve, 0, n)
            if mod:
                dve.wait_ge(core.free.sem, core.free.at(BUFS + OUT_BLOCKS))
                mod.finish(dve)
    core.close(OUT_BLOCKS, OUT_BLOCKS)
    sq.close(KT)
    if mod:
        mod.close()
    if mix is not None:
        hi.close(KT)
        ready.close(KT)


def squared_relu_mlp(core, norm, acts, tokens, gates, groups, mods):
    nc = core.nc
    per = Q_TILES + KT
    per_mod = MOD_BLOCKS // QUARTERS
    squared = core.counter("hidden_squared")
    hi, ready = core.counter("hidden_hi"), core.counter("hidden_ready")
    sq = Squares(core, tokens)
    with ExitStack() as ctx:
        hid_hi, hid_lo = (ctx.enter_context(core.space(n, [P, Q_TILES, ALL], F32R)) for n in ("hid_hi", "hid_lo"))
        tmp = ctx.enter_context(core.space("tmp", [P, 2, ALL]))
        sqt = ctx.enter_context(core.space("sq", [P, 2, ALL]))
        if mods:
            mod = Modulation(core, 1, 0, MOD_BLOCKS, ctx.enter_context(core.space("mod_ring", [P, MOD_RING * BLOCK]))[:],
                             ctx.enter_context(core.space("silu_rows", [P, 4, D]))[:], lead=KT)
        norm.tmp = tmp
        with nc.Block(no_gpsimd_drain=True) as block:
            @block.sync
            def _(sp):
                if mods:
                    core.loaded += MLP_BLOCKS
                    with sp.Fori(0, QUARTERS) as t:
                        for i in range(per):
                            core.load(sp, core.block0 + RING + i, t, per)
                            if 0 <= i - 2 < per_mod:
                                mod.load(sp, t, i - 2, per_mod)
                else:
                    core.feed(sp, MLP_BLOCKS)

            @block.gpsimd
            def _(pool):
                pool.wait_ge(norm.ready.sem, norm.ready.at(KT))
                with pool.Fori(0, QUARTERS) as t:
                    for m in range(KT):
                        sq.add(pool, sqt, m, t=t, inner=KT)

            @block.tensor
            def _(pe):
                norm.on_pe(pe)
                with pe.Fori(0, QUARTERS) as t:
                    free = lambda i: pe.wait_ge(core.free.sem, t * per + core.free.at(i + 1))
                    hidden = lambda k: (hid_hi[:, k, :], hid_lo[:, k, :])
                    for b0, kts, src, before in (
                            (0, KT, acts, norm.wait_tile(pe)),
                            (Q_TILES, Q_TILES, hidden, lambda k: pe.wait_ge(ready.sem, t * Q_TILES + ready.at(k + 1)))):
                        for i in range(b0, b0 + 8):
                            w = core.arrived(pe, t, i, per)
                            free(i)
                            product_parts(nc, core.buf(i), w, kts, src, tokens,
                                          before=before if i == b0 else None).then_inc(core.done, 1)

            @block.scalar
            def _(act):
                if mods:
                    mod.load_rows(act)
                norm.on_act(act)
                if mods:
                    mod.sigmoid(act)
                with act.Fori(0, QUARTERS) as t:
                    for i in range(per):
                        core.part_hi(act, t, i + SPLIT, per)
                        if i < Q_TILES:
                            core.computed(act, t, i, per)
                            if i == 0:
                                act.wait_ge(core.free.sem, t * per + core.free.at(BUFS))
                            act.wait_ge(ready.sem, t * Q_TILES + ready.at(max(i - 1, 0)))
                            r = tmp[:, i % 2, 0:tokens]
                            nc.scalar.activation(r, core.buf(i)[:, 0:tokens], ACT.Relu).then_inc(core.free.sem, 1)
                            act.wait_ge(core.free.sem, t * per + core.free.at(BUFS + i + 1))
                            nc.scalar.activation(r, r, ACT.Square).then_inc(squared.sem, 1)
                        else:
                            act.wait_ge(core.free.sem, t * per + core.free.at(BUFS + i + 1))
                            sq.square(act, sqt, i - Q_TILES, t=t, inner=KT)

            @block.vector
            def _(dve):
                norm.on_dve(dve, tmp)
                if mods:
                    mod.begin(dve)
                with dve.Fori(0, QUARTERS) as t:
                    for i in range(per):
                        core.part_lo(dve, t, i + SPLIT, per)
                        if i < Q_TILES:
                            r = tmp[:, i % 2, 0:tokens]
                            dve.wait_ge(squared.sem, t * Q_TILES + squared.at(i + 1))
                            nc.vector.tensor_copy(hid_hi[:, i, 0:tokens], r).then_inc(hi.sem, 1)
                            dve.wait_ge(hi.sem, t * Q_TILES + hi.at(i + 1))
                            nc.vector.tensor_tensor(hid_lo[:, i, 0:tokens], r, hid_hi[:, i, 0:tokens],
                                                    ALU.subtract).then_inc(ready.sem, 1)
                        else:
                            m = i - Q_TILES
                            core.computed(dve, t, i, per)
                            if m == 0:
                                dve.wait_ge(core.free.sem, t * per + core.free.at(BUFS + Q_TILES))
                                if mods:
                                    mod.finish_lead(dve, t, per_mod)
                            add_output(core, dve, core.x[:, m, :], core.buf(i), tokens, groups,
                                       lambda c: gates(m, c)).then_inc(core.free.sem, 1)
                        if mods and i < per_mod:
                            mod.sums(dve, t, i, per_mod)
                if mods:
                    dve.wait_ge(core.free.sem, core.free.at(BUFS + QUARTERS * per))
                    mod.finish(dve)
    core.close(MLP_BLOCKS, QUARTERS * per)
    for c, n in ((squared, Q_TILES), (hi, Q_TILES), (ready, Q_TILES)):
        c.close(n * QUARTERS)
    sq.close(KT * QUARTERS)
    norm.close()
    if mods:
        mod.close(QUARTERS)


def swiglu_mlp(core, norm, acts):
    nc = core.nc
    n_up, n_down = 2 * H_TILES, 2 * KT
    outs = n_up + KT
    sigmoid = core.counter("gate_sigmoid")
    hi, ready = core.counter("hidden_hi"), core.counter("hidden_ready")
    cleared = core.counter("sumsq_cleared")
    sq = Squares(core, SEQ2)
    with ExitStack() as ctx:
        hid_hi, hid_lo = (ctx.enter_context(core.space(n, [P, H_TILES, SEQ2], F32R)) for n in ("hid_hi", "hid_lo"))
        tmp = ctx.enter_context(core.space("tmp", [P, 2, SEQ2]))
        sqt = ctx.enter_context(core.space("sq", [P, 2, SEQ2]))
        norm.tmp = tmp
        with nc.Block(no_gpsimd_drain=True) as block:
            @block.sync
            def _(sp):
                core.feed(sp, FFN_BLOCKS)

            @block.gpsimd
            def _(pool):
                pool.wait_ge(norm.ready.sem, norm.ready.at(KT))
                for half in range(HALVES):
                    if half:
                        pool.wait_ge(core.added.sem, core.added.at(half * KT))
                    nc.gpsimd.memset(core.sumsq[:, 0:SEQ2], 0.0).then_inc(cleared.sem, 1)
                    pool.wait_ge(cleared.sem, cleared.at(half + 1))
                    with pool.Fori(0, KT // 2) as t:
                        for o in range(2):
                            sq.add(pool, sqt, o, i=half * KT + o, t=t, inner=2, fresh=False)

            @block.tensor
            def _(pe):
                norm.on_pe(pe)
                for half in range(HALVES):
                    b0, f0 = half * (n_up + n_down), half * outs

                    def up(t, i):
                        w = core.arrived(pe, t, b0 + i)
                        pe.wait_ge(core.free.sem, t * UNROLL + core.free.at(f0 + i + 1))
                        product_parts(nc, core.buf(i), w, KT, acts, SEQ2,
                                      before=norm.wait_tile(pe) if i == 0 and half == 0 else None
                                      ).then_inc(core.done, 1)

                    def down(t, i):
                        o, p = divmod(i, 2)
                        w = core.arrived(pe, t, b0 + n_up + i)
                        if p == 0:
                            pe.wait_ge(core.free.sem, t * 2 + core.free.at(f0 + n_up + o + 1))
                        k0 = p * H_KT[0]
                        product_parts(nc, core.buf(o), w, H_KT[p], lambda k: (hid_hi[:, k0 + k, :], hid_lo[:, k0 + k, :]),
                                      SEQ2, first=p == 0, last=p == 1,
                                      before=lambda k: pe.wait_ge(ready.sem, ready.at(half * H_TILES + k0 + k + 1))
                                      ).then_inc(core.done, 1)

                    tiles(pe, n_up, UNROLL, up)
                    tiles(pe, n_down, UNROLL, down)

            @block.scalar
            def _(act):
                norm.on_act(act)
                for half in range(HALVES):
                    b0, f0 = half * (n_up + n_down), half * outs

                    def pair(t, i):
                        core.part_hi(act, t, b0 + 2 * i + SPLIT)
                        core.computed(act, t, b0 + 2 * i)
                        act.wait_ge(ready.sem, t * 2 + ready.at(half * H_TILES + max(i - 1, 0)))
                        nc.scalar.activation(like_psum(tmp[:, i % 2, :], SEQ2), in_psum(core.buf(0), SEQ2),
                                             ACT.Sigmoid).then_inc(sigmoid.sem, 1)
                        core.part_hi(act, t, b0 + 2 * i + 1 + SPLIT)

                    def out(t, i):
                        o, p = divmod(i, 2)
                        core.part_hi(act, t, b0 + n_up + i + SPLIT)
                        if p:
                            act.wait_ge(core.free.sem, t * 2 + core.free.at(f0 + n_up + BUFS + o + 1))
                            sq.square(act, sqt, t * 2 + o, i=half * KT + o, t=t, inner=2)

                    tiles(act, H_TILES, 2, pair)
                    tiles(act, n_down - UNROLL, UNROLL, out)
                    for i in range(UNROLL):
                        out((n_down - UNROLL) // UNROLL, i)

            @block.vector
            def _(dve):
                v = nc.vector
                norm.on_dve(dve, tmp)
                for half in range(HALVES):
                    b0, f0 = half * (n_up + n_down), half * outs

                    def pair(t, i):
                        s = tmp[:, i % 2, :]
                        n = half * H_TILES + i + 1
                        core.part_lo(dve, t, b0 + 2 * i + SPLIT)
                        dve.wait_ge(sigmoid.sem, t * 2 + sigmoid.at(n))
                        v.tensor_tensor(like_psum(s, SEQ2), in_psum(core.buf(0), SEQ2), like_psum(s, SEQ2),
                                        ALU.mult).then_inc(core.free.sem, 1)
                        core.part_lo(dve, t, b0 + 2 * i + 1 + SPLIT)
                        dve.wait_ge(core.free.sem, t * UNROLL + core.free.at(f0 + BUFS + 2 * i + 1))
                        core.computed(dve, t, b0 + 2 * i + 1)
                        v.tensor_tensor(like_psum(s, SEQ2), in_psum(core.buf(1), SEQ2), like_psum(s, SEQ2),
                                        ALU.mult).then_inc(core.free.sem, 1)
                        dve.wait_ge(core.free.sem, t * UNROLL + core.free.at(f0 + BUFS + 2 * i + 2))
                        v.tensor_copy(hid_hi[:, t * 2 + i, :], s).then_inc(hi.sem, 1)
                        dve.wait_ge(hi.sem, t * 2 + hi.at(n))
                        v.tensor_tensor(hid_lo[:, t * 2 + i, :], s, hid_hi[:, t * 2 + i, :],
                                        ALU.subtract).then_inc(ready.sem, 1)

                    def out(t, i):
                        o, p = divmod(i, 2)
                        core.part_lo(dve, t, b0 + n_up + i + SPLIT)
                        if p:
                            core.computed(dve, t, b0 + n_up + i)
                            add_output(core, dve, core.x[:, t * 2 + o, :], core.buf(o), SEQ2, [(0, SEQ2, 0)],
                                       None).then_inc(core.free.sem, 1)

                    tiles(dve, H_TILES, 2, pair)
                    tiles(dve, n_down - UNROLL, UNROLL, out)
                    for i in range(UNROLL):
                        out((n_down - UNROLL) // UNROLL, i)
    core.close(FFN_BLOCKS, HALVES * outs)
    for c, n in ((sigmoid, H_TILES), (hi, H_TILES), (ready, H_TILES), (cleared, 1)):
        c.close(n * HALVES)
    sq.close(KT * HALVES)
    norm.close()


def fourier(core, arena, acts, mix, tokens, norm, l, mod_first, mods):
    nc, dram = core.nc, core.dram
    tiles_of = [(0, LT, 0, LAT)] + ([(LT, TT, LAT, ALL)] if tokens == ALL else [])
    a = Alloc(arena, KT * ALL)
    u, spec = a(2, ALL), a(TT, 4 * P)
    cos = [a(LT, LAT), a(CT, CTX)]
    sin = [a(LT, LAT), a(CT, CTX)]
    mod = Modulation(core, l, mod_first, mods, mix[:, 2:KT, :].rearrange("p k n -> p (k n)")[:, 0:MOD_RING * BLOCK],
                     a(4, BLOCK)) if mods else None
    norm.tmp = a(2, ALL)
    tables = core.counter("tables_in")
    evacuated = core.counter("fourier_evacuated")
    feature = core.counter("fourier_features")
    token = core.counter("fourier_tokens")
    nt = tokens // P
    with nc.Block(no_gpsimd_drain=True) as block:
        @block.sync
        def _(sp):
            core.feed(sp, FOURIER_BLOCKS)
            if mods:
                mod.feed(sp)

        @block.gpsimd
        def _(pool):
            for name, dst in (("cos_lat", cos[0]), ("sin_lat", sin[0]), ("cos_ctx", cos[1]), ("sin_ctx", sin[1])):
                pool.dma_start(dst, dram[name]).then_inc(tables.sem, 16)

        @block.tensor
        def _(pe):
            norm.on_pe(pe)
            product_pair(core, pe, 0, 0, UNROLL, KT, acts, tokens,
                         lambda j: pe.wait_ge(core.free.sem, core.free.at(j + 1)), norm.wait_tile(pe))
            pe.wait_ge(core.free.sem, core.free.at(BUFS + FOURIER_BLOCKS))
            for t in range(nt):
                if t >= 2:
                    pe.wait_ge(evacuated.sem, evacuated.at(t - 1))
                for j in range(2):
                    last = nc.tensor.matmul(core.ps[:, 4 + t % 2, j * 2 * P:(j + 1) * 2 * P],
                                            u[:, j, t * P:(t + 1) * P], core.const[:, C_DFT:C_END],
                                            start=True, stop=True)
                last.then_inc(feature.sem, 1)
            pe.wait_ge(evacuated.sem, evacuated.at(nt))
            pe.wait_ge(tables.sem, tables.at(64))
            for j in range(2):
                for n, (t0, t1, c0, c1) in enumerate(tiles_of):
                    for t in range(t0, t1):
                        for part, table in enumerate((cos[n], sin[n])):
                            last = nc.tensor.matmul(core.buf(j)[:, c0:c1],
                                                    spec[:, t, (2 * j + part) * P:(2 * j + part + 1) * P],
                                                    table[:, t - t0, :], start=t == t0 and part == 0,
                                                    stop=t == t1 - 1 and part == 1)
                last.then_inc(token.sem, 1)

        @block.scalar
        def _(act):
            if mods:
                mod.load_rows(act)
            norm.on_act(act)
            if mods:
                mod.sigmoid(act)
            for j in range(FOURIER_BLOCKS):
                core.part_hi(act, 0, j + SPLIT)
                core.computed(act, 0, j)
                nc.scalar.activation(u[:, j, 0:tokens], core.buf(j)[:, 0:tokens], ACT.Copy).then_inc(core.free.sem, 1)
            for j in range(2):
                act.wait_ge(token.sem, token.at(j + 1))
                nc.scalar.activation(mix[:, j, 0:tokens], core.buf(j)[:, 0:tokens], ACT.Copy)

        @block.vector
        def _(dve):
            norm.on_dve(dve, norm.tmp)
            if mods:
                mod.begin(dve)
            for j in range(FOURIER_BLOCKS):
                core.part_lo(dve, 0, j + SPLIT)
            for t in range(nt):
                dve.wait_ge(feature.sem, feature.at(t + 1))
                nc.vector.tensor_copy(spec[:, t, :], core.ps[:, 4 + t % 2, :]).then_inc(evacuated.sem, 1)
            if mods:
                mod.all_sums(dve)
                mod.finish(dve)
    core.close(FOURIER_BLOCKS, FOURIER_BLOCKS)
    if mods:
        mod.close()
    norm.close()
    tables.close(64)
    evacuated.close(nt)
    feature.close(nt)
    token.close(2)


def latent_attention(core, arena, acts, l, mix, ctx_queries):
    nc, dram = core.nc, core.dram
    a = Alloc(arena, KT * ALL)
    qt = a(A_HEADS, ALL)
    first, second = a(3, ALL), a(4, ALL)
    cq, ckv = first[:, 0:2, :], first[:, 2:3, :]
    work, rstd = second[:, 0:2, :], second[:, 2:4, :]
    kt, kr = a(A_HEADS, ALL), a(1, ALL)[:, 0, :]
    v = a(TT, A_HEADS * A_V)
    cos, sin = a(1, LAT)[:, 0, :], a(1, LAT)[:, 0, :]
    w_ukv = a(1, A_HEADS * (A_NOPE + A_V))[:, 0, :]
    y = first.rearrange("p a b -> p (a b)").rearrange("p (t n) -> p t n", t=TT)
    probs = second[:, 0:3, :]
    probs_t = a(2, ALL)
    w_uq = probs_t.rearrange("p a b -> p (a b)")[:, 0:BLOCK]
    top, total, inv = a(1, 32)[:, 0, :], a(1, 32)[:, 0, :], a(1, 32)[:, 0, :]
    scale = float(A_QK) ** -0.5
    rot = slice(A_NOPE, A_QK)
    gq, gkv = P_GQ + l * 2, P_GKV + l
    units = [(h, t, 0, TT) for t in range(LT) for h in range(A_HEADS)]
    if ctx_queries:
        units += [(h, t, LT, TT) for t in range(LT, TT) for h in range(A_HEADS)]
    qtiles = TT if ctx_queries else LT

    tables = core.counter("tables_in")
    steps = core.counter("latent_steps")
    squared = core.counter("latent_squared")
    summed = core.counter("latent_summed")
    root = core.counter("latent_root")
    lora_in = core.counter("lora_weights_in")
    rotated = core.counter("rotary_keys_ready")
    normed = core.counter("latent_normed")
    qk_psum = core.counter("qk_products")
    qk_copied = core.counter("qk_copied")
    scored = core.counter("scores_ready")
    peak = core.counter("row_max_ready")
    expd = core.counter("probs_ready")
    turned = core.counter("probs_turned")
    turned_in = core.counter("turned_probs_copied")
    summed_v = core.counter("attention_ready")
    written = core.counter("attention_written")
    y_turned = core.counter("y_turned")
    y_copied = core.counter("y_copied")

    with nc.Block(no_gpsimd_drain=True) as block:
        @block.sync
        def _(sp):
            core.feed(sp, LATENT_BLOCKS)

        @block.gpsimd
        def _(pool):
            pool.dma_start(cos[rot, :], dram["rope_cos"]).then_inc(tables.sem, 16)
            pool.dma_start(sin[rot, :], dram["rope_sin"]).then_inc(tables.sem, 16)
            pool.dma_start(sin[A_QK:P, :], dram["rope_sin"]).then_inc(tables.sem, 16)
            pool.dma_start(w_uq, dram["w_uq"][l]).then_inc(lora_in.sem, 16)
            pool.dma_start(w_ukv, dram["w_ukv"][l]).then_inc(lora_in.sem, 16)

        @block.tensor
        def _(pe):
            for j in range(LATENT_BLOCKS):
                w = core.arrived(pe, 0, j)
                pe.wait_ge(core.free.sem, core.free.at(j + 1))
                product_parts(nc, core.buf(j), w, KT, acts, ALL).then_inc(core.done, 1)
                if j == 2:
                    pe.wait_ge(squared.sem, squared.at(2))
                    product(nc, core.buf4(2), [core.ones[:]] * 2, [work[:, 0, :], work[:, 1, :]], ALL,
                            P).then_inc(summed.sem, 1)
            pe.wait_ge(squared.sem, squared.at(3))
            product(nc, core.buf4(3), [core.ones[:]], [work[:, 0, :]], ALL, P).then_inc(summed.sem, 1)
            pe.wait_ge(core.free.sem, core.free.at(BUFS + 4))
            pe.wait_ge(normed.sem, normed.at(1))
            pe.wait_ge(lora_in.sem, lora_in.at(32))
            wq, wkv = w_uq, w_ukv
            main = wq[:, 0:2 * A_HEADS * A_QK].rearrange("p (k n) -> p k n", k=2)
            swap = wq[:, 2 * A_HEADS * A_QK:BLOCK].rearrange("p (k n) -> p k n", k=2)
            for h in range(A_HEADS):
                if h == 1:
                    pe.wait_ge(root.sem, root.at(2))
                if h >= 2:
                    pe.wait_ge(qk_copied.sem, qk_copied.at(h - 1))
                product(nc, core.buf4(2 * h), [main[:, k, h * A_QK:(h + 1) * A_QK] for k in range(2)],
                        [cq[:, k, :] for k in range(2)], ALL, A_QK)
                last = product(nc, core.buf4(2 * h + 1), [swap[:, k, h * A_ROPE:(h + 1) * A_ROPE] for k in range(2)],
                               [cq[:, k, :] for k in range(2)], LAT, A_ROPE, row=A_NOPE)
                last.then_inc(qk_psum.sem, 1)
            pe.wait_ge(normed.sem, normed.at(2))
            for h in range(A_HEADS):
                pe.wait_ge(qk_copied.sem, qk_copied.at(A_HEADS - 1 + h // 2))
                product(nc, core.buf4(h), [wkv[:, h * A_NOPE:(h + 1) * A_NOPE]], [ckv[:, 0, :]], ALL,
                        A_NOPE).then_inc(qk_psum.sem, 1)
            for t in range(TT):
                pe.wait_ge(qk_copied.sem, qk_copied.at(A_HEADS + 3 + t // 2 if t < 4 else 2 * A_HEADS + t - 3))
                last = nc.tensor.matmul(core.ps[:, 4 + t % 4, 0:A_HEADS * A_V], ckv[:, 0, t * P:(t + 1) * P],
                                        wkv[:, A_HEADS * A_NOPE:A_HEADS * (A_NOPE + A_V)], start=True, stop=True)
                last.then_inc(qk_psum.sem, 1)
            pe.wait_ge(qk_copied.sem, qk_copied.at(2 * A_HEADS + TT))
            pe.wait_ge(rotated.sem, rotated.at(1))

            def scores(u):
                h, t, s0, s1 = units[u]
                if u >= 2:
                    pe.wait_ge(expd.sem, expd.at(u - 1))
                out = core.buf(u)
                for c0 in range(s0 * P, s1 * P, 512):
                    c1 = min(c0 + 512, s1 * P)
                    last = nc.tensor.matmul(out[:, c0 - s0 * P:c1 - s0 * P], qt[0:A_QK, h, t * P:(t + 1) * P],
                                            kt[0:A_QK, h, c0:c1], start=True, stop=True)
                last.then_inc(scored.sem, 1)

            def turn(u):
                h, t, s0, s1 = units[u]
                pe.wait_ge(expd.sem, expd.at(u + 1))
                if u >= 1:
                    pe.wait_ge(turned_in.sem, turned_in.at(u))
                for s in range(s1 - s0):
                    last = nc.tensor.transpose(core.ps[:, 4 + s // 4, (s % 4) * P:(s % 4 + 1) * P],
                                               probs[:, u % 3, s * P:(s + 1) * P], core.ident(P))
                last.then_inc(turned.sem, 1)

            def weigh(u):
                h, t, s0, s1 = units[u]
                pe.wait_ge(turned_in.sem, turned_in.at(u + 1))
                if u >= 2:
                    pe.wait_ge(written.sem, written.at(u - 1))
                for s in range(s0, s1):
                    last = nc.tensor.matmul(core.ps[:, 6 + u % 2, 0:A_V],
                                            probs_t[:, u % 2, (s - s0) * P:(s - s0 + 1) * P],
                                            v[:, s, h * A_V:(h + 1) * A_V], start=s == s0, stop=s == s1 - 1)
                last.then_inc(summed_v.sem, 1)

            scores(0)
            for u in range(len(units)):
                if u + 1 < len(units):
                    scores(u + 1)
                if u:
                    weigh(u - 1)
                turn(u)
            weigh(len(units) - 1)
            pe.wait_ge(written.sem, written.at(len(units)))
            for t in range(qtiles):
                if t >= 2:
                    pe.wait_ge(y_copied.sem, y_copied.at(t - 1))
                for j in range(3):
                    last = nc.tensor.transpose(core.ps[:, t % 2, j * P:(j + 1) * P], y[:, t, j * P:(j + 1) * P],
                                               core.ident(P))
                last.then_inc(y_turned.sem, 1)

        @block.scalar
        def _(act):
            for j in range(3):
                core.part_hi(act, 0, j + SPLIT)
                core.computed(act, 0, j)
                if j == 2:
                    act.wait_ge(summed.sem, summed.at(1))
                nc.scalar.activation(work[:, j % 2, :], core.buf(j)[:, 0:ALL], ACT.Square).then_inc(squared.sem, 1)
                nc.scalar.activation(first[:, j, :], core.buf(j)[:, 0:ALL], ACT.Copy).then_inc(core.free.sem, 1)
            nc.scalar.activation(rstd[:, 0, :], core.buf4(2)[:, 0:ALL], ACT.Sqrt, bias=core.eps[:, 0:1],
                                 scale=1.0 / Q_LORA).then_inc(root.sem, 1)
            core.part_hi(act, 0, 3 + SPLIT)
            core.computed(act, 0, 3)
            nc.scalar.activation(kr[A_NOPE:P, :], core.buf(3)[A_NOPE:P, 0:ALL], ACT.Copy).then_inc(core.free.sem, 1)
            act.wait_ge(summed.sem, summed.at(2))
            nc.scalar.activation(rstd[:, 1, :], core.buf4(3)[:, 0:ALL], ACT.Sqrt, bias=core.eps[:, 0:1],
                                 scale=1.0 / KV_LORA).then_inc(root.sem, 1)
            act.wait_ge(qk_copied.sem, qk_copied.at(A_HEADS))
            for h in range(A_HEADS):
                act.wait_ge(qk_psum.sem, qk_psum.at(A_HEADS + h + 1))
                nc.scalar.activation(kt[0:A_NOPE, h, :], core.buf4(h)[0:A_NOPE, 0:ALL],
                                     ACT.Copy).then_inc(qk_copied.sem, 1)
            for t in range(TT):
                act.wait_ge(qk_psum.sem, qk_psum.at(2 * A_HEADS + t + 1))
                nc.scalar.activation(v[:, t, :], core.ps[:, 4 + t % 4, 0:A_HEADS * A_V],
                                     ACT.Copy).then_inc(qk_copied.sem, 1)

            def exponents(u):
                h, t, s0, s1 = units[u]
                act.wait_ge(peak.sem, peak.at(u + 1))
                if u >= 3:
                    act.wait_ge(turned.sem, turned.at(u - 2))
                nc.scalar.activation(probs[:, u % 3, 0:(s1 - s0) * P], core.buf(u)[:, 0:(s1 - s0) * P], ACT.Exp,
                                     bias=top[:, u:u + 1], accum_out=total[:, u:u + 1]).then_inc(expd.sem, 1)

            exponents(0)
            for u, (h, t, s0, s1) in enumerate(units):
                act.wait_ge(turned.sem, turned.at(u + 1))
                if u >= 2:
                    act.wait_ge(summed_v.sem, summed_v.at(u - 1))
                nc.scalar.activation(probs_t[:, u % 2, 0:(s1 - s0) * P],
                                     core.ps[:, 4:6, :].rearrange("p b n -> p (b n)")[:, 0:(s1 - s0) * P],
                                     ACT.Copy).then_inc(turned_in.sem, 1)
                if u + 1 < len(units):
                    exponents(u + 1)
            for t in range(qtiles):
                act.wait_ge(y_turned.sem, y_turned.at(t + 1))
                nc.scalar.activation(mix[:, 5:8, t * P:(t + 1) * P],
                                     core.ps[:, t % 2, 0:3 * P].rearrange("p (j n) -> p j n", j=3),
                                     ACT.Copy).then_inc(y_copied.sem, 1)

        @block.vector
        def _(dve):
            step = Steps(dve, steps)
            for j in range(LATENT_BLOCKS - 1):
                core.part_lo(dve, 0, j + SPLIT)
            dve.wait_ge(root.sem, root.at(1))
            step(nc.vector.reciprocal(rstd[:, 0, :], rstd[:, 0, :]))
            dve.wait_ge(core.free.sem, core.free.at(BUFS + 2))
            for j in range(2):
                last = nc.vector.scalar_tensor_tensor(cq[:, j, :], cq[:, j, :], core.param[:, gq + j:gq + j + 1],
                                                      rstd[:, 0, :], ALU.mult, ALU.mult)
                if j:
                    last.then_inc(normed.sem, 1)
                else:
                    step(last)
            core.part_lo(dve, 0, LATENT_BLOCKS - 1 + SPLIT)
            dve.wait_ge(root.sem, root.at(2))
            step(nc.vector.reciprocal(rstd[:, 1, :], rstd[:, 1, :]))
            nc.vector.scalar_tensor_tensor(ckv[:, 0, :], ckv[:, 0, :], core.param[:, gkv:gkv + 1],
                                           rstd[:, 1, :], ALU.mult, ALU.mult).then_inc(normed.sem, 1)
            dve.wait_ge(tables.sem, tables.at(48))
            dve.wait_ge(normed.sem, normed.at(2))
            for h in range(A_HEADS):
                dve.wait_ge(qk_psum.sem, qk_psum.at(h + 1))
                main, swap = core.buf4(2 * h), core.buf4(2 * h + 1)
                step(nc.vector.tensor_scalar(qt[0:A_QK, h, :], main[0:A_QK, 0:ALL], scale, None, ALU.mult))
                step(nc.vector.scalar_tensor_tensor(work[rot, 0, 0:LAT], swap[rot, 0:LAT], scale, sin[rot, :],
                                                    ALU.mult, ALU.mult))
                step(nc.vector.tensor_tensor(work[rot, 1, 0:LAT], qt[rot, h, 0:LAT], cos[rot, :], ALU.mult))
                nc.vector.tensor_tensor(qt[rot, h, 0:LAT], work[rot, 0, 0:LAT], work[rot, 1, 0:LAT],
                                        ALU.add).then_inc(qk_copied.sem, 1)
                dve.wait_ge(qk_copied.sem, qk_copied.at(h + 1))
            swapped = slice(A_QK, P)
            step(nc.vector.tensor_tensor(kt[rot, 0, 0:LAT], kr[rot, 0:LAT], cos[rot, :], ALU.mult))
            step(nc.vector.tensor_tensor(kt[rot, 1, 0:LAT], kr[swapped, 0:LAT], sin[swapped, :], ALU.mult))
            step(nc.vector.tensor_tensor(kr[rot, 0:LAT], kt[rot, 0, 0:LAT], kt[rot, 1, 0:LAT], ALU.add))
            for h in range(A_HEADS - 1):
                step(nc.vector.tensor_copy(kt[rot, h, :], kr[rot, :]))
            nc.vector.tensor_copy(kt[rot, A_HEADS - 1, :], kr[rot, :]).then_inc(rotated.sem, 1)

            def peak_of(u):
                h, t, s0, s1 = units[u]
                dve.wait_ge(scored.sem, scored.at(u + 1))
                nc.vector.tensor_reduce(top[:, u:u + 1], core.buf(u)[:, 0:(s1 - s0) * P], AX.X, ALU.max,
                                        negate=True).then_inc(peak.sem, 1)

            def finish(u):
                h, t, s0, s1 = units[u]
                dve.wait_ge(summed_v.sem, summed_v.at(u + 1))
                nc.vector.tensor_scalar(y[:, t, h * A_V:(h + 1) * A_V], core.ps[:, 6 + u % 2, 0:A_V],
                                        inv[:, u:u + 1], None, ALU.mult).then_inc(written.sem, 1)

            peak_of(0)
            for u in range(len(units)):
                h, t, s0, s1 = units[u]
                if u + 1 < len(units):
                    peak_of(u + 1)
                if u:
                    finish(u - 1)
                dve.wait_ge(expd.sem, expd.at(u + 1))
                step(nc.vector.reciprocal(inv[:, u:u + 1], total[:, u:u + 1]))
            finish(len(units) - 1)
            steps.close(step.n)
    core.close(LATENT_BLOCKS, 4)
    n = len(units)
    for s, k in ((tables, 48), (lora_in, 32), (rotated, 1), (squared, 3), (summed, 2), (root, 2), (normed, 2), (qk_psum, 2 * A_HEADS + TT),
                 (qk_copied, 2 * A_HEADS + TT), (scored, n), (peak, n), (expd, n), (turned, n), (turned_in, n),
                 (summed_v, n), (written, n), (y_turned, qtiles), (y_copied, qtiles)):
        s.close(k)


ORDER = (tuple(range(LT, TT)) + tuple(range(LT)), tuple(reversed(range(TT))))


class Mlstm:

    def __init__(self, arena, mix):
        a = self.alloc = Alloc(arena, KT * ALL)
        self.q, self.k = a(M_HEADS, ALL), a(M_HEADS, ALL)
        self.k_tok, self.v = a(TT, M_HEADS * M_DIM), a(TT, M_HEADS, M_DIM + 1)
        self.out_gate = a(TT, M_HEADS * M_DIM)
        self.rows_i, self.rows_f = a(1, ALL)[:, 0, :], a(1, ALL)[:, 0, :]
        self.gain_row = a(1, M_HEADS * M_DIM)[:, 0, :]
        self.decay_rows = a(ROWS, TT)[0:ROWS]
        self.state_m, self.last_m, self.dec = (a(1, TT)[0:ROWS, 0, :] for _ in range(3))
        self.conv = a(2, CONV_IN), a(2, CONV_IN - 4)
        self.b, self.peak, self.w_state = (mix[0:ROWS, k, :] for k in (2, 3, 4))
        rows = self.conv[1].rearrange("p a n -> p (a n)")
        self.floor, self.top = rows[0:ROWS, 0:ALL], rows[0:ROWS, ALL:2 * ALL]
        self.w_key = self.rows_f[0:ROWS, :]


def mlstm_inputs(core, arena, acts, l, m, acc):
    nc, dram = core.nc, core.dram
    conv_n = CONV_IN - 4
    raw, sig = m.conv
    flat = raw
    heads2 = 2 * M_HEADS
    mw = M_HEADS * M_DIM
    turns = 6
    copied = core.counter("conv_input_copied")
    taps = core.counter("conv_steps")
    gate = core.counter("conv_sigmoid")
    made = core.counter("conv_made")
    turned = core.counter("values_turned")
    turned_in = core.counter("values_copied")
    k_turned = core.counter("keys_turned")
    small = core.counter("mlstm_gain_in")
    ones_in = core.counter("mlstm_ones_in")
    rows_in = core.counter("gate_rows_in")
    act_chain, exponents = core.counter("gate_act_steps"), core.counter("gate_exponents")
    lf, ai = m.rows_f[0:ROWS, :], m.rows_i[0:ROWS, :]
    bias = P_BG + l * 2
    cv = P_CONV + l * heads2 * CONV
    outs = MLSTM_BLOCKS
    out_t = core.ps[:, 4:6, :].rearrange("p b n -> p (b n)")
    with nc.Block(no_gpsimd_drain=True) as block:
        @block.sync
        def _(sp):
            core.feed(sp, MLSTM_BLOCKS)

        @block.gpsimd
        def _(pool):
            pool.dma_start(m.gain_row, dram["g_mlstm"][l]).then_inc(small.sem, 16)
            pool.memset(m.v[:, :, :, M_DIM:M_DIM + 1], 1.0).then_inc(ones_in.sem, 1)

        @block.tensor
        def _(pe):
            def turn(n):
                pe.wait_ge(core.free.sem, core.free.at(BUFS + heads2 + n + 2))
                if n:
                    pe.wait_ge(turned_in.sem, turned_in.at(n))
                for t in range(TT):
                    last = nc.tensor.transpose(out_t[:, t * P:(t + 1) * P], flat[:, n % 2, t * P:(t + 1) * P],
                                               core.ident(P))
                last.then_inc(turned.sem, 1)

            for j in range(MLSTM_BLOCKS):
                w = core.arrived(pe, 0, j)
                pe.wait_ge(core.free.sem, core.free.at(j + 1))
                product_parts(nc, core.buf(j), w, KT, acts, ALL, M_DIM if j < heads2 else P).then_inc(core.done, 1)
                if j > heads2 + 1:
                    turn(j - heads2 - 2)
            turn(turns - 1)
            pe.wait_ge(turned_in.sem, turned_in.at(turns))
            pe.wait_ge(small.sem, small.at(16))
            pe.wait_ge(ones_in.sem, ones_in.at(1))
            for t in range(TT):
                if t >= 4:
                    pe.wait_ge(made.sem, made.at(heads2 + t - 3))
                for h in range(M_HEADS):
                    last = nc.tensor.transpose(core.ps[:, 4 + t % 4, h * M_DIM:(h + 1) * M_DIM],
                                               m.k[0:M_DIM, h, t * P:(t + 1) * P], core.ident(M_DIM))
                last.then_inc(k_turned.sem, 1)

        @block.scalar
        def _(act):
            for j in range(heads2):
                core.part_hi(act, 0, j + SPLIT)
                core.computed(act, 0, j)
                if j == 0:
                    act.wait_ge(taps.sem, taps.at(1))
                if j >= 2:
                    act.wait_ge(made.sem, made.at(j - 1))
                r = raw[0:M_DIM, j % 2, :]
                nc.scalar.activation(r[:, 2:2 + LAT], core.buf(j)[0:M_DIM, 0:LAT], ACT.Copy)
                nc.scalar.activation(r[:, LAT + 6:LAT + 6 + CTX], core.buf(j)[0:M_DIM, LAT:ALL],
                                     ACT.Copy).then_inc(core.free.sem, 1)
                if j >= 1:
                    act.wait_ge(copied.sem, copied.at(j))
                    nc.scalar.activation(sig[0:M_DIM, (j - 1) % 2, :], acc[0:M_DIM, (j - 1) % 2, :],
                                         ACT.Sigmoid).then_inc(gate.sem, 1)
            act.wait_ge(copied.sem, copied.at(heads2))
            nc.scalar.activation(sig[0:M_DIM, 1, :], acc[0:M_DIM, 1, :], ACT.Sigmoid).then_inc(gate.sem, 1)
            core.part_hi(act, 0, heads2 + SPLIT)
            core.computed(act, 0, heads2)
            last = core.buf(heads2)
            nc.scalar.activation(m.rows_i[0:ROWS, :], last[0:ROWS, 0:ALL], ACT.Identity,
                                 bias=core.param[0:ROWS, bias:bias + 1]).then_inc(rows_in.sem, 1)
            nc.scalar.activation(lf, last[F_ROW:F_ROW + ROWS, 0:ALL], ACT.Copy).then_inc(core.free.sem, 1)
            act.wait_ge(core.free.sem, core.free.at(BUFS + heads2 + 1))
            nc.scalar.activation(lf, lf, ACT.Identity, bias=core.param[0:ROWS, bias + 1:bias + 2]).then_inc(rows_in.sem, 1)
            act.wait_ge(rows_in.sem, rows_in.at(2))
            step = Steps(act, act_chain)
            act.wait_ge(made.sem, made.at(heads2))
            step(nc.scalar.activation(m.top, lf, ACT.Abs))
            step(nc.scalar.activation(m.top, m.top, ACT.Exp, scale=-1.0))
            step(nc.scalar.activation(m.top, m.top, ACT.Ln, bias=core.ones[0:ROWS, 0:1]))
            for n in range(turns):
                core.part_hi(act, 0, heads2 + 1 + n + SPLIT)
                core.computed(act, 0, heads2 + 1 + n)
                if n >= 2:
                    act.wait_ge(turned.sem, turned.at(n - 1))
                dst, src = flat[:, n % 2, 0:ALL], core.buf(heads2 + 1 + n)[:, 0:ALL]
                nc.scalar.activation(dst, src, ACT.Copy if n < 3 else ACT.Sigmoid).then_inc(core.free.sem, 1)
            act.wait_ge(exponents.sem, exponents.at(1))
            for ap, sign in ((m.dec, 1.0), (m.w_state, 1.0), (m.floor, -1.0), (m.w_key, 1.0)):
                step(nc.scalar.activation(ap, ap, ACT.Exp, scale=sign))

        @block.vector
        def _(dve):
            step = Steps(dve, taps)
            step(nc.vector.memset(raw, 0.0))

            def silu(j):
                dst = (m.q if j < M_HEADS else m.k)[0:M_DIM, j % M_HEADS, :]
                dve.wait_ge(gate.sem, gate.at(j + 1))
                for n, (t0, t1, c) in enumerate(((0, LAT, 0), (LAT, ALL, LAT + 4))):
                    s = slice(c, c + t1 - t0)
                    last = nc.vector.tensor_tensor(dst[:, t0:t1], acc[0:M_DIM, j % 2, s], sig[0:M_DIM, j % 2, s],
                                                   ALU.mult)
                last.then_inc(made.sem, 1)

            v = nc.vector
            tile = lambda ap, t: ap[:, t * P:(t + 1) * P]

            def run(d, dst, src, t, initial, op):
                rs = slice(ROW0[d], ROW0[d] + M_HEADS)
                o, s = tile(dst[rs, :], t), tile(src[rs, :], t)
                if d:
                    o, s = o[:, ::-1], s[:, ::-1]
                return v.tensor_tensor_scan(o, s, s, initial, op, op if op == ALU.max else ALU.bypass)

            def gates_begin():
                dve.wait_ge(made.sem, made.at(heads2))
                for ap in (m.b, m.peak, m.state_m, m.last_m):
                    step(v.memset(ap, 0.0))
                dve.wait_ge(act_chain.sem, act_chain.at(3))
                step(v.scalar_tensor_tensor(lf, lf, 0.0, m.top, ALU.min, ALU.subtract))
                for t in range(TT):
                    for d in range(2):
                        last = run(d, m.b, lf, t, 0.0, ALU.add)
                step(last)
                step(v.tensor_tensor(ai, ai, m.b, ALU.subtract))

            def gates_step(i):
                for d in range(2):
                    rs = slice(ROW0[d], ROW0[d] + M_HEADS)
                    t = ORDER[d][i]
                    last = run(d, m.peak, ai, t, m.state_m[rs, t:t + 1], ALU.max)
                step(last)
                for d in range(2):
                    t = ORDER[d][i]
                    rs = slice(ROW0[d], ROW0[d] + M_HEADS)
                    c = t * P + (P - 1 if d == 0 else 0)
                    last = v.tensor_copy(m.last_m[rs, t:t + 1], m.peak[rs, c:c + 1])
                    if i < TT - 1:
                        n = ORDER[d][i + 1]
                        last = v.tensor_tensor(m.state_m[rs, n:n + 1], m.b[rs, c:c + 1], m.peak[rs, c:c + 1], ALU.add)
                step(last)

            def gates_end():
                by_t = lambda ap: ap.rearrange("p (t n) -> p t n", t=TT)
                bc = lambda ap: ap[:, :, None].to_broadcast([ROWS, TT, P])
                v.tensor_tensor(m.dec, m.state_m, m.last_m, ALU.subtract)
                v.tensor_tensor(by_t(m.w_state), bc(m.state_m), by_t(m.peak), ALU.subtract)
                v.tensor_tensor(m.floor, m.b, m.peak, ALU.add)
                v.tensor_tensor(by_t(m.w_key), by_t(ai), bc(m.last_m), ALU.subtract)
                v.tensor_scalar(m.top, m.peak, -1.0, None, ALU.mult).then_inc(exponents.sem, 1)

            for j in range(heads2):
                core.part_lo(dve, 0, j + SPLIT)
                dve.wait_ge(core.free.sem, core.free.at(BUFS + j + 1))
                r, o = raw[0:M_DIM, j % 2, :], acc[0:M_DIM, j % 2, :]
                tap = lambda i: core.param[0:M_DIM, cv + j * CONV + i:cv + j * CONV + i + 1]
                if j >= 2:
                    dve.wait_ge(made.sem, made.at(j - 1))
                step(nc.vector.tensor_scalar(o, r[:, 0:conv_n], tap(0), None, ALU.mult))
                for i in range(1, CONV - 1):
                    step(nc.vector.scalar_tensor_tensor(o, r[:, i:i + conv_n], tap(i), o, ALU.mult, ALU.add))
                nc.vector.scalar_tensor_tensor(o, r[:, CONV - 1:CONV - 1 + conv_n], tap(CONV - 1), o, ALU.mult,
                                               ALU.add).then_inc(copied.sem, 1)
                if j >= 1:
                    silu(j - 1)
            core.part_lo(dve, 0, heads2 + SPLIT)
            silu(heads2 - 1)
            gates_begin()
            for n in range(turns):
                core.part_lo(dve, 0, heads2 + n + 1 + SPLIT)
                if n < TT // 2:
                    gates_step(2 * n)
                    gates_step(2 * n + 1)
                elif n == TT // 2:
                    gates_end()
                dve.wait_ge(turned.sem, turned.at(n + 1))
                by_t = out_t[:, 0:ALL].rearrange("p (t n) -> p t n", t=TT)
                if n >= 3:
                    c = (n - 3) * P
                    nc.vector.tensor_copy(m.out_gate[:, :, c:c + P], by_t).then_inc(turned_in.sem, 1)
                    continue
                f = n * P
                while f < (n + 1) * P:
                    h, d = divmod(f, M_DIM)
                    e = min((h + 1) * M_DIM, (n + 1) * P)
                    last = nc.vector.tensor_copy(m.v[:, :, h, d:d + e - f], by_t[:, :, f - n * P:e - n * P])
                    f = e
                last.then_inc(turned_in.sem, 1)
            for t in range(TT):
                dve.wait_ge(k_turned.sem, k_turned.at(t + 1))
                nc.vector.tensor_copy(m.k_tok[:, t, :], core.ps[:, 4 + t % 4, 0:mw]).then_inc(made.sem, 1)
            dve.wait_ge(act_chain.sem, act_chain.at(7))
            step(v.tensor_scalar(m.w_state, m.w_state, float(M_DIM) ** -0.5, None, ALU.mult))
            step(v.tensor_tensor(m.decay_rows, core.const[0:ROWS, C_IDENT:C_IDENT + ROWS][:, :, None].to_broadcast(
                [ROWS, ROWS, TT]), m.dec[:, None, :].to_broadcast([ROWS, ROWS, TT]), ALU.mult))
            taps.close(step.n)
    core.close(MLSTM_BLOCKS, outs)
    small.close(16)
    ones_in.close(1)
    rows_in.close(2)
    act_chain.close(7)
    exponents.close(1)
    copied.close(heads2)
    gate.close(heads2)
    made.close(heads2 + TT)
    turned.close(turns)
    turned_in.close(turns)
    k_turned.close(TT)


def mlstm(core, arena, scratch, m, mix, ctx_out):
    nc, dram = core.nc, core.dram
    hflat = scratch
    hid = M_HEADS * M_DIM
    out = hflat[:, 0:TT * hid].rearrange("p (t n) -> p t n", t=TT)
    select = hflat[:, 2304:2304 + 8 * P].rearrange("p (r n) -> p r n", r=8)
    per_token = hflat[:, 3328:3328 + 24 * ROWS].rearrange("p (n r) -> p n r", r=ROWS)
    decay = hflat[:, 4192:4192 + ROWS * TT].rearrange("p (r t) -> p r t", t=TT)
    a = Alloc(scratch, 4192 + ROWS * TT)
    weight, score = a(2, M_HEADS * P), a(2, M_HEADS * P)
    keyed = a(2, hid)
    part, both = a(1, M_HEADS * (M_DIM + 1)), a(2, M_HEADS * (M_DIM + 1))
    state = a(2, M_HEADS * (M_DIM + 1))
    den, ms = a(2, M_HEADS), a(1, TT * M_HEADS)[:, 0, :]
    sq = a(1, hid)[:, 0, :]
    ai = m.rows_i[0:ROWS, :]
    tile = lambda ap, t: ap[:, t * P:(t + 1) * P]
    scale = float(M_DIM) ** -0.5
    nt = TT if ctx_out else LT

    steps_all = [(d, i, ORDER[d][i]) for i in range(TT) for d in range(2)]
    outs = [u for u, (d, i, t) in enumerate(steps_all) if t < nt]
    upds = [u for u, (d, i, t) in enumerate(steps_all) if i < TT - 1]
    done_at = lambda t: max(u for u in outs if steps_all[u][2] == t)
    tiles_done = sorted(range(nt), key=done_at)
    n_out = lambda u: sum(v < u for v in outs)
    n_upd = lambda u: sum(v < u for v in upds)

    chain = core.counter("mlstm_steps")
    mean_sq, root, normed = core.counter("mean_squares"), core.counter("head_norm_roots"), core.counter("output_normed")
    gated = core.counter("gates_with_gain")
    turned = core.counter("gate_rows_turned")
    select_in = core.counter("select_in")
    weights_p = core.counter("weight_exponents")
    scores_p = core.counter("mlstm_scores")
    w_exp = core.counter("weights_ready")
    scored = core.counter("weighted_scores")
    summed = core.counter("mlstm_sums")
    keys = core.counter("weighted_keys")
    grown = core.counter("state_products")
    passed = core.counter("state_ready")
    written = core.counter("mlstm_written")
    token_rows = core.counter("token_rows_copied")
    y_turned = core.counter("y_turned")

    with nc.Block(no_gpsimd_drain=True) as block:
        @block.gpsimd
        def _(pool):
            pool.dma_start(select[0:ROWS, :, :], dram["select"]).then_inc(select_in.sem, 16)
            nc.gpsimd.tensor_tensor(m.out_gate[:, 0:nt, :], m.out_gate[:, 0:nt, :], m.gain_row[:, None, :].to_broadcast(
                [P, nt, hid]), ALU.mult).then_inc(gated.sem, 1)
            pool.wait_ge(gated.sem, gated.at(1))
            pool.wait_ge(token_rows.sem, token_rows.at(2))
            for u in upds:
                d, i, t = steps_all[u]
                n = n_upd(u)
                if n >= 2:
                    pool.wait_ge(grown.sem, grown.at(n - 1))
                wk = per_token[:, 3 * TT + t, ROW0[d]:ROW0[d] + M_HEADS]
                nc.gpsimd.tensor_tensor(keyed[:, n % 2, :].rearrange("p (h d) -> p h d", h=M_HEADS),
                                        m.k_tok[:, t, :].rearrange("p (h d) -> p h d", h=M_HEADS),
                                        wk[:, :, None].to_broadcast([P, M_HEADS, M_DIM]),
                                        ALU.mult).then_inc(keys.sem, 1)

        @block.tensor
        def _(pe):
            for q, rows in enumerate((ai, m.w_state, m.floor, m.w_key)):
                for t in range(TT):
                    n = q * TT + t
                    last = nc.tensor.transpose(core.ps[:, 4 + n // 12, n % 12 * ROWS:(n % 12 + 1) * ROWS],
                                               tile(rows, t), core.ident(ROWS))
            last = nc.tensor.matmul(core.ps[:, 6, 0:ROWS * TT], core.ones[0:ROWS, :],
                                    m.decay_rows.rearrange("p r t -> p (r t)"), start=True, stop=True)
            last.then_inc(turned.sem, 1)
            pe.wait_ge(select_in.sem, select_in.at(16))

            def weigh(u):
                d, i, t = steps_all[u]
                n = n_out(u)
                if n >= 2:
                    pe.wait_ge(w_exp.sem, w_exp.at(n - 1))
                mask = core.const[:, C_UPPER:C_UPPER + P] if d == 0 else core.const[:, C_LOWER:C_LOWER + P]
                nc.tensor.matmul(core.ps[:, n % 2, :], core.ident(P), mask[:, None, :].to_broadcast([P, M_HEADS, P]),
                                 start=True, stop=False)
                for h in range(M_HEADS):
                    last = nc.tensor.matmul(core.ps[:, n % 2, h * P:(h + 1) * P], select[0:ROWS, d * M_HEADS + h, :],
                                            tile(m.top, t), start=False, stop=h == M_HEADS - 1)
                last.then_inc(weights_p.sem, 1)
                if n >= 2:
                    pe.wait_ge(scored.sem, scored.at(n - 1))
                for h in range(M_HEADS):
                    last = nc.tensor.matmul(core.ps[:, 2 + n % 2, h * P:(h + 1) * P], tile(m.k[0:M_DIM, h, :], t),
                                            tile(m.q[0:M_DIM, h, :], t), start=True, stop=True)
                last.then_inc(scores_p.sem, 1)

            def sums(u):
                d, i, t = steps_all[u]
                n = n_out(u)
                pe.wait_ge(scored.sem, scored.at(n + 1))
                if n >= 1:
                    pe.wait_ge(written.sem, written.at(n))
                for h in range(M_HEADS):
                    c = slice(h * (M_DIM + 1), (h + 1) * (M_DIM + 1))
                    last = nc.tensor.matmul(core.ps[:, 4 + n % 2, c], score[:, n % 2, h * P:(h + 1) * P],
                                            m.v[:, t, h, :], start=True, stop=True)
                if i:
                    pe.wait_ge(passed.sem, passed.at(n_upd(2 * (i - 1) + d) + 1))
                    for h in range(M_HEADS):
                        c = slice(h * (M_DIM + 1), (h + 1) * (M_DIM + 1))
                        last = nc.tensor.matmul(core.ps[:, 6, c], tile(m.q[0:M_DIM, h, :], t), state[0:M_DIM, d, c],
                                                start=True, stop=True)
                last.then_inc(summed.sem, 1)

            def grow(u):
                d, i, t = steps_all[u]
                n = n_upd(u)
                pe.wait_ge(keys.sem, keys.at(n + 1))
                if n >= 1:
                    pe.wait_ge(passed.sem, passed.at(n))
                for h in range(M_HEADS):
                    last = nc.tensor.matmul(core.ps[0:M_DIM, 7, h * (M_DIM + 1):(h + 1) * (M_DIM + 1)],
                                            keyed[:, n % 2, h * M_DIM:(h + 1) * M_DIM], m.v[:, t, h, :],
                                            start=True, stop=True)
                last.then_inc(grown.sem, 1)

            pe.wait_ge(token_rows.sem, token_rows.at(3))
            weigh(outs[0])
            for u in range(len(steps_all)):
                n = n_out(u)
                if u in outs and n + 1 < len(outs):
                    weigh(outs[n + 1])
                if u in outs:
                    sums(u)
                if u in upds:
                    grow(u)
            for n, t in enumerate(tiles_done):
                pe.wait_ge(normed.sem, normed.at(n + 1))
                for j in range(3):
                    last = nc.tensor.transpose(core.ps[:, t, j * P:(j + 1) * P], out[:, t, j * P:(j + 1) * P],
                                               core.ident(P))
                last.then_inc(y_turned.sem, 1)

        @block.scalar
        def _(act):
            for u in outs:
                d, i, t = steps_all[u]
                n = n_out(u)
                if n == 0:
                    act.wait_ge(token_rows.sem, token_rows.at(2))
                act.wait_ge(weights_p.sem, weights_p.at(n + 1))
                if n >= 2:
                    act.wait_ge(scored.sem, scored.at(n - 1))
                for h in range(M_HEADS):
                    last = nc.scalar.activation(weight[:, n % 2, h * P:(h + 1) * P],
                                                core.ps[:, n % 2, h * P:(h + 1) * P], ACT.Exp,
                                                bias=per_token[:, t, ROW0[d] + h:ROW0[d] + h + 1])
                last.then_inc(w_exp.sem, 1)
            for n, t in enumerate(tiles_done):
                act.wait_ge(mean_sq.sem, mean_sq.at(n + 1))
                g = ms[:, t * M_HEADS:(t + 1) * M_HEADS]
                nc.scalar.activation(g, g, ACT.Sqrt, bias=core.eps[:, 0:1], scale=1.0 / M_DIM).then_inc(root.sem, 1)
            for n, t in enumerate(tiles_done):
                act.wait_ge(y_turned.sem, y_turned.at(n + 1))
                nc.scalar.activation(mix[:, 2:5, t * P:(t + 1) * P],
                                     core.ps[:, t, 0:3 * P].rearrange("p (j n) -> p j n", j=3), ACT.Copy)

        @block.vector
        def _(dve):
            step = Steps(dve, chain)
            v = nc.vector
            dve.wait_ge(turned.sem, turned.at(1))
            for n in range(2):
                v.tensor_copy(per_token[:, 12 * n:12 * (n + 1), :].rearrange("p n r -> p (n r)"),
                              core.ps[:, 4 + n, 0:12 * ROWS]).then_inc(token_rows.sem, 1)
            v.tensor_copy(decay.rearrange("p r t -> p (r t)"), core.ps[:, 6, 0:ROWS * TT]).then_inc(token_rows.sem, 1)
            dve.wait_ge(token_rows.sem, token_rows.at(3))
            heads = lambda ap: ap.rearrange("p (h d) -> p h d", h=M_HEADS)

            def scored_step(u):
                n = n_out(u)
                dve.wait_ge(w_exp.sem, w_exp.at(n + 1))
                dve.wait_ge(scores_p.sem, scores_p.at(n + 1))
                if n >= 2:
                    dve.wait_ge(summed.sem, summed.at(n - 1))
                v.scalar_tensor_tensor(score[:, n % 2, :], core.ps[:, 2 + n % 2, :], scale, weight[:, n % 2, :],
                                       ALU.mult, ALU.mult).then_inc(scored.sem, 1)

            def combine(u):
                d, i, t = steps_all[u]
                n = n_out(u)
                r = slice(ROW0[d], ROW0[d] + M_HEADS)
                nd, pt, dn = both[:, n % 2, :], part[:, 0, :], den[:, n % 2, :]
                w1 = M_HEADS * (M_DIM + 1)
                dve.wait_ge(summed.sem, summed.at(n + 1))
                if i:
                    step(v.tensor_tensor(heads(pt), heads(core.ps[:, 6, 0:w1]), per_token[:, TT + t, r][:, :, None]
                                         .to_broadcast([P, M_HEADS, M_DIM + 1]), ALU.mult))
                    step(v.tensor_tensor(nd, core.ps[:, 4 + n % 2, 0:w1], pt, ALU.add))
                else:
                    step(v.tensor_copy(nd, core.ps[:, 4 + n % 2, 0:w1]))
                q = heads(nd)[:, :, M_DIM]
                step(v.scalar_tensor_tensor(dn, q, -1.0, q, ALU.mult, ALU.max))
                step(v.tensor_tensor(dn, dn, per_token[:, 2 * TT + t, r], ALU.max))
                step(v.reciprocal(dn, dn))
                rb = dn[:, :, None].to_broadcast([P, M_HEADS, M_DIM])
                o = heads(out[:, t, :])
                if t not in seen:
                    seen.add(t)
                    v.tensor_tensor(o, heads(nd)[:, :, 0:M_DIM], rb, ALU.mult).then_inc(written.sem, 1)
                else:
                    step(v.tensor_tensor(heads(nd)[:, :, 0:M_DIM], heads(nd)[:, :, 0:M_DIM], rb, ALU.mult))
                    v.tensor_tensor(o, o, heads(nd)[:, :, 0:M_DIM], ALU.add).then_inc(written.sem, 1)

            def pass_on(u):
                d, i, t = steps_all[u]
                n = n_upd(u)
                st, w1 = state[0:M_DIM, d, :], M_HEADS * (M_DIM + 1)
                dve.wait_ge(grown.sem, grown.at(n + 1))
                if i == 0:
                    v.tensor_copy(st, core.ps[0:M_DIM, 7, 0:w1]).then_inc(passed.sem, 1)
                else:
                    dc = decay[0:M_DIM, ROW0[d]:ROW0[d] + M_HEADS, t]
                    dve.wait_ge(passed.sem, passed.at(n))
                    step(v.tensor_tensor(heads(st), heads(st), dc[:, :, None].to_broadcast(
                        [M_DIM, M_HEADS, M_DIM + 1]), ALU.mult))
                    v.tensor_tensor(st, st, core.ps[0:M_DIM, 7, 0:w1], ALU.add).then_inc(passed.sem, 1)

            def moments(n, t):
                if n:
                    dve.wait_ge(mean_sq.sem, mean_sq.at(n))
                dve.wait_ge(written.sem, written.at(n_out(done_at(t)) + 1))
                step(v.tensor_tensor(sq, out[:, t, :], out[:, t, :], ALU.mult))
                v.tensor_reduce(ms[:, t * M_HEADS:(t + 1) * M_HEADS], heads(sq), AX.X, ALU.add).then_inc(mean_sq.sem, 1)

            seen = set()
            scored_step(outs[0])
            for u in range(len(steps_all)):
                n = n_out(u)
                if u in outs and n + 1 < len(outs):
                    scored_step(outs[n + 1])
                if u in outs:
                    combine(u)
                if u in upds:
                    pass_on(u)
                for n, t in enumerate(tiles_done):
                    if done_at(t) == u:
                        moments(n, t)
            dve.wait_ge(gated.sem, gated.at(1))
            for n, t in enumerate(tiles_done):
                g, o = ms[:, t * M_HEADS:(t + 1) * M_HEADS], out[:, t, :]
                dve.wait_ge(root.sem, root.at(n + 1))
                step(v.reciprocal(g, g))
                step(v.tensor_tensor(heads(o), heads(o), g[:, :, None].to_broadcast([P, M_HEADS, M_DIM]), ALU.mult))
                v.tensor_tensor(o, o, m.out_gate[:, t, :], ALU.mult).then_inc(normed.sem, 1)
            chain.close(step.n)
    no, nu = len(outs), len(upds)
    for s, k in ((mean_sq, nt), (root, nt), (normed, nt), (gated, 1), (turned, 1), (select_in, 16), (weights_p, no),
                 (scores_p, no), (w_exp, no), (scored, no), (summed, no), (keys, nu), (grown, nu), (passed, nu),
                 (written, no), (token_rows, 3), (y_turned, nt)):
        s.close(k)


TOKEN_TILES = [(t * P, P) for t in range(LT)] + [(LAT, META)]


def turn_tokens(core, src, out):
    for t, (c, n) in enumerate(TOKEN_TILES):
        last = core.nc.tensor.transpose(out[0:n, t * P:(t + 1) * P], src[:, c:c + n], core.ident(P))
    return last


def token_major_copies(eng_op, out, dst):
    eng_op(dst[:, 0:LT, :], out[:, 0:LT * P].rearrange("p (t n) -> p t n", t=LT))
    return eng_op(dst[0:META, LT, :], out[0:META, LT * P:(LT + 1) * P])


def forgetting_attention(core, arena, acts, norm, l, y):
    nc = core.nc
    a = Alloc(arena, (LT + 1) * D)
    norm.tmp = a(2, SEQ2)
    flat = a(2, SEQ2)
    q, k, v = a(FOX_HEADS, SEQ2), a(FOX_HEADS, SEQ2), a(LT + 1, FOX_HEADS * FOX_DIM)
    lf, c_row, tmp = (a(1, SEQ2)[0:FOX_HEADS, 0, :] for _ in range(3))
    real_keys = lambda t: (t + 1) * P if t < LT else 0
    units = []
    for t in range(LT + 1):
        size = 2 if real_keys(t) + META <= 512 else 1
        units += [(tuple(range(h, h + size)), t) for h in range(0, FOX_HEADS, size)]
    n_units = len(units)
    rows = lambda u: TOKEN_TILES[units[u][1]][1]
    real = lambda u: real_keys(units[u][1])
    heads_of = lambda u: enumerate(units[u][0])
    meta_at = lambda u, e: e * 512 + (512 - P) if len(units[u][0]) == 2 else LAT
    probs, probs_t = a(3, 2 * (512 - P + META)), a(2, 2 * 512)
    top, total, inv = (a(1, (LT + 1) * FOX_HEADS)[:, 0, :] for _ in range(3))
    column = lambda u: sum(len(hs) for hs, _ in units[:u])
    columns = lambda ap, u: ap[0:rows(u), column(u):column(u) + len(units[u][0])]

    chain = core.counter("fox_steps")
    act_chain = core.counter("fox_act_steps")
    c_in = core.counter("c_in_keys")
    ones_in = core.counter("fox_ones_in")
    scored = core.counter("scores_ready")
    peak = core.counter("row_max_ready")
    expd = core.counter("probs_ready")
    turned = core.counter("probs_turned")
    turned_in = core.counter("turned_probs_copied")
    summed_v = core.counter("attention_ready")
    written = core.counter("attention_written")
    summed_c = core.counter("c_ready")
    v_turned = core.counter("values_turned")
    v_copied = core.counter("values_copied")
    out_t = core.ps[:, 4:6, :].rearrange("p b n -> p (b n)")

    with nc.Block(no_gpsimd_drain=True) as block:
        @block.sync
        def _(sp):
            core.feed(sp, FOX_BLOCKS)
            sp.wait_ge(summed_c.sem, summed_c.at(1))
            for h in range(FOX_HEADS):
                sp.dma_start(k[FOX_DIM:FOX_DIM + 1, h, :], c_row[h:h + 1, :]).then_inc(c_in.sem, 16)

        @block.gpsimd
        def _(pool):
            pool.wait_ge(core.added.sem, core.added.at(0))
            pool.memset(q[FOX_DIM:FOX_DIM + 1, :, :], 1.0).then_inc(ones_in.sem, 1)

        @block.tensor
        def _(pe):
            norm.on_pe(pe)

            def turn_values(n):
                pe.wait_ge(core.free.sem, core.free.at(BUFS + FOX_HEADS + 2 + n))
                if n:
                    pe.wait_ge(v_copied.sem, v_copied.at(n))
                turn_tokens(core, flat[:, n % 2, :], out_t).then_inc(v_turned.sem, 1)

            free = lambda j: pe.wait_ge(core.free.sem, core.free.at(j + 1))
            product_pair(core, pe, 0, 0, UNROLL, KT, acts, SEQ2, free, norm.wait_tile(pe))
            for j in range(2, FOX_BLOCKS):
                w = core.arrived(pe, 0, j)
                free(j)
                product_parts(nc, core.buf(j), w, KT, acts, SEQ2).then_inc(core.done, 1)
                if j > FOX_HEADS + 1:
                    turn_values(j - FOX_HEADS - 2)
            turn_values(3)
            pe.wait_ge(v_copied.sem, v_copied.at(4))
            pe.wait_ge(core.free.sem, core.free.at(BUFS + FOX_BLOCKS))
            pe.wait_ge(c_in.sem, c_in.at(16 * FOX_HEADS))
            pe.wait_ge(ones_in.sem, ones_in.at(1))

            def scores(u):
                c, n = TOKEN_TILES[units[u][1]]
                if u >= 2:
                    pe.wait_ge(expd.sem, expd.at(u - 1))
                r = real(u)
                mask = core.const[:, C_LOWER:C_LOWER + P]
                for e, h in heads_of(u):
                    out, qs = core.buf(u)[:, e * 512:], q[0:FOX_DIM + 1, h, c:c + n]
                    if r:
                        nc.tensor.matmul(out[:, 0:r], qs, k[0:FOX_DIM + 1, h, 0:r], start=True, stop=False)
                        nc.tensor.matmul(out[:, r - P:r], core.ident(P), mask, start=False, stop=True)
                    last = nc.tensor.matmul(out[0:n, r:r + META], qs, k[0:FOX_DIM + 1, h, LAT:SEQ2], start=True,
                                            stop=r > 0)
                    if not r:
                        last = nc.tensor.matmul(out[0:n, 0:META], core.ident(META), mask[0:META, 0:META], start=False,
                                                stop=True)
                last.then_inc(scored.sem, 1)

            def turn(u):
                n, r = rows(u), real(u)
                pe.wait_ge(expd.sem, expd.at(u + 1))
                if u >= 1:
                    pe.wait_ge(turned_in.sem, turned_in.at(u))
                for e, _ in heads_of(u):
                    p0 = e * (r + META)
                    for s in range(r // P):
                        nc.tensor.transpose(out_t[:, e * 512 + s * P:e * 512 + (s + 1) * P],
                                            probs[:, u % 3, p0 + s * P:p0 + (s + 1) * P], core.ident(P))
                    m = meta_at(u, e)
                    last = nc.tensor.transpose(out_t[0:META, m:m + n], probs[0:n, u % 3, p0 + r:p0 + r + META],
                                               core.ident(n))
                last.then_inc(turned.sem, 1)

            def weigh(u):
                n, r = rows(u), real(u)
                pe.wait_ge(turned_in.sem, turned_in.at(u + 1))
                if u >= 2:
                    pe.wait_ge(written.sem, written.at(u - 1))
                for e, h in heads_of(u):
                    out = core.ps[0:n, 6 + u % 2, e * FOX_DIM:(e + 1) * FOX_DIM]
                    hc = slice(h * FOX_DIM, (h + 1) * FOX_DIM)
                    for s in range(r // P):
                        nc.tensor.matmul(out, probs_t[:, u % 2, e * 512 + s * P:e * 512 + (s + 1) * P], v[:, s, hc],
                                         start=s == 0, stop=False)
                    m = meta_at(u, e)
                    last = nc.tensor.matmul(out, probs_t[0:META, u % 2, m:m + n], v[0:META, LT, hc], start=r == 0,
                                            stop=True)
                last.then_inc(summed_v.sem, 1)

            scores(0)
            for u in range(n_units):
                if u + 1 < n_units:
                    scores(u + 1)
                if u:
                    weigh(u - 1)
                turn(u)
            weigh(n_units - 1)

        @block.scalar
        def _(act):
            norm.on_act(act)
            step = Steps(act, act_chain)
            core.part_hi(act, 0, SPLIT)
            core.computed(act, 0, 0)
            bias = core.param[0:FOX_HEADS, P_BF + l:P_BF + l + 1]
            g = core.buf(0)[0:FOX_HEADS, :]
            step(nc.scalar.activation(like_psum(lf, SEQ2), in_psum(g, SEQ2), ACT.Identity, bias=bias))
            nc.scalar.activation(like_psum(tmp, SEQ2), in_psum(g, SEQ2), ACT.Abs, bias=bias).then_inc(core.free.sem, 1)
            act.wait_ge(core.free.sem, core.free.at(BUFS + 1))
            step(nc.scalar.activation(tmp, tmp, ACT.Exp, scale=-1.0))
            step(nc.scalar.activation(tmp, tmp, ACT.Ln, bias=core.ones[0:FOX_HEADS, 0:1]))
            for j in range(1, FOX_HEADS + 1):
                core.part_hi(act, 0, j + SPLIT)
                core.computed(act, 0, j)
                dst, h = (q, 2 * (j - 1)) if j <= FOX_HEADS // 2 else (k, 2 * (j - 1) - FOX_HEADS)
                s = float(FOX_DIM) ** -0.5 if j <= FOX_HEADS // 2 else 1.0
                for e in range(2):
                    last = nc.scalar.activation(like_psum(dst[0:FOX_DIM, h + e, :], SEQ2),
                                                in_psum(core.buf(j)[e * FOX_DIM:(e + 1) * FOX_DIM, :], SEQ2), ACT.Copy,
                                                scale=s)
                last.then_inc(core.free.sem, 1)
            for j in range(4):
                core.part_hi(act, 0, FOX_HEADS + 1 + j + SPLIT)
                core.computed(act, 0, FOX_HEADS + 1 + j)
                if j >= 2:
                    act.wait_ge(v_turned.sem, v_turned.at(j - 1))
                nc.scalar.activation(like_psum(flat[:, j % 2, :], SEQ2), in_psum(core.buf(FOX_HEADS + 1 + j), SEQ2),
                                     ACT.Copy).then_inc(core.free.sem, 1)

            def exponents(u):
                n, w = rows(u), real(u) + META
                act.wait_ge(peak.sem, peak.at(u + 1))
                if u >= 3:
                    act.wait_ge(turned.sem, turned.at(u - 2))
                for e, _ in heads_of(u):
                    c = column(u) + e
                    last = nc.scalar.activation(probs[0:n, u % 3, e * w:(e + 1) * w],
                                                core.buf(u)[0:n, e * 512:e * 512 + w], ACT.Exp,
                                                bias=top[0:n, c:c + 1], accum_out=total[0:n, c:c + 1])
                last.then_inc(expd.sem, 1)

            exponents(0)
            for u in range(n_units):
                n, r = rows(u), real(u)
                act.wait_ge(turned.sem, turned.at(u + 1))
                if u >= 2:
                    act.wait_ge(summed_v.sem, summed_v.at(u - 1))
                size, m = len(units[u][0]), meta_at(u, 0)
                by_head = lambda ap: ap.rearrange("p (e n) -> p e n", e=2)
                if size == 1:
                    nc.scalar.activation(probs_t[:, u % 2, 0:r], out_t[:, 0:r], ACT.Copy)
                    last = nc.scalar.activation(probs_t[0:META, u % 2, m:m + n], out_t[0:META, m:m + n], ACT.Copy)
                else:
                    if r:
                        nc.scalar.activation(by_head(probs_t[:, u % 2, :])[:, :, 0:r], by_head(out_t)[:, :, 0:r],
                                             ACT.Copy)
                    last = nc.scalar.activation(by_head(probs_t[0:META, u % 2, :])[:, :, m:m + n],
                                                by_head(out_t[0:META, :])[:, :, m:m + n], ACT.Copy)
                last.then_inc(turned_in.sem, 1)
                if u + 1 < n_units:
                    exponents(u + 1)

        @block.vector
        def _(dve):
            norm.on_dve(dve, norm.tmp)
            core.part_lo(dve, 0, SPLIT)
            core.part_lo(dve, 0, SPLIT + 1)
            step = Steps(dve, chain)
            dve.wait_ge(act_chain.sem, act_chain.at(3))
            step(nc.vector.scalar_tensor_tensor(lf, lf, 0.0, tmp, ALU.min, ALU.subtract))
            meta, reals = slice(LAT, SEQ2), slice(0, LAT)
            step(nc.vector.tensor_tensor_scan(tmp[:, meta], lf[:, meta], lf[:, meta], 0.0, ALU.add, ALU.bypass))
            step(nc.vector.tensor_tensor_scan(tmp[:, reals], lf[:, reals], lf[:, reals], tmp[:, SEQ2 - 1:SEQ2], ALU.add,
                                              ALU.bypass))
            nc.vector.tensor_scalar(c_row, tmp, -1.0, None, ALU.mult).then_inc(summed_c.sem, 1)
            for j in range(2, FOX_BLOCKS):
                core.part_lo(dve, 0, j + SPLIT)
                if j > FOX_HEADS + 1:
                    n = j - FOX_HEADS - 2
                    dve.wait_ge(v_turned.sem, v_turned.at(n + 1))
                    token_major_copies(nc.vector.tensor_copy, out_t,
                                       v[:, :, n * P:(n + 1) * P]).then_inc(v_copied.sem, 1)
            dve.wait_ge(v_turned.sem, v_turned.at(4))
            token_major_copies(nc.vector.tensor_copy, out_t, v[:, :, 3 * P:4 * P]).then_inc(v_copied.sem, 1)

            def peak_of(u):
                n, w = rows(u), real(u) + META
                dve.wait_ge(scored.sem, scored.at(u + 1))
                src = core.buf(u)[0:n, 0:w]
                if len(units[u][0]) == 2:
                    src = core.buf(u)[0:n, :].rearrange("p (e n) -> p e n", e=2)[:, :, 0:w]
                nc.vector.tensor_reduce(columns(top, u), src, AX.X, ALU.max, negate=True).then_inc(peak.sem, 1)

            def finish(u):
                n, t, c = rows(u), units[u][1], column(u)
                dve.wait_ge(summed_v.sem, summed_v.at(u + 1))
                for e, h in heads_of(u):
                    last = nc.vector.tensor_scalar(y[0:n, t, h * FOX_DIM:(h + 1) * FOX_DIM],
                                                   core.ps[0:n, 6 + u % 2, e * FOX_DIM:(e + 1) * FOX_DIM],
                                                   inv[0:n, c + e:c + e + 1], None, ALU.mult)
                last.then_inc(written.sem, 1)

            peak_of(0)
            for u in range(n_units):
                if u + 1 < n_units:
                    peak_of(u + 1)
                if u:
                    finish(u - 1)
                dve.wait_ge(expd.sem, expd.at(u + 1))
                step(nc.vector.reciprocal(columns(inv, u), columns(total, u)))
            finish(n_units - 1)
            chain.close(step.n)
    core.close(FOX_BLOCKS, FOX_BLOCKS)
    norm.close()
    v_turned.close(4)
    v_copied.close(4)
    act_chain.close(3)
    for s in (scored, peak, expd, turned, turned_in, summed_v, written):
        s.close(n_units)
    c_in.close(16 * FOX_HEADS)
    ones_in.close(1)
    summed_c.close(1)


def retention(core, arena, acts, l, y, h_hi, h_lo):
    nc, dram = core.nc, core.dram
    a = Alloc(arena, (LT + 1) * D)
    qk = a(2 * RET_HEADS, SEQ2)
    cos, sin = a(1, SEQ2)[:, 0, :], a(1, SEQ2)[:, 0, :]
    decay = a(RET_HEADS, SEQ2)
    v, gate = a(LT + 1, RET_HEADS * RET_DIM), a(LT + 1, RET_HEADS * RET_DIM)
    work = a(2, SEQ2)
    score = a(LT + 1, SEQ2)
    gain = a(1, RET_HEADS * RET_DIM)[:, 0, :]
    mean, var = a(RET_HEADS, LT + 1), a(RET_HEADS, LT + 1)
    gate_sig = a(LT + 1, RET_HEADS * RET_DIM)
    sq_buf = work.rearrange("p a b -> p (a b)")[:, 0:(LT + 1) * RET_DIM].rearrange("p (t n) -> p t n", t=LT + 1)
    half = RET_DIM // 2
    scale = float(RET_DIM) ** -0.5
    outs = RET_BLOCKS
    fox = FOX_HEADS * FOX_DIM
    width = RET_HEADS * RET_DIM

    tables = core.counter("tables_in")
    chain = core.counter("ret_steps")
    rotated = core.counter("ret_rotated")
    gate_in = core.counter("ret_gate_in")
    scores_p = core.counter("ret_scores")
    scored = core.counter("ret_weighted")
    summed = core.counter("ret_sums")
    copied = core.counter("ret_copied")
    moment = core.counter("ret_variance")
    root = core.counter("ret_root")
    ready = core.counter("ret_ready")
    y_turned = core.counter("y_turned")
    y_copied = core.counter("y_copied")
    tail = core.counter("ret_tail_cleared")
    turned = core.counter("values_turned")
    t_copied = core.counter("values_copied")
    hi_done = core.counter("y_hi_ready")
    out_t = core.ps[:, 4:6, :].rearrange("p b n -> p (b n)")
    flat = score[:, 0:2, :]

    pairs = [(LT, 0, LAT, META), (LT, LAT, META, 0)] + [(s, s * P, LAT - s * P, 0) for s in range(LT)]

    with nc.Block(no_gpsimd_drain=True) as block:
        @block.sync
        def _(sp):
            core.feed(sp, RET_BLOCKS)

        @block.gpsimd
        def _(pool):
            pool.dma_start(cos, dram["ret_cos"]).then_inc(tables.sem, 16)
            pool.dma_start(sin, dram["ret_sin"]).then_inc(tables.sem, 16)
            pool.dma_start(decay, dram["ret_decay"]).then_inc(tables.sem, 16)
            pool.dma_start(gain, dram["ret_gn"][l]).then_inc(tables.sem, 16)
            pool.memset(y[:, LT, fox:D], 0.0).then_inc(tail.sem, 1)
            pool.memset(gate[:, LT, :], 0.0).then_inc(tail.sem, 1)

        @block.tensor
        def _(pe):
            two = 2 * RET_HEADS

            def turn_block(n):
                pe.wait_ge(core.free.sem, core.free.at(BUFS + two + n + 1))
                if n:
                    pe.wait_ge(t_copied.sem, t_copied.at(n))
                turn_tokens(core, flat[:, n % 2, :], out_t).then_inc(turned.sem, 1)

            for j in range(RET_BLOCKS):
                w = core.arrived(pe, 0, j)
                pe.wait_ge(core.free.sem, core.free.at(j + 1))
                product_parts(nc, core.buf(j), w, KT, acts, SEQ2).then_inc(core.done, 1)
                if j > two:
                    turn_block(j - two - 1)
            turn_block(two - 1)
            pe.wait_ge(t_copied.sem, t_copied.at(two))
            pe.wait_ge(core.free.sem, core.free.at(BUFS + RET_BLOCKS))
            pe.wait_ge(rotated.sem, rotated.at(2 * RET_HEADS))
            n = 0
            for h in range(RET_HEADS):
                for s, q0, nq, _ in pairs:
                    c, rows = TOKEN_TILES[s]
                    if n >= 4:
                        pe.wait_ge(scored.sem, scored.at(n - 3))
                    nc.tensor.matmul(core.ps[0:rows, n % 4, 0:nq], qk[:, RET_HEADS + h, c:c + rows],
                                     qk[:, h, q0:q0 + nq], start=True, stop=True).then_inc(scores_p.sem, 1)
                    n += 1
                pe.wait_ge(scored.sem, scored.at(n))
                if h:
                    pe.wait_ge(copied.sem, copied.at(h))
                for t, (c, rows) in enumerate(TOKEN_TILES):
                    keys = [LT] + (list(range(t + 1)) if t < LT else [])
                    for i, s in enumerate(keys):
                        kr = TOKEN_TILES[s][1]
                        last = nc.tensor.matmul(core.ps[0:rows, 4 + t // 4, t % 4 * P:(t % 4 + 1) * P],
                                                score[0:kr, s, c:c + rows], v[0:kr, s, h * RET_DIM:(h + 1) * RET_DIM],
                                                start=i == 0, stop=i == len(keys) - 1)
                last.then_inc(summed.sem, 1)
            for j in range(2):
                if j:
                    pe.wait_ge(ready.sem, ready.at(RET_HEADS))
                for t, (c, rows) in enumerate(TOKEN_TILES):
                    n = j * (LT + 1) + t
                    if n >= 4:
                        pe.wait_ge(y_copied.sem, y_copied.at(n - 3))
                    for i in range(4):
                        f = (4 * j + i) * P
                        last = nc.tensor.transpose(core.ps[:, n % 4, i * P:i * P + rows], y[0:rows, t, f:f + P],
                                                   core.ident(rows))
                    last.then_inc(y_turned.sem, 1)

        @block.scalar
        def _(act):
            two = 2 * RET_HEADS
            for j in range(RET_BLOCKS):
                core.part_hi(act, 0, j + SPLIT)
                if j >= two:
                    n = j - two
                    core.computed(act, 0, j)
                    if n == 0:
                        act.wait_ge(core.free.sem, core.free.at(BUFS + two))
                    if n >= 2:
                        act.wait_ge(turned.sem, turned.at(n - 1))
                    nc.scalar.activation(like_psum(flat[:, n % 2, :], SEQ2), in_psum(core.buf(j), SEQ2),
                                         ACT.Copy).then_inc(core.free.sem, 1)
            act.wait_ge(core.free.sem, core.free.at(BUFS + RET_BLOCKS))
            act.wait_ge(t_copied.sem, t_copied.at(2 * RET_HEADS))
            nc.scalar.activation(gate_sig, gate, ACT.Sigmoid).then_inc(gate_in.sem, 1)

            def roots(h):
                act.wait_ge(moment.sem, moment.at(h + 1))
                nc.scalar.activation(var[:, h, :], var[:, h, :], ACT.Sqrt, bias=core.eps[:, 0:1],
                                     scale=1.0 / RET_DIM).then_inc(root.sem, 1)

            for h in range(RET_HEADS):
                if h:
                    roots(h - 1)
                act.wait_ge(summed.sem, summed.at(h + 1))
                c = fox + h * RET_DIM
                if h == 0:
                    act.wait_ge(tail.sem, tail.at(1))
                token_major_copies(lambda o, i: nc.scalar.activation(o, i, ACT.Copy),
                                   core.ps[:, 4:6, :].rearrange("p b n -> p (b n)"),
                                   y[:, :, c:c + RET_DIM]).then_inc(copied.sem, 1)
            for n in range(2 * (LT + 1)):
                j, t = divmod(n, LT + 1)
                if n == 2:
                    roots(RET_HEADS - 1)
                c, rows = TOKEN_TILES[t]
                act.wait_ge(y_turned.sem, y_turned.at(n + 1))
                nc.scalar.activation(h_hi[:, 4 * j:4 * j + 4, c:c + rows],
                                     core.ps[:, n % 4, :].rearrange("p (i n) -> p i n", i=4)[:, :, 0:rows],
                                     ACT.Copy).then_inc(hi_done.sem, 1)

        @block.vector
        def _(dve):
            step = Steps(dve, chain)
            v_ = nc.vector
            dve.wait_ge(tables.sem, tables.at(64))
            pv = lambda j, r: in_psum(core.buf(j)[r, :], SEQ2)
            lo, hi = slice(0, half), slice(half, RET_DIM)
            for j in range(2 * RET_HEADS):
                core.part_lo(dve, 0, j + SPLIT)
                core.computed(dve, 0, j)
                step(v_.tensor_tensor(like_psum(work[:, 0, :], SEQ2), pv(j, slice(0, P)), like_psum(cos, SEQ2),
                                      ALU.mult))
                for dst, src in ((lo, hi), (hi, lo)):
                    last = v_.tensor_tensor(like_psum(work[dst, 1, :], SEQ2), pv(j, src), like_psum(sin[src, :], SEQ2),
                                            ALU.mult)
                last.then_inc(core.free.sem, 1)
                dve.wait_ge(core.free.sem, core.free.at(BUFS + j + 1))
                v_.tensor_tensor(qk[:, j, :], work[:, 0, :], work[:, 1, :], ALU.add).then_inc(rotated.sem, 1)
                dve.wait_ge(rotated.sem, rotated.at(j + 1))
            dve.wait_ge(tail.sem, tail.at(2))
            for n in range(2 * RET_HEADS + 1):
                if n < 2 * RET_HEADS:
                    core.part_lo(dve, 0, 2 * RET_HEADS + n + SPLIT)
                if n:
                    b = n - 1
                    dst = v if b < RET_HEADS else gate
                    dve.wait_ge(turned.sem, turned.at(n))
                    c = b % RET_HEADS * P
                    token_major_copies(v_.tensor_copy, out_t, dst[:, :, c:c + P]).then_inc(t_copied.sem, 1)
            dve.wait_ge(t_copied.sem, t_copied.at(2 * RET_HEADS))
            dve.wait_ge(gate_in.sem, gate_in.at(1))
            step(v_.tensor_tensor(gate, gate, gate_sig, ALU.mult))
            step(v_.tensor_tensor(gate, gate, gain[:, None, :].to_broadcast([P, LT + 1, width]), ALU.mult))

            def group_norm(h):
                g = slice(h * RET_DIM, (h + 1) * RET_DIM)
                o = y[:, :, fox + h * RET_DIM:fox + (h + 1) * RET_DIM]
                bc = lambda ap: ap[:, :, None].to_broadcast([P, LT + 1, RET_DIM])
                dve.wait_ge(copied.sem, copied.at(h + 1))
                step(v_.tensor_reduce(mean[:, h, :], o, AX.X, ALU.add))
                step(v_.tensor_scalar(mean[:, h, :], mean[:, h, :], 1.0 / RET_DIM, None, ALU.mult))
                step(v_.tensor_tensor(o, o, bc(mean[:, h, :]), ALU.subtract))
                step(v_.tensor_tensor(sq_buf, o, o, ALU.mult))
                v_.tensor_reduce(var[:, h, :], sq_buf, AX.X, ALU.add).then_inc(moment.sem, 1)
                step(v_.tensor_tensor(o, o, gate[:, :, g], ALU.mult))
                dve.wait_ge(root.sem, root.at(h + 1))
                step(v_.reciprocal(var[:, h, :], var[:, h, :]))
                v_.tensor_tensor(o, o, bc(var[:, h, :]), ALU.mult).then_inc(ready.sem, 1)

            n = 0
            for h in range(RET_HEADS):
                if h:
                    dve.wait_ge(summed.sem, summed.at(h))
                for s, q0, nq, c in pairs:
                    rows = TOKEN_TILES[s][1]
                    dve.wait_ge(scores_p.sem, scores_p.at(n + 1))
                    v_.scalar_tensor_tensor(score[0:rows, s, q0:q0 + nq], core.ps[0:rows, n % 4, 0:nq], scale,
                                            decay[0:rows, h, c:c + nq], ALU.mult, ALU.mult).then_inc(scored.sem, 1)
                    n += 1
                if h:
                    group_norm(h - 1)
            group_norm(RET_HEADS - 1)
            for n in range(2 * (LT + 1)):
                j, t = divmod(n, LT + 1)
                c, rows = TOKEN_TILES[t]
                dve.wait_ge(hi_done.sem, hi_done.at(n + 1))
                v_.tensor_tensor(h_lo[:, 4 * j:4 * j + 4, c:c + rows],
                                 core.ps[:, n % 4, :].rearrange("p (i n) -> p i n", i=4)[:, :, 0:rows],
                                 h_hi[:, 4 * j:4 * j + 4, c:c + rows], ALU.subtract).then_inc(y_copied.sem, 1)
            chain.close(step.n)
    core.close(RET_BLOCKS, outs)
    for s, k in ((tables, 64), (tail, 2), (rotated, 2 * RET_HEADS), (gate_in, 1), (scores_p, RET_HEADS * len(pairs)),
                 (scored, RET_HEADS * len(pairs)), (summed, RET_HEADS), (copied, RET_HEADS), (moment, RET_HEADS),
                 (root, RET_HEADS), (ready, RET_HEADS), (y_turned, 2 * (LT + 1)), (y_copied, 2 * (LT + 1)),
                 (turned, 2 * RET_HEADS), (t_copied, 2 * RET_HEADS), (hi_done, 2 * (LT + 1))):
        s.close(k)


def load_meta(core):
    nc = core.nc
    meta = core.counter("meta_in")
    sq = Squares(core, SEQ2)
    with core.space("sq", [P, 2, ALL]) as tmp:
        with nc.Block(no_gpsimd_drain=True) as block:
            @block.sync
            def _(sp):
                sp.dma_start(core.x[:, :, LAT:SEQ2], core.dram["meta"]).then_inc(meta.sem, 16)

            @block.scalar
            def _(act):
                act.wait_ge(meta.sem, meta.at(16))
                for m in range(KT):
                    sq.square(act, tmp, m)

            @block.gpsimd
            def _(pool):
                for m in range(KT):
                    sq.add(pool, tmp, m)
    sq.close(KT)
    meta.close(16)


def store(core, result):
    stored = core.counter("result_stored")
    with core.nc.Block(no_gpsimd_drain=True) as block:
        @block.sync
        def _(sp):
            sp.dma_start(core.dram["out"], result[:, :, 0:LAT]).then_inc(stored.sem, 16)
            sp.wait_ge(stored.sem, 16)


def build(nc, dram):
    with ExitStack() as ctx:
        core = Core(nc, ctx, dram)
        for l in range(DEPTH):
            for half in range(HALVES):
                end = DEPTH * LAYER1 + (l + 1) * LAYER2 - (HALVES - 1 - half) * FFN_BLOCKS // HALVES
                core.narrow.append((end - 2 * KT, end))
        param = core.param
        setup(core)

        @contextmanager
        def parts(width):
            with core.space("h_hi", [P, KT, width], F32R) as hi, core.space("h_lo", [P, KT, width], F32R) as lo:
                yield (hi, lo), lambda k: (hi[:, k, :], lo[:, k, :])

        for l in range(DEPTH):
            last = l == DEPTH - 1
            whole = [(0, LAT, 0), (LAT, ALL, 1)]
            some, tokens = (whole[:1], LAT) if last else (whole, ALL)
            with core.space("arena", [P, ARENA]) as arena:
                mix = arena[:, 0:KT * ALL].rearrange("p (k n) -> p k n", k=KT)
                with parts(ALL) as (h, acts):
                    norm = Norm(core, ALL, lambda k, c: core.gain[:, 0, k, c:c + 1],
                                lambda k, c: core.mod[:, 0, k, c:c + 1], whole, h)
                    fourier(core, arena, acts, mix, tokens, norm, l, MOD_BLOCKS - KT if l else MOD_FIRST, MOD_FOURIER)
                    latent_attention(core, arena, acts, l, mix, not last)
                    m = Mlstm(arena, mix)
                    acc = arena[:, 2 * ALL:2 * ALL + 2 * (CONV_IN - 4)].rearrange("p (a n) -> p a n", a=2)
                    mlstm_inputs(core, arena, acts, l, m, acc)
                with core.space("scratch", [P, 2 * KT * ALL]) as scratch:
                    mlstm(core, arena, scratch, m, mix, not last)
                with parts(ALL) as (h, acts):
                    tmp = arena[:, KT * ALL:(KT + 2) * ALL].rearrange("p (a n) -> p a n", a=2)
                    mod = None
                    if l == 0:
                        free = arena[:, (KT + 2) * ALL:(KT + 2) * ALL + (MOD_RING + 4) * BLOCK]
                        mod = Modulation(core, 0, MOD_FIRST + MOD_FOURIER, MOD_BLOCKS - MOD_FIRST - MOD_FOURIER - KT,
                                         free[:, 0:MOD_RING * BLOCK],
                                         free[:, MOD_RING * BLOCK:].rearrange("p (r n) -> p r n", r=4))
                    out_projection(core, h, mix, tokens, lambda j, c: core.mod[:, 2, j, c:c + 1], some, tmp, mod)
            with parts(ALL) as (h, acts):
                norm = Norm(core, tokens, lambda k, c: core.gain[:, 1, k, c:c + 1],
                            lambda k, c: core.mod[:, 3, k, c:c + 1], some, h)
                squared_relu_mlp(core, norm, acts, tokens, lambda j, c: core.mod[:, 5, j, c:c + 1], some, not last)
        plain_norm(core, LAT, P_GFINAL, core.x)
        load_meta(core)
        every = [(0, SEQ2, 0)]
        for l in range(DEPTH):
            with parts(SEQ2) as (h, acts):
                with core.space("arena", [P, ARENA]) as arena:
                    y = arena[:, 0:(LT + 1) * D].rearrange("p (t n) -> p t n", t=LT + 1)
                    norm = Norm(core, SEQ2, lambda k, c: param[:, P_ANORM + l * KT + k:P_ANORM + l * KT + k + 1],
                                None, every, h)
                    forgetting_attention(core, arena, acts, norm, l, y)
                    retention(core, arena, acts, l, y, *h)
                with core.space("sq", [P, 2, SEQ2]) as tmp:
                    out_projection(core, h, None, SEQ2, None, every, tmp)
                norm = Norm(core, SEQ2, lambda k, c: param[:, P_FNORM + l * KT + k:P_FNORM + l * KT + k + 1],
                            None, every, h)
                swiglu_mlp(core, norm, acts)
        with core.space("result", [P, KT, LAT]) as result:
            plain_norm(core, LAT, P_FINAL, result)
            store(core, result)



def _blocks(w, cols):
    parts = w[:, cols].reshape(-1, P, len(cols)).transpose(1, 0, 2).reshape(P, -1)
    out = np.zeros((P, BLOCK), np.float32)
    out[:, :parts.shape[1]] = parts
    return out[None]


def _stream(i):
    r = np.arange
    out = []

    def by_cols(w, start, stop, width=P):
        out.extend(_blocks(w, r(c, c + width)) for c in range(start, stop, width))

    def padded(w, groups, width):
        z = np.zeros((w.shape[0], width * len(groups)), np.float32)
        for n, g in enumerate(groups):
            for at, cols in g:
                z[:, n * width + at:n * width + at + len(cols)] = w[:, cols]
        zz = np.zeros((w.shape[0], P), np.float32)
        zz[:, :z.shape[1]] = z
        out.append(_blocks(zz, r(P)))

    f = 4 * F_GROUP
    mw = M_HEADS * M_DIM
    rot = A_ROPE // 4
    swap = np.concatenate([r(rot, 2 * rot), r(rot), r(3 * rot, 4 * rot), r(2 * rot, 3 * rot)])
    for l in range(DEPTH):
        w = i["w_in"][l]
        g0 = f + 4 * mw
        q0 = g0 + 4 * M_HEADS
        kr0 = q0 + Q_LORA + KV_LORA
        by_cols(w, 0, f)
        by_cols(w, q0, kr0)
        padded(w, [[(A_NOPE, kr0 + r(A_ROPE)), (A_QK, kr0 + swap)]], P)
        by_cols(w, f, f + 2 * mw, M_DIM)
        gate = lambda n: g0 + n * M_HEADS + r(M_HEADS)
        padded(w, [[(FWD, gate(0)), (BWD, gate(2)), (F_ROW + FWD, gate(1)), (F_ROW + BWD, gate(3))]], P)
        by_cols(w, f + 2 * mw, f + 4 * mw)
        by_cols(i["w_out"][l], 0, D)
        for q in range(QUARTERS):
            by_cols(i["w_up"][l], q * D, (q + 1) * D)
            by_cols(i["w_down"][l][q * D:(q + 1) * D], 0, D)
    fw = FOX_HEADS * FOX_DIM
    for l in range(DEPTH):
        w = i["w_in_2"][l]
        padded(w, [[(0, 3 * fw + r(FOX_HEADS))]], P)
        by_cols(w, 0, 3 * fw)
        by_cols(w, 3 * fw + FOX_HEADS, w.shape[1])
        by_cols(i["w_out_2"][l], 0, D)
        half = H_TILES * P
        for n in range(HALVES):
            for c in range(n * half, (n + 1) * half, P):
                by_cols(i["w_gate_2"][l], c, c + P)
                by_cols(i["w_up_2"][l], c, c + P)
            for c in range(0, D, P):
                k = n * half
                for kts in H_KT:
                    out.append(_blocks(i["w_down_2"][l][k:k + kts * P], r(c, c + P)))
                    k += kts * P
    out.append(np.zeros((SPLIT, P, BLOCK), np.float32))
    return np.concatenate(out)


def _modulation(i):
    return i["w_mod"].transpose(0, 2, 1).reshape(DEPTH * MOD_BLOCKS, P, D)


def _lora(i):
    rot = A_ROPE // 4
    r = np.arange
    swap = np.concatenate([r(rot, 2 * rot), r(rot), r(3 * rot, 4 * rot), r(2 * rot, 3 * rot)])
    rows = lambda v: v.reshape(2, P, -1).transpose(1, 0, 2).reshape(P, -1)
    q, kv = [], []
    for l in range(DEPTH):
        uq = i["w_uq"][l].reshape(2, P, A_HEADS, A_QK)
        q.append(np.concatenate([rows(uq), rows(uq[:, :, :, A_NOPE + swap])], 1))
        ukv = i["w_ukv"][l].reshape(P, A_HEADS, A_NOPE + A_V)
        kv.append(np.concatenate([ukv[:, :, :A_NOPE].reshape(P, -1), ukv[:, :, A_NOPE:].reshape(P, -1)], 1))
    return np.stack(q), np.stack(kv)


def _params(i):
    p = np.zeros((P, P_END), np.float32)
    tiled = lambda v: v.reshape(-1, P).T

    def put(at, v):
        p[:v.shape[0], at:at + v.shape[1]] = v

    for l in range(DEPTH):
        put(P_BMOD + l * MOD_BLOCKS, tiled(i["b_mod"][l]))
        put(P_G1 + l * KT, tiled(i["g_norm1"][l]))
        put(P_G2 + l * KT, tiled(i["g_norm2"][l]))
        conv = i["conv_qk"][l].reshape(CONV, 2 * M_HEADS, M_DIM).transpose(2, 1, 0).reshape(M_DIM, -1)
        put(P_CONV + l * 2 * M_HEADS * CONV, conv)
        bg = i["b_gates"][l].reshape(4, M_HEADS)
        for n in range(2):
            p[FWD:FWD + M_HEADS, P_BG + 2 * l + n] = bg[n]
            p[BWD:BWD + M_HEADS, P_BG + 2 * l + n] = bg[2 + n]
        put(P_GQ + 2 * l, tiled(i["g_q_norm"][l]))
        put(P_GKV + l, tiled(i["g_kv_norm"][l]))
        put(P_ANORM + l * KT, tiled(i["attn_norm_2"][l]))
        put(P_FNORM + l * KT, tiled(i["ffn_norm_2"][l]))
        put(P_BF + l, i["b_fgate_2"][l].reshape(-1, 1))
    put(P_FINAL, tiled(i["final_norm_2"]))
    put(P_GFINAL, tiled(i["g_final"]))
    return p


def _tables():
    t = {}
    p, f = np.arange(P)[:, None], np.arange(P)[None, :]
    const = np.zeros((P, C_END))
    const[:, C_IDENT:C_IDENT + P] = np.eye(P)
    const[:, C_LOWER:C_LOWER + P] = np.where(f <= p, 0.0, NEG)
    const[:, C_UPPER:C_UPPER + P] = np.where(f >= p, 0.0, NEG)
    same = (p // F_GROUP) == (f // F_GROUP)
    ang = 2 * np.pi * ((p % F_GROUP) * (f % F_GROUP) % F_GROUP) / F_GROUP
    const[:, C_DFT:C_DFT + P] = np.cos(ang) * same
    const[:, C_DFT + P:C_END] = np.sin(ang) * same
    t["const"] = const
    for name, n in (("lat", LAT), ("ctx", CTX)):
        ang = 2 * np.pi * (np.outer(np.arange(n), np.arange(n)) % n) / n
        norm = 1.0 / np.sqrt(n * F_GROUP)
        t["cos_" + name] = (np.cos(ang) * norm).reshape(n // P, P, n).transpose(1, 0, 2)
        t["sin_" + name] = (-np.sin(ang) * norm).reshape(n // P, P, n).transpose(1, 0, 2)
    nf = A_ROPE // 4
    freqs = (10000.0 ** (-np.arange(nf, dtype=np.float32) / np.float32(nf))).astype(np.float32)
    pos = np.arange(LAT)
    axes = [(pos // GRID_W).astype(np.float32), (pos % GRID_W).astype(np.float32)]
    cos, sin = np.zeros((A_ROPE, LAT)), np.zeros((A_ROPE, LAT))
    for axis in range(2):
        a = freqs[:, None] * axes[axis][None, :]
        for part in range(2):
            rows = slice((2 * axis + part) * nf, (2 * axis + part + 1) * nf)
            cos[rows] = np.cos(a)
            sin[rows] = np.sin(a) * (-1.0 if part == 0 else 1.0)
    t["rope_cos"], t["rope_sin"] = cos, sin
    select = np.zeros((ROWS, 2 * M_HEADS, P))
    for d, row in enumerate((FWD, BWD)):
        for h in range(M_HEADS):
            select[row + h, d * M_HEADS + h] = 1.0
    t["select"] = select
    inv = (10000.0 ** (-np.arange(0, RET_DIM, 2, dtype=np.float32) / np.float32(RET_DIM))).astype(np.float32)
    place = np.concatenate([META + np.arange(LAT), np.arange(META)]).astype(np.float32)
    a = inv[:, None] * place[None, :]
    t["ret_cos"] = np.concatenate([np.cos(a), np.cos(a)])
    t["ret_sin"] = np.concatenate([np.sin(a), -np.sin(a)])
    j = np.arange(SEQ2)[None, :] - np.arange(P)[:, None]
    t["ret_decay"] = np.stack([np.where(j >= 0, np.exp(np.maximum(j, 0) * g), 0.0) for g in LOG_GAMMA], 1)
    return {k: np.ascontiguousarray(v, np.float32) for k, v in t.items()}


def _arrays(i):
    to_features = lambda v: v.reshape(v.shape[-2], KT, P).transpose(2, 1, 0)
    rows = lambda v: np.broadcast_to(v[:, None, :], (DEPTH, P, v.shape[-1]))
    arrays = {
        "weights": _stream(i),
        "w_mod": _modulation(i),
        "c_rows": np.stack([i["c"].reshape(-1), i["c_ctx"].reshape(-1)]).reshape(1, 2 * D),
        "param": _params(i),
        "x": np.concatenate([to_features(i["x"]), to_features(i["ctx"])], 2),
        "meta": to_features(i["meta_tokens_2"]),
        "g_mlstm": rows(i["g_mlstm"]),
        "ret_gn": rows(i["ret_gn_2"]),
    }
    arrays["w_uq"], arrays["w_ukv"] = _lora(i)
    arrays.update(_tables())
    return {k: np.ascontiguousarray(v) for k, v in arrays.items()}


def kernel(**inputs):
    import concourse.bacc as bacc
    from concourse.bass_utils import run_bass_kernel_spmd

    nc = bacc.Bacc("TRN2", target_bir_lowering=False, num_devices=1)
    arrays = _arrays({k: np.asarray(v) for k, v in inputs.items()})
    dram = {k: nc.dram_tensor(k + "_dram", v.shape, mybir.dt.from_np(v.dtype), kind="ExternalInput").ap()
            for k, v in arrays.items()}
    dram["out"] = nc.dram_tensor("out_dram", (P, KT, LAT), F32, kind="ExternalOutput").ap()
    build(nc, dram)
    r = run_bass_kernel_spmd(nc, [{k + "_dram": v for k, v in arrays.items()}], core_ids=[0])
    out = r.results[0]["out_dram"]
    return np.ascontiguousarray(out.transpose(2, 1, 0).reshape(1, LAT, D))
```
